# Optimizing a Trainium2 kernel written in Bass

```python
import math
import jax, jax.numpy as jnp
from jax import lax
import numpy as np

D_MODEL = 1024
BATCH = 1
SEQ = 512
DEPTH = 1

D_MIX = D_MODEL
N_GROUPS = 4
GROUP_W = D_MIX // N_GROUPS

A_HEADS = 4
A_QK_DIM = GROUP_W // A_HEADS // 2
A_V_DIM = 2 * A_QK_DIM

B_HEADS = 4
B_HEAD_DIM = GROUP_W // B_HEADS
MOBA_BLOCK = 256
MOBA_TOPK = 3

C_HEADS = 4
C_V_DIM = GROUP_W // C_HEADS
C_K_DIM = C_V_DIM // 2
GLA_RANK = 16
GLA_TAU = 16.0
GLA_CHUNK = 64

D_WIDTH = GROUP_W
D_BLOCKS = 4
D_BLOCK_DIM = D_WIDTH // D_BLOCKS
CONV_W = 4
LRU_C = 8.0

N_EXPERTS = 32
TOP_K = 4
D_FF = D_MODEL
SWIGLU_ALPHA = 1.702
SWIGLU_LIMIT = 7.0
MOE_BLOCK = 128

Q_BLOCK = 128
EPS = 1e-6

A_Q = A_HEADS * 2 * A_QK_DIM
A_K = A_HEADS * 2 * A_QK_DIM
A_V = A_HEADS * A_V_DIM
B_Q = GROUP_W
B_K = GROUP_W
B_V = GROUP_W
C_Q = C_HEADS * C_K_DIM
C_K = C_HEADS * C_K_DIM
C_V = C_HEADS * C_V_DIM
C_G = GLA_RANK
C_R = C_HEADS * C_V_DIM
D_X = D_WIDTH
D_G = D_WIDTH
D_IN = A_Q + A_K + A_V + B_Q + B_K + B_V + C_Q + C_K + C_V + C_G + C_R + D_X + D_G


def rms_norm(x, gain):
    xf = x.astype(jnp.float32)
    y = xf * lax.rsqrt(jnp.mean(xf * xf, axis=-1, keepdims=True) + EPS)
    return (y * gain.astype(jnp.float32)).astype(x.dtype)

def to_heads(t, n):
    b, s, f = t.shape
    return t.reshape(b, s, n, f // n).transpose(0, 2, 1, 3)

def merge_heads(t):
    b, h, s, d = t.shape
    return t.transpose(0, 2, 1, 3).reshape(b, s, h * d)

def split_columns(proj):
    sizes = (A_Q, A_K, A_V, B_Q, B_K, B_V, C_Q, C_K, C_V, C_G, C_R, D_X, D_G)
    out, off = [], 0
    for sz in sizes:
        out.append(proj[..., off:off + sz])
        off += sz
    return out

def diff_attention(q, k, v, q_gain, k_gain, lam_q1, lam_k1, lam_q2, lam_k2, out_gain, layer_idx):
    bsz, s, _ = q.shape
    q = rms_norm(q.reshape(bsz, s, A_HEADS, 2, A_QK_DIM), q_gain).transpose(0, 2, 3, 1, 4)
    k = rms_norm(k.reshape(bsz, s, A_HEADS, 2, A_QK_DIM), k_gain).transpose(0, 2, 3, 1, 4)
    v = to_heads(v, A_HEADS)
    lam_init = 0.8 - 0.6 * math.exp(-0.3 * layer_idx)
    lam = (jnp.exp(jnp.sum(lam_q1.astype(jnp.float32) * lam_k1.astype(jnp.float32)))
           - jnp.exp(jnp.sum(lam_q2.astype(jnp.float32) * lam_k2.astype(jnp.float32))) + lam_init)
    scale = A_QK_DIM ** -0.5
    nq = s // Q_BLOCK
    qb = q.reshape(bsz, A_HEADS, 2, nq, Q_BLOCK, A_QK_DIM).transpose(3, 0, 1, 2, 4, 5)
    kpos = jnp.arange(s)

    def block(args):
        j, qj = args
        qpos = j * Q_BLOCK + jnp.arange(Q_BLOCK)
        sc = jnp.einsum('bhiqd,bhikd->bhiqk', qj, k).astype(jnp.float32) * scale
        sc = jnp.where(kpos[None, :] <= qpos[:, None], sc, -jnp.inf)
        p = jax.nn.softmax(sc, axis=-1)
        w = p[:, :, 0] - lam * p[:, :, 1]
        return jnp.einsum('bhqk,bhkd->bhqd', w.astype(v.dtype), v)

    o = lax.map(block, (jnp.arange(nq), qb))
    o = o.transpose(1, 2, 0, 3, 4).reshape(bsz, A_HEADS, s, A_V_DIM)
    o = rms_norm(o, out_gain) * (1.0 - lam_init)
    return merge_heads(o)

def moba_attention(q, k, v, q_gain, k_gain):
    bsz, s, _ = q.shape
    q = rms_norm(to_heads(q, B_HEADS), q_gain)
    k = rms_norm(to_heads(k, B_HEADS), k_gain)
    v = to_heads(v, B_HEADS)
    nb = -(-s // MOBA_BLOCK)
    pad = nb * MOBA_BLOCK - s
    k_p = jnp.pad(k, ((0, 0), (0, 0), (0, pad), (0, 0)))
    v_p = jnp.pad(v, ((0, 0), (0, 0), (0, pad), (0, 0)))
    kb = k_p.reshape(bsz, B_HEADS, nb, MOBA_BLOCK, B_HEAD_DIM)
    vb = v_p.reshape(bsz, B_HEADS, nb, MOBA_BLOCK, B_HEAD_DIM)
    k_mean = jnp.mean(kb.astype(jnp.float32), axis=3)
    topk = min(MOBA_TOPK, nb)
    scale = B_HEAD_DIM ** -0.5
    nq = s // Q_BLOCK
    qb = q.reshape(bsz, B_HEADS, nq, Q_BLOCK, B_HEAD_DIM).transpose(2, 0, 1, 3, 4)
    b_idx = jnp.arange(bsz)[:, None, None, None]
    h_idx = jnp.arange(B_HEADS)[None, :, None, None]
    blk_ids = jnp.arange(nb)

    def block(args):
        j, qj = args
        qpos = j * Q_BLOCK + jnp.arange(Q_BLOCK)
        own = (j * Q_BLOCK) // MOBA_BLOCK
        gate = jnp.einsum('bhqd,bhnd->bhqn', qj.astype(jnp.float32), k_mean)
        gate = jnp.where(blk_ids < own, gate, -jnp.inf)
        _, sel = lax.top_k(gate, topk)
        valid = sel < own
        k_sel = kb[b_idx, h_idx, sel]
        v_sel = vb[b_idx, h_idx, sel]
        s_sel = jnp.einsum('bhqd,bhqnkd->bhqnk', qj, k_sel).astype(jnp.float32) * scale
        s_sel = jnp.where(valid[..., None], s_sel, -jnp.inf).reshape(bsz, B_HEADS, Q_BLOCK, topk * MOBA_BLOCK)
        k_own = lax.dynamic_slice_in_dim(k_p, own * MOBA_BLOCK, MOBA_BLOCK, axis=2)
        v_own = lax.dynamic_slice_in_dim(v_p, own * MOBA_BLOCK, MOBA_BLOCK, axis=2)
        kpos = own * MOBA_BLOCK + jnp.arange(MOBA_BLOCK)
        s_own = jnp.einsum('bhqd,bhkd->bhqk', qj, k_own).astype(jnp.float32) * scale
        s_own = jnp.where(kpos[None, :] <= qpos[:, None], s_own, -jnp.inf)
        p = jax.nn.softmax(jnp.concatenate([s_sel, s_own], axis=-1), axis=-1).astype(v.dtype)
        p_sel = p[..., :topk * MOBA_BLOCK].reshape(bsz, B_HEADS, Q_BLOCK, topk, MOBA_BLOCK)
        p_own = p[..., topk * MOBA_BLOCK:]
        return (jnp.einsum('bhqnk,bhqnkd->bhqd', p_sel, v_sel)
                + jnp.einsum('bhqk,bhkd->bhqd', p_own, v_own))

    o = lax.map(block, (jnp.arange(nq), qb))
    o = o.transpose(1, 2, 0, 3, 4).reshape(bsz, B_HEADS, s, B_HEAD_DIM)
    return merge_heads(o)

def gla(q, k, v, g_low, r, w_g2, b_g, out_gain):
    bsz, s, _ = q.shape
    dt = q.dtype
    f32 = jnp.float32
    q = to_heads(q, C_HEADS).astype(f32) * (C_K_DIM ** -0.5)
    k = to_heads(k, C_HEADS).astype(f32)
    v = to_heads(v, C_HEADS).astype(f32)
    g = jax.nn.log_sigmoid((g_low @ w_g2 + b_g).astype(f32)) / GLA_TAU
    g = to_heads(g, C_HEADS)
    nc = s // GLA_CHUNK

    def chunks(t):
        return t.reshape(bsz, C_HEADS, nc, GLA_CHUNK, t.shape[-1]).transpose(2, 0, 1, 3, 4)

    causal = jnp.tril(jnp.ones((GLA_CHUNK, GLA_CHUNK), bool))

    def step(state, inp):
        qc, kc, vc, gc = inp
        bcum = jnp.cumsum(gc, axis=2)
        o_inter = jnp.einsum('bhcd,bhde->bhce', qc * jnp.exp(bcum), state)
        diff = bcum[:, :, :, None, :] - bcum[:, :, None, :, :]
        decay = jnp.exp(jnp.where(causal[:, :, None], diff, -jnp.inf))
        att = jnp.einsum('bhid,bhjd,bhijd->bhij', qc, kc, decay)
        o_intra = jnp.einsum('bhij,bhje->bhie', att, vc)
        b_last = bcum[:, :, -1:, :]
        state = (jnp.exp(b_last[:, :, 0, :])[..., None] * state
                 + jnp.einsum('bhcd,bhce->bhde', kc * jnp.exp(b_last - bcum), vc))
        return state, o_inter + o_intra

    state0 = jnp.zeros((bsz, C_HEADS, C_K_DIM, C_V_DIM), f32)
    _, o = lax.scan(step, state0, (chunks(q), chunks(k), chunks(v), chunks(g)))
    o = o.transpose(1, 2, 0, 3, 4).reshape(bsz, C_HEADS, s, C_V_DIM)
    o = merge_heads(rms_norm(o, out_gain)) * jax.nn.silu(r.astype(f32))
    return o.astype(dt)

def rg_lru(xb, gate_in, conv_w, conv_b, w_a, b_a, w_x, b_x, lam):
    bsz, s, cw = xb.shape
    f32 = jnp.float32
    xc = lax.conv_general_dilated(xb, conv_w[:, None, :], window_strides=(1,),
                                  padding=[(CONV_W - 1, 0)],
                                  dimension_numbers=('NWC', 'WIO', 'NWC'),
                                  feature_group_count=cw) + conv_b
    xs = xc.reshape(bsz, s, D_BLOCKS, D_BLOCK_DIM)
    r_gate = jax.nn.sigmoid((jnp.einsum('bsnd,nde->bsne', xs, w_a).reshape(bsz, s, cw) + b_a).astype(f32))
    i_gate = jax.nn.sigmoid((jnp.einsum('bsnd,nde->bsne', xs, w_x).reshape(bsz, s, cw) + b_x).astype(f32))
    log_a = LRU_C * r_gate * jax.nn.log_sigmoid(lam.astype(f32))
    a = jnp.exp(log_a)
    bt = jnp.sqrt(-jnp.expm1(2.0 * log_a)) * (i_gate * xc.astype(f32))

    def combine(c1, c2):
        a1, b1 = c1
        a2, b2 = c2
        return a1 * a2, a2 * b1 + b2

    _, h = lax.associative_scan(combine, (a, bt), axis=1)
    return (h * jax.nn.gelu(gate_in.astype(f32))).astype(xb.dtype)

def hybrid_mixer(h, w_in, w_out, a_q_gain, a_k_gain, a_lam_q1, a_lam_k1, a_lam_q2, a_lam_k2,
                 a_out_gain, b_q_gain, b_k_gain, c_w_g2, c_b_g, c_out_gain, d_conv_w, d_conv_b,
                 d_w_a, d_b_a, d_w_x, d_b_x, d_lambda, layer_idx):
    proj = h @ w_in
    aq, ak, av, bq, bk, bv, cq, ck, cv, cg, cr, dx, dg = split_columns(proj)
    o_a = diff_attention(aq, ak, av, a_q_gain, a_k_gain, a_lam_q1, a_lam_k1, a_lam_q2, a_lam_k2,
                         a_out_gain, layer_idx)
    o_b = moba_attention(bq, bk, bv, b_q_gain, b_k_gain)
    o_c = gla(cq, ck, cv, cg, cr, c_w_g2, c_b_g, c_out_gain)
    o_d = rg_lru(dx, dg, d_conv_w, d_conv_b, d_w_a, d_b_a, d_w_x, d_b_x, d_lambda)
    y = jnp.concatenate([o_a.astype(h.dtype), o_b.astype(h.dtype), o_c, o_d], axis=-1)
    return y @ w_out

def moe(h, router_w, router_b, w_up, b_up, w_down, b_down):
    bsz, s, d = h.shape
    t = bsz * s
    xt = h.reshape(t, d)
    logits = (xt @ router_w + router_b).astype(jnp.float32)
    top_vals, top_idx = lax.top_k(logits, TOP_K)
    gates = jax.nn.softmax(top_vals, axis=-1)
    n = t * TOP_K
    e_flat = top_idx.reshape(n)
    tok_flat = jnp.arange(n, dtype=jnp.int32) // TOP_K
    g_flat = gates.reshape(n)
    order = jnp.argsort(e_flat)
    e_sorted = e_flat[order]
    tok_sorted = tok_flat[order]
    g_sorted = g_flat[order]
    counts = jax.ops.segment_sum(jnp.ones((n,), jnp.int32), e_flat, num_segments=N_EXPERTS)
    starts = jnp.cumsum(counts) - counts
    padded = (counts + MOE_BLOCK - 1) // MOE_BLOCK * MOE_BLOCK
    pad_ends = jnp.cumsum(padded)
    pad_starts = pad_ends - padded
    dest = pad_starts[e_sorted] + (jnp.arange(n, dtype=jnp.int32) - starts[e_sorted])
    n_rows = -(-n // MOE_BLOCK) * MOE_BLOCK + N_EXPERTS * MOE_BLOCK
    n_blocks = n_rows // MOE_BLOCK
    row_tok = jnp.full((n_rows,), t, jnp.int32).at[dest].set(tok_sorted)
    row_gate = jnp.zeros((n_rows,), jnp.float32).at[dest].set(g_sorted)
    blk_expert = jnp.minimum(jnp.searchsorted(pad_ends, jnp.arange(n_blocks) * MOE_BLOCK, side='right'),
                             N_EXPERTS - 1)
    x_pad = jnp.concatenate([xt, jnp.zeros((1, d), xt.dtype)], axis=0)
    x_rows = x_pad[row_tok].reshape(n_blocks, MOE_BLOCK, d)

    def expert_block(args):
        e, xb = args
        hu = xb @ w_up[e] + b_up[e]
        g = jnp.minimum(hu[:, :D_FF], SWIGLU_LIMIT)
        lin = jnp.clip(hu[:, D_FF:], -SWIGLU_LIMIT, SWIGLU_LIMIT)
        glu = g * jax.nn.sigmoid(SWIGLU_ALPHA * g)
        return ((lin + 1.0) * glu) @ w_down[e] + b_down[e]

    y_rows = lax.map(expert_block, (blk_expert, x_rows)).reshape(n_rows, d)
    y = jax.ops.segment_sum(y_rows * row_gate[:, None].astype(y_rows.dtype), row_tok, num_segments=t + 1)[:t]
    return y.reshape(bsz, s, d)

def first_inputs(seed: int = 0) -> dict:
    key = jax.random.key(seed)
    ks = iter(jax.random.split(key, 40))
    L = DEPTH
    f32 = jnp.float32

    def nrm(shape, scale):
        return jax.random.normal(next(ks), shape, f32) * scale

    def gain(shape):
        return 1.0 + nrm(shape, 0.05)

    x = nrm((BATCH, SEQ, D_MODEL), 1.0)
    c = nrm((BATCH, D_MODEL), 1.0)
    ada_w = nrm((L, D_MODEL, 6 * D_MODEL), 0.5 * D_MODEL ** -0.5)
    ada_b = nrm((L, 6 * D_MODEL), 0.02)
    norm1_g = gain((L, D_MODEL))
    norm2_g = gain((L, D_MODEL))
    w_in = nrm((L, D_MODEL, D_IN), D_MODEL ** -0.5)
    w_out = nrm((L, D_MIX, D_MODEL), D_MIX ** -0.5)
    a_q_gain = gain((L, A_QK_DIM))
    a_k_gain = gain((L, A_QK_DIM))
    a_lam_q1 = nrm((L, A_QK_DIM), 0.1)
    a_lam_k1 = nrm((L, A_QK_DIM), 0.1)
    a_lam_q2 = nrm((L, A_QK_DIM), 0.1)
    a_lam_k2 = nrm((L, A_QK_DIM), 0.1)
    a_out_gain = gain((L, A_V_DIM))
    b_q_gain = gain((L, B_HEAD_DIM))
    b_k_gain = gain((L, B_HEAD_DIM))
    c_w_g2 = nrm((L, GLA_RANK, C_HEADS * C_K_DIM), GLA_RANK ** -0.5)
    c_b_g = nrm((L, C_HEADS * C_K_DIM), 0.1)
    c_out_gain = gain((L, C_V_DIM))
    d_conv_w = nrm((L, CONV_W, D_WIDTH), CONV_W ** -0.5)
    d_conv_b = nrm((L, D_WIDTH), 0.02)
    d_w_a = nrm((L, D_BLOCKS, D_BLOCK_DIM, D_BLOCK_DIM), D_BLOCK_DIM ** -0.5)
    d_b_a = nrm((L, D_WIDTH), 0.02)
    d_w_x = nrm((L, D_BLOCKS, D_BLOCK_DIM, D_BLOCK_DIM), D_BLOCK_DIM ** -0.5)
    d_b_x = nrm((L, D_WIDTH), 0.02)
    u = jax.random.uniform(next(ks), (L, D_WIDTH), f32, 0.9, 0.999)
    p = u ** (1.0 / LRU_C)
    d_lambda = jnp.log(p) - jnp.log1p(-p)
    router_w = nrm((L, D_MODEL, N_EXPERTS), D_MODEL ** -0.5)
    router_b = nrm((L, N_EXPERTS), 0.01)
    exp_w_up = nrm((L, N_EXPERTS, D_MODEL, 2 * D_FF), D_MODEL ** -0.5)
    exp_b_up = nrm((L, N_EXPERTS, 2 * D_FF), 0.01)
    exp_w_down = nrm((L, N_EXPERTS, D_FF, D_MODEL), D_FF ** -0.5)
    exp_b_down = nrm((L, N_EXPERTS, D_MODEL), 0.01)
    return {"x": x, "c": c, "ada_w": ada_w, "ada_b": ada_b, "norm1_g": norm1_g, "norm2_g": norm2_g,
            "w_in": w_in, "w_out": w_out, "a_q_gain": a_q_gain, "a_k_gain": a_k_gain,
            "a_lam_q1": a_lam_q1, "a_lam_k1": a_lam_k1, "a_lam_q2": a_lam_q2, "a_lam_k2": a_lam_k2,
            "a_out_gain": a_out_gain, "b_q_gain": b_q_gain, "b_k_gain": b_k_gain,
            "c_w_g2": c_w_g2, "c_b_g": c_b_g, "c_out_gain": c_out_gain,
            "d_conv_w": d_conv_w, "d_conv_b": d_conv_b, "d_w_a": d_w_a, "d_b_a": d_b_a,
            "d_w_x": d_w_x, "d_b_x": d_b_x, "d_lambda": d_lambda,
            "router_w": router_w, "router_b": router_b, "exp_w_up": exp_w_up, "exp_b_up": exp_b_up,
            "exp_w_down": exp_w_down, "exp_b_down": exp_b_down}

def first_block(x, c, ada_w, ada_b, norm1_g, norm2_g, w_in, w_out, a_q_gain, a_k_gain,
              a_lam_q1, a_lam_k1, a_lam_q2, a_lam_k2, a_out_gain, b_q_gain, b_k_gain,
              c_w_g2, c_b_g, c_out_gain, d_conv_w, d_conv_b, d_w_a, d_b_a, d_w_x, d_b_x, d_lambda,
              router_w, router_b, exp_w_up, exp_b_up, exp_w_down, exp_b_down):
    cond = jax.nn.silu(c)
    for l in range(DEPTH):
        mod = cond @ ada_w[l] + ada_b[l]
        sh1, sc1, g1, sh2, sc2, g2 = jnp.split(mod, 6, axis=-1)
        h = rms_norm(x, norm1_g[l]) * (1.0 + sc1[:, None, :]) + sh1[:, None, :]
        y = hybrid_mixer(h, w_in[l], w_out[l], a_q_gain[l], a_k_gain[l], a_lam_q1[l], a_lam_k1[l],
                         a_lam_q2[l], a_lam_k2[l], a_out_gain[l], b_q_gain[l], b_k_gain[l],
                         c_w_g2[l], c_b_g[l], c_out_gain[l], d_conv_w[l], d_conv_b[l],
                         d_w_a[l], d_b_a[l], d_w_x[l], d_b_x[l], d_lambda[l], l)
        x = x + g1[:, None, :] * y
        h = rms_norm(x, norm2_g[l]) * (1.0 + sc2[:, None, :]) + sh2[:, None, :]
        y = moe(h, router_w[l], router_b[l], exp_w_up[l], exp_b_up[l], exp_w_down[l], exp_b_down[l])
        x = x + g2[:, None, :] * y
    return x


DEPTH_2 = 2

NSA_HEADS = 8
NSA_KV_GROUPS = 2
NSA_HEAD_DIM = 64
NSA_BRANCHES = 3
CMP_BLOCK = 32
CMP_STRIDE = 16
CMP_HIDDEN = 256
SEL_BLOCK = 64
N_SELECT = 16
N_LOCAL = 2
WINDOW = 512
NSA_Q_CHUNK = 64

MLA_HEADS = 8
MLA_NOPE_DIM = 64
MLA_ROPE_DIM = 32
MLA_V_DIM = 64
Q_LORA_RANK = 256
KV_LORA_RANK = 128
ATTN_BLOCK = 128

D_FF_2 = 4 * D_MODEL
ROPE_THETA = 10000.0
NORM_EPS = 1e-6
NEG_INF = -1e30
FORCE_BONUS = 1e4

NSA_WIDTH = NSA_HEADS * NSA_HEAD_DIM
NSA_KV_WIDTH = NSA_KV_GROUPS * NSA_HEAD_DIM
MLA_WIDTH = MLA_HEADS * MLA_V_DIM
MIX_WIDTH = NSA_WIDTH + MLA_WIDTH
IN_SIZES = (NSA_WIDTH, NSA_KV_WIDTH, NSA_KV_WIDTH, NSA_KV_WIDTH, NSA_KV_WIDTH,
            NSA_KV_WIDTH, NSA_KV_WIDTH, NSA_BRANCHES * NSA_HEADS,
            Q_LORA_RANK, KV_LORA_RANK, MLA_ROPE_DIM)
IN_WIDTH = sum(IN_SIZES)


def _rms_norm(x, gain):
    xf = x.astype(jnp.float32)
    y = xf * lax.rsqrt(jnp.mean(xf * xf, axis=-1, keepdims=True) + NORM_EPS)
    return (y * gain.astype(jnp.float32)).astype(x.dtype)

def _rope_tables(seq, dim, dtype):
    inv_freq = 1.0 / (ROPE_THETA ** (jnp.arange(0, dim, 2, dtype=jnp.float32) / dim))
    ang = jnp.arange(seq, dtype=jnp.float32)[:, None] * inv_freq[None, :]
    ang = jnp.concatenate([ang, ang], axis=-1)
    return jnp.cos(ang).astype(dtype), jnp.sin(ang).astype(dtype)

def _rope(x, cos, sin):
    half = x.shape[-1] // 2
    rot = jnp.concatenate([-x[..., half:], x[..., :half]], axis=-1)
    return x * cos[:, None, :] + rot * sin[:, None, :]

def _masked_softmax(s, mask):
    s = jnp.where(mask, s, NEG_INF)
    m = jnp.max(s, axis=-1, keepdims=True)
    e = jnp.where(mask, jnp.exp(s - m), 0.0)
    return e / jnp.maximum(jnp.sum(e, axis=-1, keepdims=True), 1e-30)

def _heads(t, n):
    b, s, w = t.shape
    return t.reshape(b, s, n, w // n)

def _compress(kv, pos_emb, w1, w2):
    B, S, G, dk = kv.shape
    ratio = CMP_BLOCK // CMP_STRIDE
    n_cmp = S // CMP_STRIDE - ratio + 1
    chunks = kv.reshape(B, S // CMP_STRIDE, CMP_STRIDE, G, dk)
    blocks = jnp.concatenate([chunks[:, i:i + n_cmp] for i in range(ratio)], axis=2)
    blocks = blocks + pos_emb[None, None, :, None, :]
    flat = jnp.swapaxes(blocks, 2, 3).reshape(B, n_cmp, G, CMP_BLOCK * dk)
    return jax.nn.silu(flat @ w1) @ w2

def _nsa(q, k_cmp, v_cmp, k_sel, v_sel, k_win, v_win, gates):
    B, S, H, dk = q.shape
    G = k_sel.shape[2]
    R = H // G
    n_cmp = k_cmp.shape[1]
    n_blk = S // SEL_BLOCK
    n_sel = min(N_SELECT, n_blk)
    QC = NSA_Q_CHUNK
    scale = dk ** -0.5
    qg = q.reshape(B, S, G, R, dk)
    gg = gates.reshape(B, S, G, R, NSA_BRANCHES)
    k_blocks = k_sel.reshape(B, n_blk, SEL_BLOCK, G, dk).transpose(0, 3, 1, 2, 4)
    v_blocks = v_sel.reshape(B, n_blk, SEL_BLOCK, G, dk).transpose(0, 3, 1, 2, 4)
    pad = ((0, 0), (WINDOW, 0), (0, 0), (0, 0))
    k_win_pad = jnp.pad(k_win, pad)
    v_win_pad = jnp.pad(v_win, pad)
    cmp_end = jnp.arange(n_cmp) * CMP_STRIDE + CMP_BLOCK - 1
    blk_ids = jnp.arange(n_blk)
    a = SEL_BLOCK // CMP_STRIDE
    b = CMP_BLOCK // CMP_STRIDE
    overlap = np.convolve(np.ones(a), np.ones(b))
    bi = jnp.arange(B)[:, None, None, None]
    gi = jnp.arange(G)[None, :, None, None]

    def chunk(c):
        s0 = c * QC
        t = s0 + jnp.arange(QC)
        qc = lax.dynamic_slice_in_dim(qg, s0, QC, axis=1)
        gc = lax.dynamic_slice_in_dim(gg, s0, QC, axis=1)
        s_cmp = jnp.einsum('bqgrd,bngd->bgrqn', qc, k_cmp, preferred_element_type=jnp.float32) * scale
        p_cmp = _masked_softmax(s_cmp, cmp_end[None, :] <= t[:, None])
        o_cmp = jnp.einsum('bgrqn,bngd->bqgrd', p_cmp.astype(v_cmp.dtype), v_cmp)
        imp = jnp.pad(p_cmp.sum(axis=2), ((0, 0), (0, 0), (0, 0), (b - 1, b - 1)))
        imp_blk = sum(float(overlap[j]) * imp[..., j:j + a * (n_blk - 1) + 1:a] for j in range(a + b - 1))
        cur = t // SEL_BLOCK
        valid = blk_ids[None, :] <= cur[:, None]
        forced = valid & ((blk_ids[None, :] == 0) | (blk_ids[None, :] > cur[:, None] - N_LOCAL))
        score = jnp.where(forced, FORCE_BONUS, jnp.where(valid, imp_blk, -1.0))
        _, idx = lax.top_k(score, n_sel)
        k_g = k_blocks[bi, gi, idx]
        v_g = v_blocks[bi, gi, idx]
        key_pos = idx[..., None] * SEL_BLOCK + jnp.arange(SEL_BLOCK)
        m_sel = (key_pos <= t[:, None, None]).reshape(B, G, 1, QC, n_sel * SEL_BLOCK)
        s_sel = jnp.einsum('bqgrd,bgqnkd->bgrqnk', qc, k_g, preferred_element_type=jnp.float32) * scale
        p_sel = _masked_softmax(s_sel.reshape(B, G, R, QC, n_sel * SEL_BLOCK), m_sel)
        o_sel = jnp.einsum('bgrqj,bgqjd->bqgrd', p_sel.astype(v_g.dtype),
                           v_g.reshape(B, G, QC, n_sel * SEL_BLOCK, dk))
        kw = lax.dynamic_slice_in_dim(k_win_pad, s0, WINDOW + QC, axis=1)
        vw = lax.dynamic_slice_in_dim(v_win_pad, s0, WINDOW + QC, axis=1)
        win_pos = s0 - WINDOW + jnp.arange(WINDOW + QC)
        m_win = ((win_pos[None, :] <= t[:, None]) & (win_pos[None, :] > t[:, None] - WINDOW)
                 & (win_pos[None, :] >= 0))
        s_win = jnp.einsum('bqgrd,bkgd->bgrqk', qc, kw, preferred_element_type=jnp.float32) * scale
        p_win = _masked_softmax(s_win, m_win)
        o_win = jnp.einsum('bgrqk,bkgd->bqgrd', p_win.astype(vw.dtype), vw)
        return gc[..., 0:1] * o_cmp + gc[..., 1:2] * o_sel + gc[..., 2:3] * o_win

    out = lax.map(chunk, jnp.arange(S // QC))
    return jnp.swapaxes(out, 0, 1).reshape(B, S, H * dk)

def _causal_attention(q, k, v):
    B, S, H, dk = q.shape
    dv = v.shape[-1]
    scale = dk ** -0.5
    kpos = jnp.arange(S)

    def block(c):
        s0 = c * ATTN_BLOCK
        qb = lax.dynamic_slice_in_dim(q, s0, ATTN_BLOCK, axis=1)
        s = jnp.einsum('bqhd,bkhd->bhqk', qb, k, preferred_element_type=jnp.float32) * scale
        mask = kpos[None, :] <= (s0 + jnp.arange(ATTN_BLOCK))[:, None]
        p = _masked_softmax(s, mask)
        return jnp.einsum('bhqk,bkhd->bqhd', p.astype(v.dtype), v)

    out = lax.map(block, jnp.arange(S // ATTN_BLOCK))
    return jnp.swapaxes(out, 0, 1).reshape(B, S, H, dv)

def _mla(c_q, c_kv, k_rope, q_norm, w_q_up, kv_norm, w_kv_up, cos, sin):
    B, S, _ = c_q.shape
    q = (_rms_norm(c_q, q_norm) @ w_q_up).reshape(B, S, MLA_HEADS, MLA_NOPE_DIM + MLA_ROPE_DIM)
    q = jnp.concatenate([q[..., :MLA_NOPE_DIM], _rope(q[..., MLA_NOPE_DIM:], cos, sin)], axis=-1)
    kv = (_rms_norm(c_kv, kv_norm) @ w_kv_up).reshape(B, S, MLA_HEADS, MLA_NOPE_DIM + MLA_V_DIM)
    k_nope, v = kv[..., :MLA_NOPE_DIM], kv[..., MLA_NOPE_DIM:]
    k_pe = _rope(k_rope[:, :, None, :], cos, sin)
    k = jnp.concatenate([k_nope, jnp.broadcast_to(k_pe, (B, S, MLA_HEADS, MLA_ROPE_DIM))], axis=-1)
    return _causal_attention(q, k, v).reshape(B, S, MLA_WIDTH)

def second_inputs(seed: int = 0) -> dict:
    key = jax.random.key(seed)
    ks = jax.random.split(key, 20)
    L = DEPTH_2
    dk = NSA_HEAD_DIM

    def dense(k, shape, fan_in):
        return jax.random.normal(k, shape, jnp.float32) * fan_in ** -0.5

    def gain(k, shape):
        return 1.0 + 0.02 * jax.random.normal(k, shape, jnp.float32)

    return {
        "x": jax.random.normal(ks[0], (BATCH, SEQ, D_MODEL), jnp.float32),
        "attn_norm": gain(ks[1], (L, D_MODEL)),
        "w_in": dense(ks[2], (L, D_MODEL, IN_WIDTH), D_MODEL),
        "cmp_pos_k": 0.1 * jax.random.normal(ks[3], (L, CMP_BLOCK, dk), jnp.float32),
        "cmp_w1_k": dense(ks[4], (L, CMP_BLOCK * dk, CMP_HIDDEN), CMP_BLOCK * dk),
        "cmp_w2_k": dense(ks[5], (L, CMP_HIDDEN, dk), CMP_HIDDEN),
        "cmp_pos_v": 0.1 * jax.random.normal(ks[6], (L, CMP_BLOCK, dk), jnp.float32),
        "cmp_w1_v": dense(ks[7], (L, CMP_BLOCK * dk, CMP_HIDDEN), CMP_BLOCK * dk),
        "cmp_w2_v": dense(ks[8], (L, CMP_HIDDEN, dk), CMP_HIDDEN),
        "mla_q_norm": gain(ks[9], (L, Q_LORA_RANK)),
        "w_q_up": dense(ks[10], (L, Q_LORA_RANK, MLA_HEADS * (MLA_NOPE_DIM + MLA_ROPE_DIM)), Q_LORA_RANK),
        "mla_kv_norm": gain(ks[11], (L, KV_LORA_RANK)),
        "w_kv_up": dense(ks[12], (L, KV_LORA_RANK, MLA_HEADS * (MLA_NOPE_DIM + MLA_V_DIM)), KV_LORA_RANK),
        "nsa_out_norm": gain(ks[13], (L, NSA_WIDTH)),
        "mla_out_norm": gain(ks[14], (L, MLA_WIDTH)),
        "w_out": dense(ks[15], (L, MIX_WIDTH, D_MODEL), MIX_WIDTH),
        "mlp_norm": gain(ks[16], (L, D_MODEL)),
        "w_ff1": dense(ks[17], (L, D_MODEL, D_FF_2), D_MODEL),
        "w_ff2": dense(ks[18], (L, D_FF_2, D_MODEL), D_FF_2),
        "final_norm": gain(ks[19], (D_MODEL,)),
    }

def second_block(x, attn_norm, w_in, cmp_pos_k, cmp_w1_k, cmp_w2_k, cmp_pos_v, cmp_w1_v, cmp_w2_v,
              mla_q_norm, w_q_up, mla_kv_norm, w_kv_up, nsa_out_norm, mla_out_norm, w_out,
              mlp_norm, w_ff1, w_ff2, final_norm):
    B, S, _ = x.shape
    cos_a, sin_a = _rope_tables(S, NSA_HEAD_DIM, x.dtype)
    cos_b, sin_b = _rope_tables(S, MLA_ROPE_DIM, x.dtype)
    offsets = [int(o) for o in np.cumsum(IN_SIZES)[:-1]]
    G = NSA_KV_GROUPS
    for l in range(DEPTH_2):
        h = _rms_norm(x, attn_norm[l])
        proj = h @ w_in[l]
        (q_a, k_c, v_c, k_s, v_s, k_w, v_w, g_a, c_q, c_kv, k_r) = jnp.split(proj, offsets, axis=-1)
        q_a = _rope(_heads(q_a, NSA_HEADS), cos_a, sin_a)
        k_cmp = _compress(_rope(_heads(k_c, G), cos_a, sin_a), cmp_pos_k[l], cmp_w1_k[l], cmp_w2_k[l])
        v_cmp = _compress(_heads(v_c, G), cmp_pos_v[l], cmp_w1_v[l], cmp_w2_v[l])
        gates = jax.nn.sigmoid(g_a).reshape(B, S, NSA_HEADS, NSA_BRANCHES)
        o_a = _nsa(q_a, k_cmp, v_cmp,
                   _rope(_heads(k_s, G), cos_a, sin_a), _heads(v_s, G),
                   _rope(_heads(k_w, G), cos_a, sin_a), _heads(v_w, G), gates)
        o_b = _mla(c_q, c_kv, k_r, mla_q_norm[l], w_q_up[l], mla_kv_norm[l], w_kv_up[l], cos_b, sin_b)
        mixed = jnp.concatenate([_rms_norm(o_a, nsa_out_norm[l]), _rms_norm(o_b, mla_out_norm[l])], axis=-1)
        x = x + mixed @ w_out[l]
        h = _rms_norm(x, mlp_norm[l])
        x = x + jnp.square(jax.nn.relu(h @ w_ff1[l])) @ w_ff2[l]
    return _rms_norm(x, final_norm)


def setup_inputs(seed=0):
    out = dict(first_inputs(seed))
    for name, value in second_inputs(seed + 1).items():
        if name != "x":
            out[name + "_2"] = value
    return out


def reference(
    x, c, ada_w, ada_b, norm1_g, norm2_g, w_in, w_out, a_q_gain, a_k_gain, a_lam_q1, a_lam_k1,
    a_lam_q2, a_lam_k2, a_out_gain, b_q_gain, b_k_gain, c_w_g2, c_b_g, c_out_gain, d_conv_w,
    d_conv_b, d_w_a, d_b_a, d_w_x, d_b_x, d_lambda, router_w, router_b, exp_w_up, exp_b_up,
    exp_w_down, exp_b_down, attn_norm_2, w_in_2, cmp_pos_k_2, cmp_w1_k_2, cmp_w2_k_2,
    cmp_pos_v_2, cmp_w1_v_2, cmp_w2_v_2, mla_q_norm_2, w_q_up_2, mla_kv_norm_2, w_kv_up_2,
    nsa_out_norm_2, mla_out_norm_2, w_out_2, mlp_norm_2, w_ff1_2, w_ff2_2, final_norm_2,
):
    x = first_block(
        x, c, ada_w, ada_b, norm1_g, norm2_g, w_in, w_out, a_q_gain, a_k_gain, a_lam_q1,
        a_lam_k1, a_lam_q2, a_lam_k2, a_out_gain, b_q_gain, b_k_gain, c_w_g2, c_b_g, c_out_gain,
        d_conv_w, d_conv_b, d_w_a, d_b_a, d_w_x, d_b_x, d_lambda, router_w, router_b, exp_w_up,
        exp_b_up, exp_w_down, exp_b_down,
    )
    return second_block(
        x, attn_norm_2, w_in_2, cmp_pos_k_2, cmp_w1_k_2, cmp_w2_k_2, cmp_pos_v_2, cmp_w1_v_2,
        cmp_w2_v_2, mla_q_norm_2, w_q_up_2, mla_kv_norm_2, w_kv_up_2, nsa_out_norm_2,
        mla_out_norm_2, w_out_2, mlp_norm_2, w_ff1_2, w_ff2_2, final_norm_2,
    )


_drawn_inputs = setup_inputs


def setup_inputs(seed=0):
    import zlib

    import numpy as np

    out = dict(_drawn_inputs(seed))
    spreads = {}
    factors = {'a_q_gain': 6.613,
     'a_k_gain': 6.739,
     'a_lam_q1': 2.844,
     'a_lam_k1': 4.531,
     'a_lam_q2': 200.0,
     'b_q_gain': 8.0,
     'b_k_gain': 8.0,
     'c_b_g': 6.244,
     'c_out_gain': 6.771,
     'd_b_a': 8.0,
     'd_b_x': 8.0,
     'router_b': 4.732,
     'exp_b_up': 8.0,
     'exp_b_down': 8.0,
     'cmp_pos_k_2': 7.894,
     'mla_q_norm_2': 8.0,
     'mla_kv_norm_2': 3.315,
     'nsa_out_norm_2': 4.198,
     'mla_out_norm_2': 4.234,
     'mlp_norm_2': 2.885}
    for name, (base, spread) in spreads.items():
        noise = np.random.default_rng([zlib.crc32(name.encode()), seed]).standard_normal(out[name].shape)
        drawn = base * np.exp(spread * noise) if base else spread * noise
        out[name] = __import__('jax').numpy.asarray(drawn.astype(out[name].dtype))
    for name, factor in factors.items():
        out[name] = (out[name] * factor).astype(out[name].dtype)
    return out
```

```python
import math
from contextlib import ExitStack, contextmanager

import numpy as np

import concourse.bass as bass
from concourse import mybir

F32 = mybir.dt.float32
I32 = mybir.dt.int32
U32 = mybir.dt.uint32
ALU = mybir.AluOpType
ACT = mybir.ActivationFunctionType
X = mybir.AxisListType.X

P = 128
S = 512
NT = S // P
D = 1024
ND = D // P
EPS = 1e-6
NEG = -1e30
COL = 512
SLOTS = 3
SLOT = ND * COL

A_HEADS, A_DK, A_DV = 4, 32, 64
B_HEADS, B_DK = 4, 64
C_HEADS, C_DK, C_DV, C_RANK, C_TAU = 4, 32, 64, 16, 16.0
SUB = 16
NSUB = P // SUB
DECAY_CLAMP = 60.0
W_D = 256
CONV_W = 4
LAM_INIT = 0.8 - 0.6 * math.exp(-0.3 * 0)
NE, TOPK, FF = 32, 4, 1024
MAXB = S * TOPK // P + NE
ALPHA, LIMIT = 1.702, 7.0

OUT_A, OUT_B, OUT_C = 0, 768, 1024
CR = 1792

LAYERS = 2
H2, G2, R2, DK2 = 8, 2, 4, 64
CB, CS, CHID = 32, 16, 256
NCMP = S // CS - 1
CPAD = 32
RQ, RKV, DR, DN, DV2 = 256, 128, 32, 64, 64
DQ = DN + DR
FF2 = 4096


class Job:

    def __init__(self, mm, m, n, evac, eng, chunk=None):
        self.mm, self.m, self.n, self.evac, self.eng, self.chunk = mm, m, n, evac, eng, chunk


class Step:

    def __init__(self, i, q, k, v, out, gate=None):
        self.i, self.q, self.k, self.v, self.out, self.gate = i, q, k, v, out, gate


class Chain:

    def __init__(self, engine, sem):
        self.engine, self.sem, self.n = engine, sem, 0

    def __call__(self, instruction):
        self.n += 1
        instruction.then_inc(self.sem, 1)
        self.engine.wait_ge(self.sem, self.n)


def host_constants():
    p = np.arange(P)
    tok = np.arange(S)
    f32 = np.float32
    out = {}
    out["ident"] = np.eye(P, dtype=f32)
    out["causal_bias"] = np.where(p[None, :] <= p[:, None], 0.0, NEG).astype(f32)
    out["upper_incl"] = (p[:, None] <= p[None, :]).astype(f32)
    out["upper_strict"] = (p[:, None] < p[None, :]).astype(f32)
    out["iota"] = np.tile(np.arange(P, dtype=f32), (P, 1))
    out["place_no"] = (1 + TOPK * tok.reshape(NT, P).T[:, :, None] + np.arange(TOPK)).reshape(P, NT * TOPK).astype(f32)
    out["spare_no"] = (1 + TOPK * S + p[:, None]).astype(f32)
    n = np.arange(CPAD)
    seen = (n[None, :] * CS + CB - 1 <= tok[:, None]) & (n[None, :] < NCMP)
    seen = np.ascontiguousarray(seen.reshape(NT, P, CPAD).transpose(1, 0, 2))
    out["cmp_mask"] = seen.astype(f32)
    out["cmp_bias"] = np.where(seen, 0.0, NEG).astype(f32)
    for name, dim in (("a", DK2), ("b", DR)):
        inv = (1.0 / (np.float32(10000.0) ** (np.arange(0, dim, 2, dtype=f32) / np.float32(dim)))).astype(f32)
        ang = (tok.astype(f32)[:, None] * inv[None, :]).astype(f32)
        ang = np.concatenate([ang, ang], axis=-1)
        sign = np.where(np.arange(dim) < dim // 2, -1.0, 1.0).astype(f32)
        out[f"cos_{name}"] = np.ascontiguousarray(np.cos(ang).astype(f32).reshape(NT, P, dim).transpose(1, 0, 2))
        out[f"sin_{name}"] = np.ascontiguousarray((np.sin(ang) * sign).astype(f32).reshape(NT, P, dim).transpose(1, 0, 2))
    return out




def plan_chunks(a):
    plan = []

    def cols(key, w, c0, c1):
        plan.append((key, [(0, w.shape[0] // P * (c1 - c0), w[:, c0:c1].rearrange("(k p) n -> p k n", p=P), c1 - c0)]))

    for n in range(12):
        cols(("ada", n), a["ada_w"][0], n * COL, (n + 1) * COL)
    for n, (c0, c1) in enumerate(IN1):
        cols(("in1", n), a["w_in"][0], c0, c1)
    for n in range(2):
        cols(("out1", n), a["w_out"][0], n * COL, (n + 1) * COL)
    for l in range(LAYERS):
        for n, (c0, c1) in enumerate(IN2):
            cols(("in2", l, n), a["w_in_2"][l], c0, c1)
        for kv in "kv":
            w = a[f"cmp_w1_{kv}_2"][l].rearrange("(k p) n -> p k n", p=P)
            plan.append((("cmp", l, kv), [(0, 16 * CHID, w, CHID)]))
        plan.append((("up", l), [
            (0, 2 * H2 * DQ, a["w_q_up_2"][l].rearrange("(k p) n -> p k n", p=P), H2 * DQ),
            (2 * H2 * DQ, H2 * (DN + DV2), a["w_kv_up_2"][l].rearrange("(k p) n -> p k n", p=P), H2 * (DN + DV2)),
        ]))
        for n in range(2):
            cols(("out2", l, n), a["w_out_2"][l], n * COL, (n + 1) * COL)
        for n in range(FF2 // COL):
            cols(("ff1", l, n), a["w_ff1_2"][l], n * COL, (n + 1) * COL)
        for half in range(2):
            for q in range(4):
                w = a["w_ff2_2"][l][q * D:(q + 1) * D, half * COL:(half + 1) * COL].rearrange("(k p) n -> p k n", p=P)
                plan.append((("ff2", l, half, q), [(0, SLOT, w, COL)]))
    return plan


IN1 = [(0, 512), (512, 1024), (1024, 1536), (1536, 2048), (2048, 2320), (2320, 2832)]
IN2 = [(0, 512), (512, 1024), (1024, 1536), (1536, 1720)]


def chunk_view(k, key):
    n = k.chunk_no[key]
    base = (n % SLOTS) * SLOT
    _, parts = k.plan[n]
    return [k.ring[:, base + off:base + off + size].rearrange("p (k n) -> p k n", n=width)
            for off, size, _, width in parts]


def wait_chunk(k, eng, key):
    n = k.chunk_no[key]
    eng.wait_ge(k.ring_loaded[n % SLOTS], k.loaded_at[n])


def load_chunks(k, sp, last_key):
    limit = k.chunk_no[last_key] + SLOTS if last_key is not None else SLOTS - 1
    while k.next_load <= min(limit, k.load_end):
        n = k.next_load
        if n >= SLOTS:
            sp.wait_ge(k.groups_done, k.last_group[n - SLOTS])
        base = (n % SLOTS) * SLOT
        for off, size, src, width in k.plan[n][1]:
            sp.dma_start(k.ring[:, base + off:base + off + size].rearrange("p (k n) -> p k n", n=width),
                         src).then_inc(k.ring_loaded[n % SLOTS], 16)
        k.next_load += 1




def gemm_stage(k, name, jobs, banks=8, last_key=None, extra=None):
    nc = k.nc
    first = k.n_groups
    for n, job in enumerate(jobs):
        if job.chunk is not None:
            k.last_group[k.chunk_no[job.chunk]] = first + n + 1
    k.n_groups += len(jobs)
    order = {"act": [n for n, j in enumerate(jobs) if j.eng == "act"],
             "dve": [n for n, j in enumerate(jobs) if j.eng == "dve"]}
    rank = {n: i for e in order for i, n in enumerate(order[e])}
    with ExitStack() as ctx:
        evac_done = {e: nc.alloc_semaphore(f"{name}_{e}_evacuated") for e in order}
        evac_step = {e: nc.alloc_semaphore(f"{name}_{e}_step") for e in order}
        bank = [ctx.enter_context(nc.psum_tensor(f"{name}_bank{i}", [P, COL], F32)) for i in range(banks)]
        block = ctx.enter_context(nc.Block())

        @block.sync
        def _(sp):
            if last_key is not None:
                load_chunks(k, sp, last_key)

        @block.tensor
        def _(pe):
            seen = None
            for n, job in enumerate(jobs):
                if job.chunk is not None and job.chunk != seen:
                    wait_chunk(k, pe, job.chunk)
                    seen = job.chunk
                if n >= banks:
                    e = jobs[n - banks].eng
                    pe.wait_ge(evac_done[e], rank[n - banks] + 1)
                out = bank[n % banks][:job.m, :job.n]
                for i, (lhsT, rhs) in enumerate(job.mm):
                    mm = nc.tensor.matmul(out, lhsT, rhs, start=(i == 0), stop=(i == len(job.mm) - 1))
                mm.then_inc(k.groups_done, 1)

        def evacuate(eng, e):
            chain = Chain(eng, evac_step[e])
            for i, n in enumerate(order[e]):
                eng.wait_ge(k.groups_done, first + n + 1)
                if i >= 1:
                    eng.wait_ge(evac_done[e], i)
                jobs[n].evac(jobs[n].eng, chain, bank[n % banks][:jobs[n].m, :jobs[n].n]).then_inc(evac_done[e], 1)

        @block.scalar
        def _(act):
            evacuate(act, "act")

        @block.vector
        def _(dve):
            evacuate(dve, "dve")


def copy_to(k, dst, scale=None, bias=None):
    nc = k.nc

    def evac(e, chain, psum):
        src = psum if dst.shape == psum.shape else psum
        if e == "act":
            if scale is None and bias is None:
                return nc.scalar.activation(dst, src, ACT.Copy)
            return nc.scalar.activation(dst, src, ACT.Identity, bias=bias if bias is not None else 0.0,
                                        scale=scale if scale is not None else 1.0)
        if scale is None and bias is None:
            return nc.vector.tensor_copy(dst, src)
        if scale is None:
            return nc.vector.tensor_scalar(dst, src, bias, None, ALU.add)
        if bias is None:
            return nc.vector.tensor_scalar(dst, src, scale, None, ALU.mult)
        return nc.vector.tensor_scalar(dst, src, scale, bias, ALU.mult, ALU.add)
    return evac


def engine_of(n):
    return "act" if n % 2 == 0 else "dve"




def transpose_stage(k, name, blocks, last_key=None):
    nc = k.nc
    with ExitStack() as ctx:
        turned = nc.alloc_semaphore(f"{name}_turned")
        taken = [nc.alloc_semaphore(f"{name}_taken_{e}") for e in ("act", "dve")]
        bank = [ctx.enter_context(nc.psum_tensor(f"{name}_bank{i}", [P, COL], F32)) for i in range(4)]
        block = ctx.enter_context(nc.Block())

        @block.sync
        def _(sp):
            if last_key is not None:
                load_chunks(k, sp, last_key)

        @block.tensor
        def _(pe):
            for n, (src, _, _, _) in enumerate(blocks):
                if n >= 4:
                    pe.wait_ge(taken[n % 2], (n - 4) // 2 + 1)
                w = src[0].shape[-1] if len(src[0].shape) == 2 else src[0].shape[1] * src[0].shape[2]
                for t in range(NT):
                    tr = nc.tensor.transpose(bank[n % 4][:w, t * P:(t + 1) * P], src[t], k.ident[:])
                tr.then_inc(turned, 1)

        def take(eng, e):
            for n, (src, dst, scale, bias) in enumerate(blocks):
                if n % 2 == e:
                    eng.wait_ge(turned, n + 1)
                    lo, w = (dst[1], dst[0].shape[0]) if isinstance(dst, tuple) else (0, dst.shape[0])
                    out = dst[0] if isinstance(dst, tuple) else dst
                    copy_to(k, out, scale, bias)("act" if e == 0 else "dve", None,
                                                 bank[n % 4][lo:lo + w, :]).then_inc(taken[e], 1)

        @block.scalar
        def _(act):
            take(act, 0)

        @block.vector
        def _(dve):
            take(dve, 1)


def rms_stage(k, name, groups):
    nc = k.nc
    with ExitStack() as ctx:
        squares = nc.alloc_semaphore(f"{name}_sums")
        roots = nc.alloc_semaphore(f"{name}_roots")
        step = nc.alloc_semaphore(f"{name}_step")
        sq = ctx.enter_context(nc.sbuf_tensor(f"{name}_sq", [P, 1024], F32))
        total = sum(g[0].shape[1] for g in groups)
        ss = ctx.enter_context(nc.sbuf_tensor(f"{name}_ss", [P, total], F32))
        rms = ctx.enter_context(nc.sbuf_tensor(f"{name}_rms", [P, total], F32))
        rinv = ctx.enter_context(nc.sbuf_tensor(f"{name}_rinv", [P, total], F32))
        block = ctx.enter_context(nc.Block())
        at = [sum(g[0].shape[1] for g in groups[:i]) for i in range(len(groups))]

        @block.vector
        def _(dve):
            chain = Chain(dve, step)
            for i, (src, dst, w, gain) in enumerate(groups):
                n = src.shape[1]
                tmp = sq[:, 0:n * w].rearrange("p (n w) -> p n w", w=w)
                chain(nc.vector.tensor_tensor(tmp, src, src, ALU.mult))
                nc.vector.tensor_reduce(ss[:, at[i]:at[i] + n], tmp, X, ALU.add).then_inc(squares, 1)
                dve.wait_ge(squares, i + 1)
            for i, (src, dst, w, gain) in enumerate(groups):
                n = src.shape[1]
                r = rinv[:, at[i]:at[i] + n]
                dve.wait_ge(roots, i + 1)
                chain(nc.vector.reciprocal(r, rms[:, at[i]:at[i] + n]))
                if gain is None:
                    chain(nc.vector.tensor_tensor(dst, src, r.unsqueeze(2).to_broadcast([P, n, w]), ALU.mult))
                else:
                    chain(nc.vector.tensor_tensor(dst, src, r.unsqueeze(2).to_broadcast([P, n, w]), ALU.mult))
                    chain(nc.vector.tensor_tensor(dst, dst, gain.unsqueeze(1).to_broadcast([P, n, w]), ALU.mult))

        @block.scalar
        def _(act):
            for i, (src, dst, w, gain) in enumerate(groups):
                n = src.shape[1]
                act.wait_ge(squares, i + 1)
                nc.scalar.activation(rms[:, at[i]:at[i] + n], ss[:, at[i]:at[i] + n], ACT.Sqrt,
                                     bias=k.eps[:], scale=1.0 / w).then_inc(roots, 1)


def row_norm_groups(src, dst, gain=None):
    return [(src[:, t:t + 1, :], dst[:, t:t + 1, :], src.shape[2], gain) for t in range(NT)]


def columns_of(src, c0, w):
    return [src[:, t, c0:c0 + w] for t in range(NT)]




def attention_stage(k, name, steps, scale, pair, lam=None, gated=False, last_key=None):
    nc = k.nc
    maps = 2
    turns = 1 if pair else 2
    with ExitStack() as ctx:
        def sem(s):
            return nc.alloc_semaphore(f"{name}_{s}")

        def sb(s, shape):
            return ctx.enter_context(nc.sbuf_tensor(f"{name}_{s}", shape, F32))

        scores_ready, bias_ready, exp_ready = sem("scores"), sem("bias"), sem("exp")
        weights_ready, turned = sem("weights"), sem("turned")
        taken_act, taken_dve, values_ready, out_taken = sem("taken_act"), sem("taken_dve"), sem("values"), sem("out")
        step_dve = sem("step")
        p = sb("p", [P, 2, maps, S])
        pt = sb("pt", [P, 2, turns, S])
        w = sb("w", [P, 2, S]) if pair else None
        top = sb("top", [P, 2, maps])
        neg = sb("neg", [P, 2, maps])
        total = sb("total", [P, 2, maps])
        inv = sb("inv", [P, 2, maps])
        lam_inv = sb("lam_inv", [P, 2, 1]) if pair else None
        sc = [ctx.enter_context(nc.psum_tensor(f"{name}_s{b}", [P, maps, COL], F32)) for b in range(2)]
        tr = [ctx.enter_context(nc.psum_tensor(f"{name}_t{b}", [P, COL], F32)) for b in range(2)]
        ov = [ctx.enter_context(nc.psum_tensor(f"{name}_o{b}", [P, COL], F32)) for b in range(2)]
        block = ctx.enter_context(nc.Block())
        n_steps = len(steps)

        @block.sync
        def _(sp):
            if last_key is not None:
                load_chunks(k, sp, last_key)

        @block.tensor
        def _(pe):
            def scores(n):
                st, b = steps[n], n % 2
                nk = P * (st.i + 1)
                if n >= 2:
                    pe.wait_ge(exp_ready, maps * (n - 1))
                for m in range(maps):
                    nc.tensor.matmul(sc[b][:, m, 0:nk], st.q[m], st.k[m][:, 0:nk], start=True, stop=False)
                    mm = nc.tensor.matmul(sc[b][:, m, nk - P:nk], k.ident[:], k.causal_bias[:], start=False, stop=True)
                mm.then_inc(scores_ready, 1)

            def values(n):
                st, b = steps[n], n % 2
                src = w if pair else p
                for m in range(turns):
                    u = n * turns + m
                    if pair:
                        pe.wait_ge(weights_ready, n + 1)
                    else:
                        pe.wait_ge(exp_ready, maps * n + m + 1)
                    if u >= 2:
                        pe.wait_ge(taken_act if u % 2 == 0 else taken_dve, (u - 2) // 2 + 1)
                    for j in range(st.i + 1):
                        row = w[:, b, j * P:(j + 1) * P] if pair else p[:, b, m, j * P:(j + 1) * P]
                        t = nc.tensor.transpose(tr[u % 2][:, j * P:(j + 1) * P], row, k.ident[:])
                    t.then_inc(turned, 1)
                if n >= 2:
                    pe.wait_ge(out_taken, n - 1)
                for m in range(turns):
                    u = n * turns + m
                    pe.wait_ge(taken_act if u % 2 == 0 else taken_dve, u // 2 + 1)
                    for j in range(st.i + 1):
                        mm = nc.tensor.matmul(ov[b][:, m * 64:(m + 1) * 64], pt[:, b, m, j * P:(j + 1) * P],
                                              st.v(m, j), start=(j == 0), stop=(j == st.i))
                mm.then_inc(values_ready, 1)

            scores(0)
            for n in range(n_steps):
                if n + 1 < n_steps:
                    scores(n + 1)
                values(n)

        def take_turned(eng, n, m):
            u, b = n * turns + m, n % 2
            nk = P * (steps[n].i + 1)
            if n >= 2:
                eng.wait_ge(values_ready, n - 1)
            eng.wait_ge(turned, u + 1)
            if u % 2 == 0:
                nc.scalar.activation(pt[:, b, m, 0:nk], tr[0][:, 0:nk], ACT.Copy).then_inc(taken_act, 1)
            else:
                nc.vector.tensor_copy(pt[:, b, m, 0:nk], tr[1][:, 0:nk]).then_inc(taken_dve, 1)

        @block.scalar
        def _(act):
            def exps(n):
                st, b = steps[n], n % 2
                nk = P * (st.i + 1)
                act.wait_ge(bias_ready, n + 1)
                if n >= 2:
                    if pair:
                        act.wait_ge(weights_ready, n - 1)
                    else:
                        act.wait_ge(turned, turns * (n - 1))
                    act.wait_ge(out_taken, n - 1)
                for m in range(maps):
                    nc.scalar.activation(p[:, b, m, 0:nk], sc[b][:, m, 0:nk], ACT.Exp, bias=neg[:, b, m:m + 1],
                                         scale=scale, accum_out=total[:, b, m:m + 1]).then_inc(exp_ready, 1)

            exps(0)
            for n in range(n_steps):
                if n + 1 < n_steps:
                    exps(n + 1)
                for m in range(turns):
                    if (n * turns + m) % 2 == 0:
                        take_turned(act, n, m)

        @block.vector
        def _(dve):
            chain = Chain(dve, step_dve)

            def maxima(n):
                st, b = steps[n], n % 2
                nk = P * (st.i + 1)
                dve.wait_ge(scores_ready, n + 1)
                chain(nc.vector.tensor_reduce(top[:, b, :], sc[b][:, :, 0:nk], X, ALU.max))
                if n >= 2:
                    dve.wait_ge(exp_ready, maps * (n - 1))
                nc.vector.tensor_scalar(neg[:, b, :], top[:, b, :], -scale, None, ALU.mult).then_inc(bias_ready, 1)

            maxima(0)
            for n in range(n_steps):
                st, b = steps[n], n % 2
                nk = P * (st.i + 1)
                if n + 1 < n_steps:
                    maxima(n + 1)
                dve.wait_ge(exp_ready, maps * (n + 1))
                chain(nc.vector.reciprocal(inv[:, b, :], total[:, b, :]))
                if gated:
                    chain(nc.vector.tensor_tensor(inv[:, b, :], inv[:, b, :], st.gate, ALU.mult))
                if pair:
                    chain(nc.vector.tensor_tensor(lam_inv[:, b, :], inv[:, b, 1:2], lam, ALU.mult))
                    chain(nc.vector.tensor_scalar(p[:, b, 1, 0:nk], p[:, b, 1, 0:nk], lam_inv[:, b, :], None, ALU.mult))
                    if n >= 2:
                        dve.wait_ge(turned, n - 1)
                    nc.vector.scalar_tensor_tensor(w[:, b, 0:nk], p[:, b, 0, 0:nk], inv[:, b, 0:1], p[:, b, 1, 0:nk],
                                                   ALU.mult, ALU.subtract).then_inc(weights_ready, 1)
                for m in range(turns):
                    if (n * turns + m) % 2 == 1:
                        take_turned(dve, n, m)
                dve.wait_ge(values_ready, n + 1)
                for m in range(turns):
                    last = st.out(chain, ov[b][:, m * 64:(m + 1) * 64], inv[:, b, m:m + 1], m)
                last.then_inc(out_taken, 1)




def load_stage(k, a):
    nc = k.nc
    with ExitStack() as ctx:
        loaded = {e: nc.alloc_semaphore(f"small_{e}_loaded") for e in ("sp", "act")}
        loaded["pool"] = k.small_pool_loaded
        made = nc.alloc_semaphore("constants_made")
        block = ctx.enter_context(nc.Block())
        share = {"sp": k.small[0::3], "act": k.small[1::3], "pool": k.small[2::3]}

        def run(eng, e):
            for dst, src in share[e]:
                eng.dma_start(dst, src, allow_slow_non_contiguous=True).then_inc(loaded[e], 16)

        @block.sync
        def _(sp):
            sp.dma_start(k.x[:], a["x"][0].rearrange("(t p) d -> p t d", p=P)).then_inc(loaded["sp"], 16)
            load_chunks(k, sp, None)
            run(sp, "sp")
            sp.wait_ge(made, 3)
            for dst, src in k.lru_blocks:
                sp.dma_start(dst, src).then_inc(loaded["sp"], 16)
            sp.wait_ge(loaded["sp"], 16 * (len(share["sp"]) + 1 + len(k.lru_blocks)))

        @block.scalar
        def _(act):
            run(act, "act")
            act.wait_ge(loaded["act"], 16 * len(share["act"]))

        @block.gpsimd
        def _(pool):
            run(pool, "pool")
            pool.wait_ge(loaded["pool"], 16 * len(share["pool"]))

        @block.vector
        def _(dve):
            nc.vector.memset(k.eps[:], EPS).then_inc(made, 1)
            nc.vector.memset(k.ones[:], 1.0).then_inc(made, 1)
            nc.vector.memset(k.lru_w[:], 0.0).then_inc(made, 1)


def condition_stage(k, a):
    nc = k.nc
    with ExitStack() as ctx:
        cond = ctx.enter_context(nc.sbuf_tensor("cond", [P, ND], F32))
        cond_rows = ctx.enter_context(nc.sbuf_tensor("cond_rows", [P, ND, P], F32))
        ada_b = ctx.enter_context(nc.sbuf_tensor("ada_b_row", [1, 6 * D], F32))
        first = ctx.enter_context(nc.sbuf_tensor("mod_first", [P, 2, D], F32))
        with ExitStack() as inner:
            activated = nc.alloc_semaphore("cond_activated")
            spread = nc.alloc_semaphore("cond_spread")
            row_loaded = nc.alloc_semaphore("ada_b_loaded")
            block = inner.enter_context(nc.Block())

            @block.sync
            def _(sp):
                sp.dma_start(ada_b[:], a["ada_b"]).then_inc(row_loaded, 16)
                sp.wait_ge(row_loaded, 16)

            @block.scalar
            def _(act):
                nc.scalar.activation(cond[:], k.c_col[:], ACT.Silu).then_inc(activated, 1)

            @block.vector
            def _(dve):
                dve.wait_ge(activated, 1)
                nc.vector.tensor_copy(cond_rows[:], cond[:].unsqueeze(2).to_broadcast([P, ND, P])).then_inc(spread, 1)

        jobs = []
        for n in range(12):
            (w,) = chunk_view(k, ("ada", n))
            mm = [(cond_rows[:, j, :], w[:, j, :]) for j in range(ND)]
            mm.append((k.ones[0:1, :], ada_b[0:1, n * COL:(n + 1) * COL]))
            part, half = divmod(n, 2)
            dst = first[:, part, half * COL:(half + 1) * COL] if part < 2 else k.mod[:, part - 2, half * COL:(half + 1) * COL]
            jobs.append(Job(mm, P, COL, copy_to(k, dst), engine_of(n), ("ada", n)))
        gemm_stage(k, "ada", jobs, last_key=("ada", 11))

        with ExitStack() as inner:
            turned = nc.alloc_semaphore("mod_turned")
            step = nc.alloc_semaphore("mod_step")
            bank = inner.enter_context(nc.psum_tensor("mod_bank", [P, COL], F32))
            block = inner.enter_context(nc.Block())

            @block.tensor
            def _(pe):
                for part in range(2):
                    for j in range(ND):
                        mm = nc.tensor.matmul(bank[:, part * ND + j:part * ND + j + 1], first[0:1, part, j * P:(j + 1) * P],
                                              k.ones[0:1, 0:1], start=True, stop=True)
                mm.then_inc(turned, 1)

            @block.vector
            def _(dve):
                chain = Chain(dve, step)
                dve.wait_ge(turned, 1)
                chain(nc.vector.tensor_copy(k.shift1[:], bank[:, 0:ND]))
                chain(nc.vector.scalar_tensor_tensor(k.scale1[:], bank[:, ND:2 * ND], 1.0, k.norm1[:], ALU.add, ALU.mult))
                chain(nc.vector.scalar_tensor_tensor(k.mod[:, 2, :], k.mod[:, 2, :], 1.0, k.norm2_row[:], ALU.add, ALU.mult))


def project1_stage(k, tok, fm, glow, dxg):
    jobs = []
    n = 0

    def token_major(key, lo, width, dst0):
        nonlocal n
        (w,) = chunk_view(k, key)
        for t in range(NT):
            mm = [(k.hT[:, j, t * P:(t + 1) * P], w[:, j, lo:lo + width]) for j in range(ND)]
            jobs.append(Job(mm, P, width, copy_to(k, tok[:, t, dst0:dst0 + width]), engine_of(n), key))
            n += 1

    def feature_major(key, lo, width, dst):
        nonlocal n
        (w,) = chunk_view(k, key)
        mm = [(w[:, j, lo:lo + width], k.hT[:, j, :]) for j in range(ND)]
        jobs.append(Job(mm, width, S, copy_to(k, dst), engine_of(n), key))
        n += 1

    for c in range(3):
        token_major(("in1", c), 0, COL, c * COL)
    feature_major(("in1", 3), 0, P, fm[:, 0, :])
    feature_major(("in1", 3), P, P, fm[:, 1, :])
    token_major(("in1", 3), 2 * P, 256, 1536)
    feature_major(("in1", 4), 0, C_RANK, glow[0:C_RANK, :])
    token_major(("in1", 4), C_RANK, 256, 1792)
    for j in range(4):
        feature_major(("in1", 5), j * P, P, dxg[:, j, :])
    gemm_stage(k, "in1", jobs, last_key=("in1", 5))


def lambda_stage(k):
    nc = k.nc
    with ExitStack() as ctx:
        dots = nc.alloc_semaphore("lam_dots")
        raised = nc.alloc_semaphore("lam_raised")
        step = nc.alloc_semaphore("lam_step")
        prod = ctx.enter_context(nc.sbuf_tensor("lam_prod", [P, 2, A_DK], F32))
        dot = ctx.enter_context(nc.sbuf_tensor("lam_dot", [P, 2], F32))
        e = ctx.enter_context(nc.sbuf_tensor("lam_exp", [P, 2], F32))
        block = ctx.enter_context(nc.Block())

        @block.vector
        def _(dve):
            chain = Chain(dve, step)
            chain(nc.vector.tensor_tensor(prod[:], k.lam_q[:], k.lam_k[:], ALU.mult))
            nc.vector.tensor_reduce(dot[:], prod[:], X, ALU.add).then_inc(dots, 1)
            dve.wait_ge(raised, 1)
            chain(nc.vector.tensor_tensor(k.lam[:], e[:, 0:1], e[:, 1:2], ALU.subtract))
            chain(nc.vector.tensor_scalar(k.lam[:], k.lam[:], LAM_INIT, None, ALU.add))

        @block.scalar
        def _(act):
            act.wait_ge(dots, 1)
            nc.scalar.activation(e[:], dot[:], ACT.Exp).then_inc(raised, 1)


def gla_stages(k, tok, fm, glow, a):
    nc = k.nc
    qs = C_DK ** -0.5
    with ExitStack() as ctx:
        def sb(s, shape):
            return ctx.enter_context(nc.sbuf_tensor(f"gla_{s}", shape, F32))

        z, b, ex = sb("z", [P, S]), sb("b", [P, S]), sb("ex", [P, S])
        qin, kout = sb("qin", [P, S]), sb("kout", [P, S])
        qsub = sb("qsub", [P, S // SUB, C_HEADS, SUB])
        gemm_stage(k, "gla_gate", [Job([(k.c_wg2[0:C_RANK, :], glow[0:C_RANK, :])], P, S,
                                       copy_to(k, z[:], bias=k.c_bg[:]), "dve")], banks=1)
        with ExitStack() as inner:
            def sem(s):
                return nc.alloc_semaphore(f"gla_{s}")

            soft, cum, raised, zeroed, step, astep = sem("soft"), sem("cum"), sem("raised"), sem("zeroed"), sem("step"), sem("astep")
            diff = inner.enter_context(nc.sbuf_tensor("gla_diff", [P, S], F32))
            end = inner.enter_context(nc.sbuf_tensor("gla_end", [P, S], F32))
            block = inner.enter_context(nc.Block())

            @block.gpsimd
            def _(pool):
                nc.gpsimd.memset(qsub[:], 0.0).then_inc(zeroed, 1)
                nc.gpsimd.memset(k.gla_state[:], 0.0).then_inc(zeroed, 1)

            @block.scalar
            def _(act):
                chain = Chain(act, astep)
                chain(nc.scalar.activation(ex[:], z[:], ACT.Abs))
                chain(nc.scalar.activation(ex[:], ex[:], ACT.Exp, scale=-1.0))
                nc.scalar.activation(ex[:], ex[:], ACT.Ln, bias=k.ones[:, 0:1]).then_inc(soft, 1)
                act.wait_ge(cum, 1)
                nc.scalar.activation(qin[:], b[:], ACT.Exp).then_inc(raised, 1)
                for t in range(NT):
                    nc.scalar.activation(kout[:, t * P:(t + 1) * P], b[:, t * P:(t + 1) * P], ACT.Exp, scale=-1.0,
                                         bias=b[:, t * P + P - 1:t * P + P]).then_inc(raised, 1)
                nc.scalar.activation(k.gla_tile_decay[:], b[:].rearrange("p (t n) -> p t n", n=P)[:, :, P - 1],
                                     ACT.Exp).then_inc(raised, 1)
                act.wait_ge(cum, 2)
                nc.scalar.activation(diff[:], diff[:], ACT.Exp).then_inc(raised, 1)

            @block.vector
            def _(dve):
                chain = Chain(dve, step)
                dve.wait_ge(soft, 1)
                chain(nc.vector.scalar_tensor_tensor(z[:], z[:], 0.0, ex[:], ALU.min, ALU.subtract))
                chain(nc.vector.tensor_scalar(z[:], z[:], 1.0 / C_TAU, None, ALU.mult))
                chain(nc.vector.memset(end[:], 1.0))
                for t in range(NT):
                    c = slice(t * P, (t + 1) * P)
                    scan = nc.vector.tensor_tensor_scan(b[:, c], end[:, c], z[:, c], 0.0, ALU.mult, ALU.add)
                    if t < NT - 1:
                        chain(scan)
                scan.then_inc(cum, 1)
                dve.wait_ge(cum, 1)
                bs = b[:].rearrange("p (n s) -> p n s", s=SUB)
                ref = bs[:, :, SUB // 2:SUB // 2 + 1].to_broadcast([P, S // SUB, SUB])
                nc.vector.tensor_tensor(diff[:].rearrange("p (n s) -> p n s", s=SUB), bs, ref, ALU.subtract).then_inc(cum, 1)
                dve.wait_ge(raised, 1 + NT + 1)
                chain(nc.vector.scalar_tensor_tensor(qin[:], fm[:, 0, :], qs, qin[:], ALU.mult, ALU.mult))
                chain(nc.vector.tensor_tensor(kout[:], fm[:, 1, :], kout[:], ALU.mult))
                dve.wait_ge(raised, 1 + NT + 2)
                dve.wait_ge(zeroed, 2)
                for h in range(C_HEADS):
                    r = slice(h * C_DK, (h + 1) * C_DK)
                    chain(nc.vector.scalar_tensor_tensor(
                        qsub[r, :, h, :], fm[r, 0, :].rearrange("p (n s) -> p n s", s=SUB), qs,
                        diff[r, :].rearrange("p (n s) -> p n s", s=SUB), ALU.mult, ALU.mult))

        with ExitStack() as inner:
            def sem(s):
                return nc.alloc_semaphore(f"gla2_{s}")

            def isb(s, shape):
                return inner.enter_context(nc.sbuf_tensor(f"gla2_{s}", shape, F32))

            def ps(s):
                return inner.enter_context(nc.psum_tensor(f"gla2_{s}", [P, COL], F32))

            spread, raised, keys, att_ready, masked, turned, copied, state_ready, updated, out_ready, out_taken, step = (
                sem(s) for s in ("spread", "raised", "keys", "att_ready", "masked", "turned", "copied", "state_ready",
                                 "updated", "out_ready", "out_taken", "step"))
            ksub = isb("ksub", [P, 2, NSUB, P])
            att = isb("att", [P, C_HEADS, P])
            kt = isb("kt", [P, P])
            att_bank, kt_bank, u_bank, o_bank = ps("att_bank"), ps("kt_bank"), ps("u_bank"), ps("o_bank")
            block = inner.enter_context(nc.Block())
            cv = 1536

            @block.scalar
            def _(act):
                for t in range(NT):
                    act.wait_ge(spread, t + 1)
                    nc.scalar.activation(ksub[:, t % 2], ksub[:, t % 2], ACT.Exp, scale=-1.0).then_inc(raised, 1)

            @block.vector
            def _(dve):
                chain = Chain(dve, step)

                def spread_tile(t):
                    if t >= 2:
                        dve.wait_ge(att_ready, t - 1)
                    bt = b[:, t * P:(t + 1) * P]
                    ref = bt.rearrange("p (n s) -> p n s", s=SUB)[:, :, SUB // 2:SUB // 2 + 1].to_broadcast([P, NSUB, P])
                    chain(nc.vector.tensor_tensor(ksub[:, t % 2], bt.unsqueeze(1).to_broadcast([P, NSUB, P]), ref, ALU.subtract))
                    nc.vector.tensor_scalar(ksub[:, t % 2], ksub[:, t % 2], -DECAY_CLAMP, None, ALU.max).then_inc(spread, 1)

                spread_tile(0)
                for t in range(NT):
                    if t + 1 < NT:
                        spread_tile(t + 1)
                    dve.wait_ge(raised, t + 1)
                    nc.vector.tensor_tensor(ksub[:, t % 2], ksub[:, t % 2],
                                            fm[:, 1, t * P:(t + 1) * P].unsqueeze(1).to_broadcast([P, NSUB, P]),
                                            ALU.mult).then_inc(keys, 1)
                    dve.wait_ge(att_ready, t + 1)
                    if t >= 1:
                        dve.wait_ge(out_ready, t)
                    for h in range(C_HEADS):
                        last = nc.vector.tensor_tensor(
                            att[:, h, :].rearrange("p (n s) -> p n s", s=SUB),
                            att_bank[:].rearrange("p (n h s) -> p n h s", h=C_HEADS, s=SUB)[:, :, h, :],
                            k.upper_incl[:].rearrange("p (n s) -> p n s", s=SUB), ALU.mult)
                        if h < C_HEADS - 1:
                            chain(last)
                    last.then_inc(masked, 1)
                    dve.wait_ge(turned, t + 1)
                    if t >= 1:
                        dve.wait_ge(state_ready, t)
                    nc.vector.tensor_copy(kt[:], kt_bank[:, 0:P]).then_inc(copied, 1)
                    dve.wait_ge(out_ready, t + 1)
                    nc.vector.tensor_copy(tok[:, t, OUT_C:OUT_C + 256], o_bank[:, 0:256]).then_inc(out_taken, 1)
                    dve.wait_ge(state_ready, t + 1)
                    for h in range(C_HEADS):
                        r, e = slice(h * C_DK, (h + 1) * C_DK), slice(h * C_DV, (h + 1) * C_DV)
                        last = nc.vector.scalar_tensor_tensor(k.gla_state[r, e], k.gla_state[r, e], k.gla_tile_decay[r, t:t + 1],
                                                              u_bank[r, e], ALU.mult, ALU.add)
                        if h < C_HEADS - 1:
                            chain(last)
                    last.then_inc(updated, 1)

            @block.tensor
            def _(pe):
                for t in range(NT):
                    c = slice(t * P, (t + 1) * P)
                    pe.wait_ge(keys, t + 1)
                    if t >= 1:
                        pe.wait_ge(masked, t)
                    for i in range(NSUB):
                        mm = nc.tensor.matmul(att_bank[:, i * 64:(i + 1) * 64], ksub[:, t % 2, i, :],
                                              qsub[:, t * NSUB + i].rearrange("p h s -> p (h s)"), start=True, stop=True)
                    mm.then_inc(att_ready, 1)
                    if t >= 1:
                        pe.wait_ge(copied, t)
                    nc.tensor.transpose(kt_bank[:, 0:P], kout[:, c], k.ident[:]).then_inc(turned, 1)
                    if t >= 1:
                        pe.wait_ge(updated, t)
                        pe.wait_ge(out_taken, t)
                    nc.tensor.matmul(o_bank[:, 0:256], qin[:, c], k.gla_state[:], start=True, stop=True)
                    pe.wait_ge(masked, t + 1)
                    for h in range(C_HEADS):
                        mm = nc.tensor.matmul(o_bank[:, h * 64:(h + 1) * 64], att[:, h, :], tok[:, t, cv + h * 64:cv + (h + 1) * 64],
                                              start=False, stop=True, skip_group_check=True)
                    mm.then_inc(out_ready, 1)
                    pe.wait_ge(copied, t + 1)
                    nc.tensor.matmul(u_bank[:, 0:256], kt[:], tok[:, t, cv:cv + 256], start=True, stop=True).then_inc(state_ready, 1)


def gla_gate_stage(k, tok):
    nc = k.nc
    with ExitStack() as ctx:
        opened = nc.alloc_semaphore("gla_opened")
        scaled = nc.alloc_semaphore("gla_scaled")
        r = ctx.enter_context(nc.sbuf_tensor("gla_silu", [P, NT, 256], F32))
        block = ctx.enter_context(nc.Block())

        @block.scalar
        def _(act):
            nc.scalar.activation(r[:], tok[:, :, CR:CR + 256], ACT.Silu).then_inc(opened, 1)

        @block.vector
        def _(dve):
            dve.wait_ge(opened, 1)
            nc.vector.tensor_tensor(tok[:, :, OUT_C:OUT_C + 256], tok[:, :, OUT_C:OUT_C + 256], r[:], ALU.mult).then_inc(scaled, 1)


def lru_stages(k, dxg):
    nc = k.nc
    with ExitStack() as ctx:
        def sb(s, shape):
            return ctx.enter_context(nc.sbuf_tensor(f"lru_{s}", shape, F32))

        xc, gates = sb("xc", [P, 2, S]), sb("gates", [P, 2, 2, S])
        with ExitStack() as inner:
            step = nc.alloc_semaphore("lru_step")
            block = inner.enter_context(nc.Block())

            @block.vector
            def _(dve):
                chain = Chain(dve, step)
                for j in range(2):
                    chain(nc.vector.tensor_scalar(xc[:, j, :], dxg[:, j, :], k.conv_w[:, CONV_W - 1, j:j + 1],
                                                  k.conv_b[:, j:j + 1], ALU.mult, ALU.add))
                    for back in range(1, CONV_W):
                        chain(nc.vector.scalar_tensor_tensor(xc[:, j, back:], dxg[:, j, :S - back],
                                                             k.conv_w[:, CONV_W - 1 - back, j:j + 1], xc[:, j, back:],
                                                             ALU.mult, ALU.add))
        jobs = [Job([(k.lru_w[:, g, j, :], xc[:, j, :])], P, S, copy_to(k, gates[:, g, j, :], bias=k.lru_b[:, g, j:j + 1]),
                    "dve") for g in range(2) for j in range(2)]
        gemm_stage(k, "lru_gates", jobs)
        with ExitStack() as inner:
            def sem(s):
                return nc.alloc_semaphore(f"lru_{s}")

            def isb(s, shape):
                return inner.enter_context(nc.sbuf_tensor(f"lru2_{s}", shape, F32))

            astep, step, opened, decayed, ready = sem("astep"), sem("step2"), sem("opened"), sem("decayed"), sem("ready")
            la, th, root = isb("la", [P, 2, S]), isb("th", [P, 2, S]), isb("root", [P, 2, S])
            lam = isb("lam", [P, 2])
            den = isb("den", [P, 2, S])
            block = inner.enter_context(nc.Block())

            @block.scalar
            def _(act):
                chain = Chain(act, astep)
                chain(nc.scalar.activation(lam[:], k.lru_lam[:], ACT.Abs))
                chain(nc.scalar.activation(lam[:], lam[:], ACT.Exp, scale=-1.0))
                nc.scalar.activation(lam[:], lam[:], ACT.Ln, bias=k.ones[:, 0:1]).then_inc(opened, 1)
                nc.scalar.activation(gates[:], gates[:], ACT.Sigmoid).then_inc(opened, 1)
                nc.scalar.activation(dxg[:, 2:4, :], dxg[:, 2:4, :], ACT.Gelu_apprx_tanh).then_inc(opened, 1)
                act.wait_ge(ready, 1)
                nc.scalar.activation(th[:], la[:], ACT.Tanh, scale=-1.0).then_inc(decayed, 1)
                nc.scalar.activation(la[:], la[:], ACT.Exp).then_inc(decayed, 1)
                act.wait_ge(ready, 2)
                nc.scalar.activation(root[:], th[:], ACT.Sqrt).then_inc(decayed, 1)

            @block.vector
            def _(dve):
                chain = Chain(dve, step)
                dve.wait_ge(opened, 3)
                chain(nc.vector.scalar_tensor_tensor(lam[:], k.lru_lam[:], 0.0, lam[:], ALU.min, ALU.subtract))
                chain(nc.vector.tensor_scalar(lam[:], lam[:], 8.0, None, ALU.mult))
                for j in range(2):
                    last = nc.vector.tensor_scalar(la[:, j, :], gates[:, 0, j, :], lam[:, j:j + 1], None, ALU.mult)
                    if j == 0:
                        chain(last)
                last.then_inc(ready, 1)
                dve.wait_ge(decayed, 1)
                chain(nc.vector.tensor_scalar(den[:], th[:], 1.0, None, ALU.add))
                chain(nc.vector.reciprocal(den[:], den[:]))
                nc.vector.scalar_tensor_tensor(th[:], th[:], 2.0, den[:], ALU.mult, ALU.mult).then_inc(ready, 1)
                chain(nc.vector.tensor_tensor(xc[:], xc[:], gates[:, 1], ALU.mult))
                dve.wait_ge(decayed, 3)
                chain(nc.vector.tensor_tensor(xc[:], xc[:], root[:], ALU.mult))
                for j in range(2):
                    chain(nc.vector.tensor_tensor_scan(den[:, j, :], la[:, j, :], xc[:, j, :], 0.0, ALU.mult, ALU.add))
                chain(nc.vector.tensor_tensor(k.hT[:, 6:8, :], den[:], dxg[:, 2:4, :], ALU.mult))


def residual(k, t, n, gate=None):
    nc = k.nc
    cols = slice(n * COL, (n + 1) * COL)

    def evac(e, chain, psum):
        if gate is None:
            return nc.vector.tensor_tensor(k.x[:, t, cols], k.x[:, t, cols], psum, ALU.add)
        chain(nc.vector.tensor_tensor(k.gated[:], psum, gate[:, cols], ALU.mult))
        return nc.vector.tensor_tensor(k.x[:, t, cols], k.x[:, t, cols], k.gated[:], ALU.add)
    return evac


def out_stage(k, name, keys, gate=None):
    jobs = []
    for n, key in enumerate(keys):
        (w,) = chunk_view(k, key)
        for t in range(NT):
            mm = [(k.hT[:, j, t * P:(t + 1) * P], w[:, j, :]) for j in range(ND)]
            jobs.append(Job(mm, P, COL, residual(k, t, n, gate), "dve", key))
    gemm_stage(k, name, jobs, last_key=keys[-1])


def part1(k, a):
    nc = k.nc
    condition_stage(k, a)
    with nc.sbuf_tensor("xn1", [P, NT, D], F32) as xn:
        rms_stage(k, "norm1", row_norm_groups(k.x, xn))
        transpose_stage(k, "turn1", [(columns_of(xn, j * P, P), k.hT[:, j, :], k.scale1[:, j:j + 1], k.shift1[:, j:j + 1])
                                     for j in range(ND)])
    with ExitStack() as ctx:
        tok = ctx.enter_context(nc.sbuf_tensor("tok1", [P, NT, 2048], F32))
        fm = ctx.enter_context(nc.sbuf_tensor("fm1", [P, 2, S], F32))
        glow = ctx.enter_context(nc.sbuf_tensor("glow1", [P, S], F32))
        dxg = ctx.enter_context(nc.sbuf_tensor("dxg1", [P, 4, S], F32))
        project1_stage(k, tok, fm, glow, dxg)
        lru_stages(k, dxg)
        with nc.sbuf_tensor("qk1", [P, 8, S], F32) as qk:
            groups = []
            for t in range(NT):
                def heads(c0, w):
                    return tok[:, t, c0:c0 + 256].rearrange("p (n w) -> p n w", w=w)
                groups += [(heads(0, A_DK), heads(0, A_DK), A_DK, k.a_q_gain[:]),
                           (heads(256, A_DK), heads(256, A_DK), A_DK, k.a_k_gain[:]),
                           (heads(768, B_DK), heads(768, B_DK), B_DK, k.b_q_gain[:]),
                           (heads(1024, B_DK), heads(1024, B_DK), B_DK, k.b_k_gain[:])]
            rms_stage(k, "qk_norm", groups)
            lambda_stage(k)
            transpose_stage(k, "turn_qk", [(columns_of(tok, c0, P), qk[:, j, :], None, None)
                                           for j, c0 in enumerate((0, 128, 256, 384, 768, 896, 1024, 1152))])

            def diff_step(h, i):
                r = [slice(64 * (h % 2) + 32 * m, 64 * (h % 2) + 32 * m + 32) for m in range(2)]

                def out(chain, psum, inv, m):
                    return nc.vector.tensor_copy(tok[:, i, OUT_A + h * 64:OUT_A + (h + 1) * 64], psum)
                return Step(i=i, q=[qk[r[m], h // 2, i * P:(i + 1) * P] for m in range(2)],
                                       k=[qk[r[m], 2 + h // 2, :] for m in range(2)],
                                       v=lambda m, j: tok[:, j, 512 + h * 64:512 + (h + 1) * 64], out=out)

            def moba_step(g, i):
                r = [slice(64 * m, 64 * m + 64) for m in range(2)]

                def out(chain, psum, inv, m):
                    h = 2 * g + m
                    return nc.vector.tensor_scalar(tok[:, i, OUT_B + h * 64:OUT_B + (h + 1) * 64], psum, inv, None, ALU.mult)
                return Step(i=i, q=[qk[r[m], 4 + g, i * P:(i + 1) * P] for m in range(2)],
                                       k=[qk[r[m], 6 + g, :] for m in range(2)],
                                       v=lambda m, j: tok[:, j, 1280 + (2 * g + m) * 64:1280 + (2 * g + m + 1) * 64], out=out)

            attention_stage(k, "diff", [diff_step(h, i) for h in range(A_HEADS) for i in range(NT)], A_DK ** -0.5, True, k.lam[:])
            attention_stage(k, "moba", [moba_step(g, i) for g in range(2) for i in range(NT)], B_DK ** -0.5, False)
        gla_stages(k, tok, fm, glow, a)
        gla_finish = []
        for t in range(NT):
            o = tok[:, t, OUT_A:OUT_A + 256].rearrange("p (n w) -> p n w", w=A_DV)
            gla_finish.append((o, o, A_DV, k.a_out_gain[:]))
        for t in range(NT):
            o = tok[:, t, OUT_C:OUT_C + 256].rearrange("p (n w) -> p n w", w=C_DV)
            gla_finish.append((o, o, C_DV, k.c_out_gain[:]))
        rms_stage(k, "head_norm", gla_finish)
        gla_gate_stage(k, tok)
        transpose_stage(k, "turn_mix", [(columns_of(tok, c0 + j * P, P), k.hT[:, 2 * g + j, :],
                                         1.0 - LAM_INIT if g == 0 else None, None)
                                        for g, c0 in enumerate((OUT_A, OUT_B, OUT_C)) for j in range(2)])
    out_stage(k, "out1", [("out1", n) for n in range(2)], k.mod[:, 0, :])




def second_norm_stages(k, h2_dram):
    nc = k.nc
    with nc.sbuf_tensor("h2", [P, NT, D], F32) as h2:
        rms_stage(k, "norm2", row_norm_groups(k.x, h2))
        with ExitStack() as ctx:
            step = nc.alloc_semaphore("h2_step")
            tile_ready = nc.alloc_semaphore("h2_tile_ready")
            stored = nc.alloc_semaphore("h2_stored")
            block = ctx.enter_context(nc.Block())

            @block.vector
            def _(dve):
                chain = Chain(dve, step)
                for t in range(NT):
                    chain(nc.vector.tensor_tensor(h2[:, t, :], h2[:, t, :], k.mod[:, 2, :], ALU.mult))
                    nc.vector.tensor_tensor(h2[:, t, :], h2[:, t, :], k.mod[:, 1, :], ALU.add).then_inc(tile_ready, 1)

            @block.sync
            def _(sp):
                for t in range(NT):
                    sp.wait_ge(tile_ready, t + 1)
                    sp.dma_start(h2_dram[t * P:(t + 1) * P, :], h2[:, t, :]).then_inc(stored, 16)
                sp.wait_ge(stored, 16 * NT)
        transpose_stage(k, "turn2", [(columns_of(h2, j * P, P), k.hT[:, j, :], None, None) for j in range(ND)])


def route_stages(k, a):
    nc = k.nc
    with ExitStack() as ctx:
        def sb(s, shape, dt=F32):
            return ctx.enter_context(nc.sbuf_tensor(f"route_{s}", shape, dt))

        def sem(s):
            return nc.alloc_semaphore(f"route_{s}")

        def ps(s, n=COL):
            return ctx.enter_context(nc.psum_tensor(f"route_{s}", [P, n], F32))

        logits = sb("logits", [P, NT, NE])
        best, best_id = sb("best", [P, NT, 8]), sb("best_id", [P, NT, 8], U32)
        ids = sb("ids", [P, NT, TOPK])
        e, total = sb("e", [P, NT, TOPK]), sb("total", [P, NT])
        hot = sb("hot", [P, NT, TOPK, NE])
        mask = sb("mask", [P, NT, NE])
        count, blocks, ends, start = sb("count", [P, NE]), sb("blocks", [P, NE]), sb("ends", [P, NE]), sb("start", [P, NE])
        place = sb("place", [P, NT, NE])
        prod = sb("prod", [P, NT, TOPK, NE])
        dest, dest_i = sb("dest", [P, NT, TOPK]), sb("dest_i", [P, NT * TOPK], I32)
        number, spare, number_i = sb("number", [P, MAXB]), sb("spare", [P, MAXB]), sb("number_i", [P, MAXB], I32)
        row_i, blk_i = sb("row_i", [P, NT * TOPK], I32), sb("blk_i", [P, NT * TOPK], I32)
        row_f, blk_f = sb("row_f", [P, NT * TOPK]), sb("blk_f", [P, NT * TOPK])
        row_hot, blk_hot = sb("row_hot", [P, NT * TOPK, P]), sb("blk_hot", [P, NT * TOPK, MAXB])
        before = sb("before", [1, MAXB, NE])
        owner = sb("owner", [1, MAXB])
        pairs = sb("pairs", [1, 1], I32)
        step, logits_ready, masked, ranked, scaled, raised, rows_ready, lists_ready = (
            sem(s) for s in ("step", "logits", "masked", "ranked", "scaled", "raised", "rows", "lists"))
        l_bank, r_bank, c_bank, t_bank = ps("l_bank"), ps("r_bank"), ps("c_bank"), ps("t_bank")
        block = ctx.enter_context(nc.Block())

        @block.tensor
        def _(pe):
            for t in range(NT):
                out = l_bank[:, t * NE:(t + 1) * NE]
                for j in range(ND):
                    nc.tensor.matmul(out, k.hT[:, j, t * P:(t + 1) * P], k.router_w[:, j, :], start=(j == 0), stop=False)
                mm = nc.tensor.matmul(out, k.ones[0:1, :], k.router_b[0:1, :], start=False, stop=True)
            mm.then_inc(logits_ready, 1)
            pe.wait_ge(masked, 1)
            for t in range(NT):
                for s in range(t + 1):
                    nc.tensor.matmul(r_bank[:, t * NE:(t + 1) * NE], k.upper_strict[:] if s == t else k.ones[:], mask[:, s, :],
                                     start=(s == 0), stop=(s == t))
            for s in range(NT):
                mm = nc.tensor.matmul(c_bank[:, 0:NE], k.ones[:], mask[:, s, :], start=(s == 0), stop=(s == NT - 1))
            mm.then_inc(ranked, 1)
            pe.wait_ge(rows_ready, 1)
            for n in range(NT * TOPK):
                mm = nc.tensor.matmul(t_bank[:, 0:MAXB], row_hot[:, n, :], blk_hot[:, n, :], start=(n == 0), stop=(n == NT * TOPK - 1))
            mm.then_inc(lists_ready, 1)

        @block.scalar
        def _(act):
            act.wait_ge(scaled, 1)
            nc.scalar.activation(e[:], e[:], ACT.Exp).then_inc(raised, 1)

        @block.vector
        def _(dve):
            chain = Chain(dve, step)
            dve.wait_ge(logits_ready, 1)
            chain(nc.vector.tensor_copy(logits[:], l_bank[:, 0:NT * NE].rearrange("p (t e) -> p t e", e=NE)))
            for t in range(NT):
                chain(nc.vector.max(best[:, t, :], logits[:, t, :]))
                chain(nc.vector.max_index(best_id[:, t, :], best[:, t, :], logits[:, t, :]))
            nc.vector.tensor_tensor(e[:], best[:, :, 0:TOPK], best[:, :, 0:1].to_broadcast([P, NT, TOPK]), ALU.subtract).then_inc(scaled, 1)
            chain(nc.vector.tensor_copy(ids[:], best_id[:, :, 0:TOPK]))
            for t in range(NT):
                chain(nc.vector.tensor_tensor(hot[:, t], k.iota[:, 0:NE].unsqueeze(1).to_broadcast([P, TOPK, NE]),
                                              ids[:, t, :].unsqueeze(2).to_broadcast([P, TOPK, NE]), ALU.is_equal))
            nc.vector.tensor_reduce(mask[:], hot[:].rearrange("p t k e -> p t e k"), X, ALU.add).then_inc(masked, 1)
            dve.wait_ge(raised, 1)
            chain(nc.vector.tensor_reduce(total[:], e[:], X, ALU.add))
            chain(nc.vector.reciprocal(total[:], total[:]))
            chain(nc.vector.tensor_tensor(k.gates[:], e[:], total[:].unsqueeze(2).to_broadcast([P, NT, TOPK]), ALU.mult))
            dve.wait_ge(ranked, 1)
            chain(nc.vector.tensor_copy(count[:], c_bank[:, 0:NE]))
            chain(nc.vector.tensor_scalar(blocks[:], count[:], 0.0, None, ALU.is_gt))
            for n in range(1, NT):
                chain(nc.vector.scalar_tensor_tensor(blocks[:], count[:], float(n * P), blocks[:], ALU.is_gt, ALU.add))
            chain(nc.vector.tensor_tensor_scan(ends[:], k.ones[:, 0:NE], blocks[:], 0.0, ALU.mult, ALU.add))
            chain(nc.vector.tensor_tensor(start[:], ends[:], blocks[:], ALU.subtract))
            chain(nc.vector.tensor_scalar(start[:], start[:], float(P), None, ALU.mult))
            chain(nc.vector.tensor_tensor(place[:], r_bank[:, 0:NT * NE].rearrange("p (t e) -> p t e", e=NE),
                                          start[:].unsqueeze(1).to_broadcast([P, NT, NE]), ALU.add))
            for t in range(NT):
                chain(nc.vector.tensor_tensor(prod[:, t], hot[:, t], place[:, t, :].unsqueeze(1).to_broadcast([P, TOPK, NE]), ALU.mult))
            chain(nc.vector.tensor_reduce(dest[:], prod[:], X, ALU.add))
            chain(nc.vector.tensor_copy(dest_i[:], dest[:].rearrange("p t k -> p (t k)")))
            chain(nc.vector.tensor_single_scalar(row_i[:], dest_i[:], P - 1, ALU.bitwise_and))
            chain(nc.vector.tensor_single_scalar(blk_i[:], dest_i[:], 7, ALU.arith_shift_right))
            chain(nc.vector.tensor_copy(row_f[:], row_i[:]))
            chain(nc.vector.tensor_copy(blk_f[:], blk_i[:]))
            for n in range(NT * TOPK):
                chain(nc.vector.tensor_scalar(row_hot[:, n, :], k.iota[:], row_f[:, n:n + 1], None, ALU.is_equal))
                last = nc.vector.tensor_scalar(blk_hot[:, n, :], k.iota[:, 0:MAXB], blk_f[:, n:n + 1], k.place_no[:, n:n + 1],
                                               ALU.is_equal, ALU.mult)
                if n < NT * TOPK - 1:
                    chain(last)
            last.then_inc(rows_ready, 1)
            chain(nc.vector.tensor_tensor(before[:], ends[0:1, :].unsqueeze(1).to_broadcast([1, MAXB, NE]),
                                          k.iota[0:1, 0:MAXB].unsqueeze(2).to_broadcast([1, MAXB, NE]), ALU.is_le))
            chain(nc.vector.tensor_reduce(owner[:], before[:], X, ALU.add))
            chain(nc.vector.tensor_scalar(owner[:], owner[:], float(NE - 1), None, ALU.min))
            chain(nc.vector.tensor_copy(k.owner[:], owner[:]))
            chain(nc.vector.tensor_copy(pairs[:], ends[0:1, NE - 1:NE]))
            chain(nc.vector.tensor_single_scalar(pairs[:], pairs[:], 1, ALU.add))
            chain(nc.vector.tensor_single_scalar(k.pairs[:], pairs[:], 1, ALU.arith_shift_right))
            dve.wait_ge(lists_ready, 1)
            chain(nc.vector.tensor_copy(number[:], t_bank[:, 0:MAXB]))
            chain(nc.vector.tensor_scalar(spare[:], number[:], 0.0, k.spare_no[:], ALU.is_equal, ALU.mult))
            chain(nc.vector.scalar_tensor_tensor(spare[:], spare[:], -1.0, number[:], ALU.add, ALU.add))
            chain(nc.vector.tensor_copy(k.row_place[:], spare[:]))
            chain(nc.vector.memset(k.row_token[:], 0))
            chain(nc.vector.tensor_scalar(number[:], number[:], -1.0, 0.0, ALU.add, ALU.max))
            chain(nc.vector.tensor_copy(number_i[:], number[:]))
            chain(nc.vector.tensor_single_scalar(k.row_token[:, 0:MAXB], number_i[:], 2, ALU.arith_shift_right))


def expert_stage(k, a, h2_dram, y_dram):
    nc = k.nc
    up_cols = [0, FF, COL, FF + COL]
    with ExitStack() as ctx:
        def sem(s):
            return nc.alloc_semaphore(f"moe_{s}")

        def sb(s, shape, dt=F32):
            return ctx.enter_context(nc.sbuf_tensor(f"moe_{s}", shape, dt))

        def ps(s):
            return ctx.enter_context(nc.psum_tensor(f"moe_{s}", [P, COL], F32))

        more = sb("w", [P, 3 * SLOT])
        chunk = [k.ring[:, c * SLOT:(c + 1) * SLOT] for c in range(3)] + [more[:, c * SLOT:(c + 1) * SLOT] for c in range(3)]
        chunk = [c.rearrange("p (k n) -> p k n", n=COL) for c in chunk]
        rows, rowsT = sb("rows", [P, 2, D]), sb("rowsT", [P, 2, ND, P])
        index, place = sb("index", [P, 2], U32), sb("place", [P, 2], U32)
        bias = sb("bias", [P, 2, 3 * FF])
        gate, lin, sig = sb("gate", [P, COL]), sb("lin", [P, COL]), sb("sig", [P, COL])
        hid, hidT = k.mod[:, 0, :], sb("hidT", [P, ND, P])
        y = [k.mod[:, 1, :], k.mod[:, 2, :]]
        loaded = [sem(f"loaded{c}") for c in range(6)]
        bias_spread, indexed, waited = sem("bias_spread"), sem("indexed"), sem("waited")
        bias_loaded = [sem(f"bias_loaded{u}") for u in range(2)]
        gathered, y_stored = k.gathered, k.y_stored
        rows_turned, rows_taken = sem("rows_turned"), sem("rows_taken")
        chunk_done, gate_ready, sig_ready, hid_ready, up_taken = sem("chunk_done"), sem("gate"), sem("sig"), sem("hid"), sem("up_taken")
        hid_turned, hid_taken = sem("hid_turned"), sem("hid_taken")
        y_ready, step = sem("y_ready"), sem("step")
        y_free = sem("y_free")
        up = [ps(f"up{c}") for c in range(4)]
        down = [ps(f"down{c}") for c in range(2)]
        turn = [ps(f"turn{c}") for c in range(2)]
        block = ctx.enter_context(nc.Block())
        w_up = a["exp_w_up"][0].rearrange("e (k p) n -> e p k n", p=P)
        w_down = a["exp_w_down"][0].rearrange("e (k p) n -> e p k n", p=P)
        CHUNKS = 6

        def turns(eng):
            return eng.value_load(k.pairs[0:1, 0:1], min_val=1, max_val=MAXB // 2)

        @block.sync
        def _(sp):
            with sp.Fori(0, turns(sp)) as i:
                for u in range(2):
                    e = sp.value_load(k.owner[0:1, bass.ds(i * 2 + u, 1)], min_val=0, max_val=NE - 1)
                    sp.wait_ge(y_ready, i * 2 + (u + 1))
                    sp.dma_start(bias[0:1, u, 0:2 * FF], a["exp_b_up"][0][bass.ds(e, 1), :]).then_inc(bias_loaded[u], 16)
                    sp.dma_start(bias[0:1, u, 2 * FF:], a["exp_b_down"][0][bass.ds(e, 1), :]).then_inc(bias_loaded[u], 16)
                    for c in range(CHUNKS):
                        sp.wait_ge(chunk_done, i * (2 * CHUNKS) + (u * CHUNKS + c + 1))
                        src = (w_up[bass.ds(e, 1), :, :, up_cols[c]:up_cols[c] + COL] if c < 4 else
                               w_down[bass.ds(e, 1), :, :, (c - 4) * COL:(c - 3) * COL])
                        sp.dma_start(chunk[c], src.rearrange("e p k n -> (e p) k n")).then_inc(loaded[c], 16)

        @block.gpsimd
        def _(pool):
            def gather(b, u, copies):
                nc.gpsimd.tensor_copy(index[:, u:u + 1], k.row_token[:, bass.ds(b, 1)]).then_inc(indexed, 1)
                pool.wait_ge(indexed, copies)
                pool.sem_inc(waited, 1)
                pool.indirect_dma_start(rows[:, u, :], None, h2_dram[:, :],
                                        bass.IndirectOffsetOnAxis(ap=index[:, u:u + 1], axis=0)).then_inc(gathered[u], 16)

            for u in range(2):
                gather(u, u, u + 1)
            pool.sem_inc(y_free, 2)
            with pool.Fori(0, turns(pool)) as i:
                for u in range(2):
                    pool.wait_ge(bias_loaded[u], i * 32 + 32)
                    pool.sem_inc(waited, 1)
                    nc.gpsimd.partition_broadcast(bias[:, u, :], bias[0:1, u, :]).then_inc(bias_spread, 1)
                for u in range(2):
                    nc.gpsimd.tensor_copy(place[:, u:u + 1], k.row_place[:, bass.ds(i * 2 + u, 1)]).then_inc(indexed, 1)
                    pool.wait_ge(indexed, i * 4 + (2 * u + 3))
                    pool.wait_ge(y_ready, i * 2 + (u + 3))
                    pool.sem_inc(waited, 1)
                    pool.indirect_dma_start(y_dram[:, :], bass.IndirectOffsetOnAxis(ap=place[:, u:u + 1], axis=0),
                                            y[u], None).then_inc(y_stored[u], 16)
                    pool.wait_ge(rows_turned, i * 4 + (2 * u + 6))
                    gather(i * 2 + (u + 2), u, i * 4 + (2 * u + 4))
                    pool.wait_ge(y_stored[u], i * 16 + 16)
                    pool.sem_inc(y_free, 1)
            for u in range(2):
                pool.wait_ge(gathered[u], turns(pool) * 16 + 16)
                pool.sem_inc(waited, 1)

        @block.tensor
        def _(pe):
            def turn_rows(i, u):
                pe.wait_ge(gathered[u], i * 16 + 16)
                for half in range(2):
                    pe.wait_ge(hid_taken, i * 4 + (2 * u + half + 1))
                    for j in range(4):
                        tr = nc.tensor.transpose(turn[half][:, j * P:(j + 1) * P], rows[:, u, (4 * half + j) * P:(4 * half + j + 1) * P], k.ident[:])
                    tr.then_inc(rows_turned, 1)

            def up_chunk(i, u, c):
                pe.wait_ge(loaded[c], i * 32 + 16 * (u + 1))
                pe.wait_ge(up_taken, i * 8 + (4 * u + c + 1))
                for j in range(ND):
                    mm = nc.tensor.matmul(up[c][:], rowsT[:, u, j, :], chunk[c][:, j, :], start=(j == 0), stop=(j == ND - 1))
                mm.then_inc(chunk_done, 1)

            def turn_hidden(i, u, half):
                pe.wait_ge(hid_ready, i * 4 + (2 * u + half + 2))
                for j in range(4):
                    tr = nc.tensor.transpose(turn[half][:, j * P:(j + 1) * P], hid[:, (4 * half + j) * P:(4 * half + j + 1) * P], k.ident[:])
                tr.then_inc(hid_turned, 1)

            def down_half(i, u, half):
                pe.wait_ge(hid_taken, i * 4 + (2 * u + half + 3))
                if half == 0:
                    pe.wait_ge(y_ready, i * 2 + (u + 2))
                for c in range(2):
                    if half == 0:
                        pe.wait_ge(loaded[4 + c], i * 32 + 16 * (u + 1))
                    for j in range(4 * half, 4 * half + 4):
                        mm = nc.tensor.matmul(down[c][:], hidT[:, j, :], chunk[4 + c][:, j, :], start=(j == 0), stop=(j == ND - 1))
                    if half == 1:
                        mm.then_inc(chunk_done, 1)

            pe.nop().then_inc(chunk_done, CHUNKS)
            pe.nop().then_inc(rows_turned, 4)
            pe.nop().then_inc(hid_turned, 2)
            with pe.Fori(0, turns(pe)) as i:
                turn_rows(i, 0)
                for u in range(2):
                    pe.wait_ge(rows_taken, i * 4 + (2 * u + 2))
                    up_chunk(i, u, 0)
                    up_chunk(i, u, 1)
                    up_chunk(i, u, 2)
                    turn_hidden(i, u, 0)
                    up_chunk(i, u, 3)
                    down_half(i, u, 0)
                    turn_hidden(i, u, 1)
                    if u == 0:
                        turn_rows(i, 1)
                    down_half(i, u, 1)

        @block.scalar
        def _(act):
            def take_rows(i, u):
                for half in range(2):
                    act.wait_ge(rows_turned, i * 4 + (2 * u + half + 5))
                    nc.scalar.activation(rowsT[:, u, 4 * half:4 * half + 4, :], turn[half][:], ACT.Copy).then_inc(rows_taken, 1)

            act.nop().then_inc(hid_taken, 2)
            with act.Fori(0, turns(act)) as i:
                take_rows(i, 0)
                for u in range(2):
                    for half in range(2):
                        act.wait_ge(gate_ready, i * 4 + (2 * u + half + 1))
                        nc.scalar.activation(sig[:], gate[:], ACT.Sigmoid, scale=ALPHA).then_inc(sig_ready, 1)
                        act.wait_ge(hid_turned, i * 4 + (2 * u + half + 3))
                        act.wait_ge(chunk_done, i * (2 * CHUNKS) + (u * CHUNKS + CHUNKS))
                        nc.scalar.activation(hidT[:, 4 * half:4 * half + 4, :], turn[half][:], ACT.Copy).then_inc(hid_taken, 1)
                    if u == 0:
                        take_rows(i, 1)

        @block.vector
        def _(dve):
            dve.nop().then_inc(up_taken, 4)
            dve.nop().then_inc(y_ready, 2)
            dve.nop().then_inc(hid_ready, 1)
            with dve.Fori(0, turns(dve)) as i:
                for u in range(2):
                    dve.wait_ge(bias_spread, i * 2 + (u + 1))
                    for half in range(2):
                        done = 4 * u + 2 * half
                        b = bias[:, u, half * COL:(half + 1) * COL]
                        dve.wait_ge(chunk_done, i * (2 * CHUNKS) + (u * CHUNKS + CHUNKS + 2 * half + 1))
                        dve.wait_ge(hid_ready, i * 4 + (2 * u + half + 1))
                        nc.vector.tensor_tensor(gate[:], up[2 * half][:], b, ALU.add).then_inc(up_taken, 1)
                        dve.wait_ge(up_taken, i * 8 + (done + 5))
                        nc.vector.tensor_scalar(gate[:], gate[:], LIMIT, None, ALU.min).then_inc(gate_ready, 1)
                        b = bias[:, u, FF + half * COL:FF + (half + 1) * COL]
                        dve.wait_ge(chunk_done, i * (2 * CHUNKS) + (u * CHUNKS + CHUNKS + 2 * half + 2))
                        nc.vector.tensor_tensor(lin[:], up[2 * half + 1][:], b, ALU.add).then_inc(up_taken, 1)
                        dve.wait_ge(up_taken, i * 8 + (done + 6))
                        nc.vector.tensor_scalar(lin[:], lin[:], LIMIT, -LIMIT, ALU.min, ALU.max).then_inc(step, 1)
                        dve.wait_ge(sig_ready, i * 4 + (2 * u + half + 1))
                        nc.vector.tensor_tensor(gate[:], gate[:], sig[:], ALU.mult).then_inc(step, 1)
                        dve.wait_ge(step, i * 8 + (done + 2))
                        dve.wait_ge(hid_turned, i * 4 + (2 * u + half + 1))
                        nc.vector.scalar_tensor_tensor(hid[:, half * COL:(half + 1) * COL], lin[:], 1.0, gate[:], ALU.add,
                                                       ALU.mult).then_inc(hid_ready, 1)
                    for c in range(2):
                        dve.wait_ge(chunk_done, i * (2 * CHUNKS) + (u * CHUNKS + CHUNKS + 5 + c))
                        if c == 0:
                            dve.wait_ge(y_free, i * 2 + (u + 1))
                        last = nc.vector.tensor_tensor(y[u][:, c * COL:(c + 1) * COL], down[c][:],
                                                       bias[:, u, 2 * FF + c * COL:2 * FF + (c + 1) * COL], ALU.add)
                    last.then_inc(y_ready, 1)


def combine_stage(k, y_dram):
    nc = k.nc
    with ExitStack() as ctx:
        rows = ctx.enter_context(nc.sbuf_tensor("combine_rows", [P, 2, TOPK, D], F32))
        acc = ctx.enter_context(nc.sbuf_tensor("combine_sum", [P, D], F32))
        loaded = [nc.alloc_semaphore(f"combine_loaded{b}") for b in range(2)]
        summed = nc.alloc_semaphore("combine_summed")
        step = nc.alloc_semaphore("combine_step")
        block = ctx.enter_context(nc.Block())

        @block.sync
        def _(sp):
            k.load_end = len(k.plan) - 1
            load_chunks(k, sp, ("out1", 1))
            for t in range(NT):
                if t >= 2:
                    sp.wait_ge(summed, t - 1)
                sp.dma_start(rows[:, t % 2], y_dram[t * P * TOPK:(t + 1) * P * TOPK, :].rearrange("(p k) d -> p k d", k=TOPK)).then_inc(loaded[t % 2], 16)

        @block.vector
        def _(dve):
            chain = Chain(dve, step)
            for t in range(NT):
                dve.wait_ge(loaded[t % 2], 16 * (t // 2 + 1))
                chain(nc.vector.tensor_scalar(acc[:], rows[:, t % 2, 0, :], k.gates[:, t, 0:1], None, ALU.mult))
                for j in range(1, TOPK):
                    last = nc.vector.scalar_tensor_tensor(acc[:], rows[:, t % 2, j, :], k.gates[:, t, j:j + 1], acc[:], ALU.mult, ALU.add)
                    if j < TOPK - 1:
                        chain(last)
                last.then_inc(summed, 1)
                dve.wait_ge(summed, t + 1)
                chain(nc.vector.tensor_tensor(acc[:], acc[:], k.mod[:, 3, :], ALU.mult))
                chain(nc.vector.tensor_tensor(k.x[:, t, :], k.x[:, t, :], acc[:], ALU.add))




def rope_stage(k, name, spans, cos, sin, groups_w):
    nc = k.nc
    w = groups_w
    with ExitStack() as ctx:
        step = nc.alloc_semaphore(f"{name}_step")
        most = max(s[0].shape[1] for s in spans)
        rot = ctx.enter_context(nc.sbuf_tensor(f"{name}_rot", [P, most, w], F32))
        block = ctx.enter_context(nc.Block())

        @block.vector
        def _(dve):
            chain = Chain(dve, step)
            for n, (view, dst) in enumerate(spans):
                t = n % NT
                heads = view.shape[1]
                c = cos[:, t, :].unsqueeze(1).to_broadcast([P, heads, w])
                s = sin[:, t, :].unsqueeze(1).to_broadcast([P, heads, w])
                r = rot[:, 0:heads, :]
                half = w // 2
                nc.vector.tensor_tensor(r[:, :, 0:half], view[:, :, half:], s[:, :, 0:half], ALU.mult)
                chain(nc.vector.tensor_tensor(r[:, :, half:], view[:, :, 0:half], s[:, :, half:], ALU.mult))
                chain(nc.vector.tensor_tensor(view, view, c, ALU.mult))
                chain(nc.vector.tensor_tensor(dst, by_group(view, dst), by_group(r, dst), ALU.add))


def by_group(view, dst):
    return view if len(dst.shape) == 3 else view.rearrange("p (g r) w -> p r g w", g=G2)


@contextmanager
def cleared_semaphores(nc):
    held = nc.snapshot_sems()
    yield
    nc.clear_and_free_semaphores(nc.allocated_since(held))
    nc.all_engine_barrier()


def in_place(views):
    return [(v, v) for v in views]


KC, VC, KS, VS, KW, VW, GA, CQ, CKV, KR = 512, 640, 768, 896, 1024, 1152, 1280, 1304, 1560, 1688
IN2_W = 1720


def project2_stage(k, l, tok):
    jobs = []
    n = 0
    for c, (c0, c1) in enumerate(IN2):
        (w,) = chunk_view(k, ("in2", l, c))
        for t in range(NT):
            mm = [(k.hT[:, j, t * P:(t + 1) * P], w[:, j, :]) for j in range(ND)]
            jobs.append(Job(mm, P, c1 - c0, copy_to(k, tok[:, t, c0:c1]), engine_of(n), ("in2", l, c)))
            n += 1
    gemm_stage(k, f"in2_{l}", jobs, last_key=("in2", l, 3))


def compress_stages(k, l, tok, kcmp, vbd):
    nc = k.nc
    with ExitStack() as ctx:
        def sb(s, shape):
            return ctx.enter_context(nc.sbuf_tensor(f"cmp{l}_{s}", shape, F32))

        pairs = [sb(f"pair_{kv}", [P, G2, S // 2]) for kv in "kv"]
        hid = [sb(f"hid_{kv}", [P, 2, G2 * CPAD]) for kv in "kv"]
        hid4 = sb("hid4", [P, 2, G2, 4, CPAD])
        posb = sb("posb", [P, 2, 2])
        w2k = sb("w2k", [P, 2, 2, DK2])
        w2v = sb("w2v", [P, 2, DK2])
        pos = sb("pos", [P, 2, CB // 2])
        with ExitStack() as inner:
            turned = nc.alloc_semaphore(f"cmp{l}_turned")
            taken = nc.alloc_semaphore(f"cmp{l}_taken")
            w2_loaded = nc.alloc_semaphore(f"cmp{l}_w2_loaded")
            zeroed = nc.alloc_semaphore(f"cmp{l}_zeroed")
            bank = [inner.enter_context(nc.psum_tensor(f"cmp{l}_t{i}", [P, COL], F32)) for i in range(2)]
            block = inner.enter_context(nc.Block())

            @block.sync
            def _(sp):
                for copy in range(2):
                    sp.dma_start(w2k[:, :, copy, :], k.a["cmp_w2_k_2"][l].rearrange("(k p) n -> p k n", p=P)).then_inc(w2_loaded, 16)
                sp.dma_start(w2v[:], k.a["cmp_w2_v_2"][l].rearrange("(k p) n -> p k n", p=P)).then_inc(w2_loaded, 16)
                for i, kv in enumerate("kv"):
                    sp.dma_start(pos[:, i, :], k.a[f"cmp_pos_{kv}_2"][l].rearrange("(u a) d -> (a d) u", a=2),
                                 allow_slow_non_contiguous=True).then_inc(w2_loaded, 16)
                sp.wait_ge(w2_loaded, 16 * 5)

            @block.gpsimd
            def _(pool):
                for i in range(2):
                    nc.gpsimd.memset(hid[i][:], 0.0).then_inc(zeroed, 1)
                nc.gpsimd.memset(vbd[:], 0.0).then_inc(zeroed, 1)

            @block.tensor
            def _(pe):
                for i, c0 in enumerate((KC, VC)):
                    for t in range(NT):
                        tr = nc.tensor.transpose(bank[i][:, t * P:(t + 1) * P], tok[:, t, c0:c0 + P], k.ident[:])
                    tr.then_inc(turned, 1)

            @block.vector
            def _(dve):
                for i in range(2):
                    dve.wait_ge(turned, i + 1)
                    for g in range(G2):
                        for parity in range(2):
                            nc.vector.tensor_copy(pairs[i][64 * parity:64 * parity + 64, g, :],
                                                  bank[i][64 * g:64 * g + 64, :].rearrange("p (n a) -> p n a", a=2)[:, :, parity]).then_inc(taken, 1)
        jobs = []
        for i, kv in enumerate("kv"):
            (w1,) = chunk_view(k, ("cmp", l, kv))
            for m in range(2):
                mm = [(w1[:, u, m * P:(m + 1) * P], pos[:, i, u:u + 1]) for u in range(CB // 2)]
                jobs.append(Job(mm, P, 1, copy_to(k, posb[:, i, m:m + 1]), "act", ("cmp", l, kv)))

                def silu(e, chain, psum, i=i, m=m):
                    return nc.scalar.activation(hid[i][:, m, :].rearrange("p (g n) -> p g n", n=CPAD)[:, :, 0:NCMP],
                                                psum.rearrange("p (g n) -> p g n", n=NCMP), ACT.Silu, bias=posb[:, i, m:m + 1])

                def after_bias(e, chain, psum, f=silu):
                    return f(e, chain, psum)
                mm = [(w1[:, u, m * P:(m + 1) * P], pairs[i][:, :, u:u + 8 * (NCMP - 1) + 1:8]) for u in range(CB // 2)]
                jobs.append(Job(mm, P, G2 * NCMP, after_bias, "act", ("cmp", l, kv)))
        gemm_stage(k, f"cmp1_{l}", jobs, last_key=("cmp", l, "v"))

        with ExitStack() as inner:
            step = nc.alloc_semaphore(f"cmp{l}_spread")
            block = inner.enter_context(nc.Block())

            @block.vector
            def _(dve):
                for m in range(2):
                    for g in range(G2):
                        nc.vector.tensor_copy(hid4[:, m, g], hid[1][:, m, g * CPAD:(g + 1) * CPAD].unsqueeze(1).to_broadcast([P, 4, CPAD])).then_inc(step, 1)

        jobs = []

        def keys(e, chain, psum):
            chain(nc.vector.tensor_copy(kcmp[0:64, :], psum[0:64, 0:CPAD]))
            return nc.vector.tensor_copy(kcmp[64:128, :], psum[64:128, CPAD:2 * CPAD])
        jobs.append(Job([(w2k[:, m].rearrange("p a n -> p (a n)"), hid[0][:, m, :]) for m in range(2)], P, G2 * CPAD, keys, "dve"))
        for g in range(G2):
            def values(e, chain, psum, g=g):
                for r in range(4):
                    last = nc.vector.tensor_copy(vbd[32 * r:32 * r + 32, g, 64 * r:64 * r + 64], psum[32 * r:32 * r + 32, :])
                    if r < 3:
                        chain(last)
                return last
            jobs.append(Job([(hid4[:, m, g].rearrange("p r n -> p (r n)"), w2v[:, m, :]) for m in range(2)], P, DK2, values, "dve"))
        gemm_stage(k, f"cmp2_{l}", jobs)


def compressed_attention_stage(k, l, qT, kcmp, vbd, gates, o):
    nc = k.nc
    scale = DK2 ** -0.5
    with ExitStack() as ctx:
        def sem(s):
            return nc.alloc_semaphore(f"ca{l}_{s}")

        def sb(s, shape):
            return ctx.enter_context(nc.sbuf_tensor(f"ca{l}_{s}", shape, F32))

        scored, shifted, raised, weighed, turned, taken, valued, done, step = (
            sem(s) for s in ("scored", "shifted", "raised", "weighed", "turned", "taken", "valued", "done", "step"))
        s = sb("s", [P, 2, H2, CPAD])
        top, inv = sb("top", [P, H2]), sb("inv", [P, 2, H2])
        pT = sb("pT", [P, 2, G2, P])
        sc = [ctx.enter_context(nc.psum_tensor(f"ca{l}_s{i}", [P, G2, COL], F32)) for i in range(2)]
        tr = [ctx.enter_context(nc.psum_tensor(f"ca{l}_t{i}", [P, COL], F32)) for i in range(2)]
        ov = [ctx.enter_context(nc.psum_tensor(f"ca{l}_o{i}", [P, COL], F32)) for i in range(2)]
        block = ctx.enter_context(nc.Block())

        @block.tensor
        def _(pe):
            def scores(t):
                if t >= 2:
                    pe.wait_ge(shifted, t - 1)
                for g in range(G2):
                    for r in range(R2):
                        mm = nc.tensor.matmul(sc[t % 2][:, g, r * CPAD:(r + 1) * CPAD], qT[64 * g:64 * g + 64, r, t * P:(t + 1) * P],
                                              kcmp[64 * g:64 * g + 64, :], start=True, stop=True)
                mm.then_inc(scored, 1)

            scores(0)
            for t in range(NT):
                if t + 1 < NT:
                    scores(t + 1)
                pe.wait_ge(weighed, t + 1)
                if t >= 2:
                    pe.wait_ge(done, t - 1)
                for g in range(G2):
                    x = nc.tensor.transpose(tr[t % 2][:, g * P:(g + 1) * P], s[:, t % 2, g * R2:(g + 1) * R2, :].rearrange("p r n -> p (r n)"), k.ident[:])
                x.then_inc(turned, 1)
                pe.wait_ge(taken, t + 1)
                for g in range(G2):
                    mm = nc.tensor.matmul(ov[t % 2][:, g * 256:(g + 1) * 256], pT[:, t % 2, g, :], vbd[:, g, :], start=True, stop=True)
                mm.then_inc(valued, 1)

        @block.scalar
        def _(act):
            for t in range(NT):
                act.wait_ge(shifted, t + 1)
                nc.scalar.activation(s[:, t % 2], s[:, t % 2], ACT.Exp).then_inc(raised, 1)
                act.wait_ge(turned, t + 1)
                if t >= 2:
                    act.wait_ge(valued, t - 1)
                nc.scalar.activation(pT[:, t % 2].rearrange("p g n -> p (g n)"), tr[t % 2][:, 0:G2 * P], ACT.Copy).then_inc(taken, 1)

        @block.vector
        def _(dve):
            chain = Chain(dve, step)
            for t in range(NT):
                b = t % 2
                dve.wait_ge(scored, t + 1)
                if t >= 2:
                    dve.wait_ge(turned, t - 1)
                for g in range(G2):
                    chain(nc.vector.scalar_tensor_tensor(
                        s[:, b, g * R2:(g + 1) * R2, :], sc[b][:, g, 0:R2 * CPAD].rearrange("p (r n) -> p r n", n=CPAD), scale,
                        k.cmp_bias[:, t, :].unsqueeze(1).to_broadcast([P, R2, CPAD]), ALU.mult, ALU.add))
                chain(nc.vector.tensor_reduce(top[:], s[:, b], X, ALU.max))
                nc.vector.tensor_tensor(s[:, b], s[:, b], top[:].unsqueeze(2).to_broadcast([P, H2, CPAD]), ALU.subtract).then_inc(shifted, 1)
                dve.wait_ge(raised, t + 1)
                nc.vector.tensor_tensor(s[:, b], s[:, b], k.cmp_mask[:, t, :].unsqueeze(1).to_broadcast([P, H2, CPAD]), ALU.mult).then_inc(weighed, 1)
                dve.wait_ge(weighed, t + 1)
                chain(nc.vector.tensor_reduce(inv[:, b, :], s[:, b], X, ALU.add))
                chain(nc.vector.tensor_scalar(inv[:, b, :], inv[:, b, :], 1e-30, None, ALU.max))
                chain(nc.vector.reciprocal(inv[:, b, :], inv[:, b, :]))
                chain(nc.vector.tensor_tensor(inv[:, b, :], inv[:, b, :], gates[:, t, :, 0], ALU.mult))
                dve.wait_ge(valued, t + 1)
                nc.vector.tensor_tensor(o[:, t, :].rearrange("p (h d) -> p h d", d=DK2), ov[b][:, :].rearrange("p (h d) -> p h d", d=DK2),
                                        inv[:, b, :].unsqueeze(2).to_broadcast([P, H2, DK2]), ALU.mult).then_inc(done, 1)


def nsa_stages(k, l, tok, o):
    nc = k.nc
    with ExitStack() as ctx:
        def sb(s, shape):
            return ctx.enter_context(nc.sbuf_tensor(f"nsa{l}_{s}", shape, F32))

        gates = sb("gates", [P, NT, H2, 3])
        qT = sb("qT", [P, R2, S])
        ksT = sb("ksT", [P, 2, S])
        kcmp, vbd = sb("kcmp", [P, CPAD]), sb("vbd", [P, G2, 256])
        with ExitStack() as inner:
            opened = nc.alloc_semaphore(f"nsa{l}_opened")
            block = inner.enter_context(nc.Block())

            @block.scalar
            def _(act):
                nc.scalar.activation(gates[:].rearrange("p t h n -> p t (h n)"), tok[:, :, GA:GA + 24], ACT.Sigmoid).then_inc(opened, 1)
        with nc.sbuf_tensor(f"nsa{l}_q", [P, NT, R2, G2, DK2], F32) as q:
            spans = [(tok[:, t, 0:512].rearrange("p (n w) -> p n w", w=DK2), q[:, t]) for t in range(NT)]
            for c0 in (KC, KS, KW):
                spans += in_place([tok[:, t, c0:c0 + P].rearrange("p (n w) -> p n w", w=DK2) for t in range(NT)])
            rope_stage(k, f"rope{l}", spans, k.cos_a, k.sin_a, DK2)
            blocks = [([q[:, t, r].rearrange("p g d -> p (g d)") for t in range(NT)], qT[:, r, :], None, None) for r in range(R2)]
            blocks += [(columns_of(tok, c0, P), ksT[:, j, :], None, None) for j, c0 in enumerate((KS, KW))]
            transpose_stage(k, f"turn_nsa{l}", blocks)
        compress_stages(k, l, tok, kcmp, vbd)
        compressed_attention_stage(k, l, qT, kcmp, vbd, gates, o)

        def step(branch, g, half, i):
            part = slice(64 * g, 64 * g + 64)
            v0 = (VS, VW)[branch]
            h0 = g * R2 + 2 * half

            def out(chain, psum, inv, m):
                h = g * R2 + 2 * half + m
                dst = o[:, i, h * DK2:(h + 1) * DK2]
                return nc.vector.scalar_tensor_tensor(dst, psum, inv, dst, ALU.mult, ALU.add)
            return Step(i=i, q=[qT[part, 2 * half + m, i * P:(i + 1) * P] for m in range(2)],
                                   k=[ksT[part, branch, :] for m in range(2)],
                                   v=lambda m, j: tok[:, j, v0 + g * DK2:v0 + (g + 1) * DK2], out=out,
                                   gate=gates[:, i, h0:h0 + 2, 1 + branch])
        attention_stage(k, f"nsa{l}", [step(br, g, half, i) for br in range(2) for g in range(G2) for half in range(2) for i in range(NT)],
                        DK2 ** -0.5, False, gated=True)


def mla_stages(k, l, tok):
    nc = k.nc
    OUT = H2 * DQ
    with ExitStack() as ctx:
        def sb(s, shape):
            return ctx.enter_context(nc.sbuf_tensor(f"mla{l}_{s}", shape, F32))

        qT = sb("qT", [DQ, H2, S])
        v = sb("v", [P, NT, H2 * DV2])
        kT = k.hT[0:DQ]
        rms_stage(k, f"mla_norm{l}", [(tok[:, t:t + 1, CQ:CQ + RQ], tok[:, t:t + 1, CQ:CQ + RQ], RQ, None) for t in range(NT)] +
                  [(tok[:, t:t + 1, CKV:CKV + RKV], tok[:, t:t + 1, CKV:CKV + RKV], RKV, None) for t in range(NT)])
        rope_stage(k, f"rope_k{l}", in_place([tok[:, t, KR:KR + DR].rearrange("p (n w) -> p n w", w=DR) for t in range(NT)]), k.cos_b, k.sin_b, DR)
        with nc.sbuf_tensor(f"mla{l}_lat", [P, 3, S], F32) as lat:
            kpe = [(qT[64:64 + DR, 0, :], 64)]
            blocks = [(columns_of(tok, CQ + j * P, P), lat[:, j, :], k.q_norm[:, l, j:j + 1], None) for j in range(2)]
            blocks.append((columns_of(tok, CKV, P), lat[:, 2, :], k.kv_norm[:, l, :], None))
            blocks += [(columns_of(tok, KR - DN, DQ), (kT[DN:DQ, h, :], DN), None, None) for h in range(H2)]
            transpose_stage(k, f"turn_lat{l}", blocks)
            wq, wkv = chunk_view(k, ("up", l))
            key = ("up", l)
            jobs = []
            for t in range(NT):
                c = slice(t * P, (t + 1) * P)
                for c0, c1 in ((0, COL), (COL, H2 * DQ)):
                    jobs.append(Job([(lat[:, j, c], wq[:, j, c0:c1]) for j in range(2)], P, c1 - c0, copy_to(k, tok[:, t, c0:c1]),
                                    engine_of(len(jobs)), key))
                wv = wkv[:, 0, :].rearrange("p (h n) -> p h n", n=DN + DV2)[:, :, DN:]
                jobs.append(Job([(lat[:, 2, c], wv)], P, H2 * DV2, copy_to(k, v[:, t, :]), engine_of(len(jobs)), key))
            for h in range(H2):
                jobs.append(Job([(wkv[:, 0, h * (DN + DV2):h * (DN + DV2) + DN], lat[:, 2, :])], DN, S, copy_to(k, kT[0:DN, h, :]),
                                engine_of(len(jobs)), key))
            gemm_stage(k, f"up{l}", jobs, last_key=key)
        rope_stage(k, f"rope_q{l}", in_place([tok[:, t, 0:H2 * DQ].rearrange("p (n w) -> p n w", w=DQ)[:, :, DN:] for t in range(NT)]), k.cos_b, k.sin_b, DR)
        transpose_stage(k, f"turn_q{l}", [(columns_of(tok, h * DQ, DQ), qT[:, h, :], None, None) for h in range(H2)])

        def step(pair, i):
            def out(chain, psum, inv, m):
                h = 2 * pair + m
                return nc.vector.tensor_scalar(tok[:, i, OUT + h * DV2:OUT + (h + 1) * DV2], psum, inv, None, ALU.mult)
            return Step(i=i, q=[qT[:, 2 * pair + m, i * P:(i + 1) * P] for m in range(2)],
                                   k=[kT[:, 2 * pair + m, :] for m in range(2)],
                                   v=lambda m, j: v[:, j, (2 * pair + m) * DV2:(2 * pair + m + 1) * DV2], out=out)
        attention_stage(k, f"mla{l}", [step(pair, i) for pair in range(H2 // 2) for i in range(NT)], DQ ** -0.5, False)


def mlp_stages(k, l):
    nc = k.nc
    with nc.sbuf_tensor(f"mlp{l}_u", [P, FF2 // P, S], F32) as u:
        jobs = []
        for n in range(FF2 // COL):
            (w,) = chunk_view(k, ("ff1", l, n))
            for f in range(4):
                def squared_relu(e, chain, psum, dst=u[:, 4 * n + f, :]):
                    chain(nc.scalar.activation(dst, psum, ACT.Relu))
                    return nc.scalar.activation(dst, dst, ACT.Square)
                jobs.append(Job([(w[:, j, f * P:(f + 1) * P], k.hT[:, j, :]) for j in range(ND)], P, S, squared_relu, "act", ("ff1", l, n)))
        gemm_stage(k, f"ff1_{l}", jobs, last_key=("ff1", l, 7))
        ff2_stage(k, l, u)


def ff2_stage(k, l, u):
    nc = k.nc
    first = k.n_groups
    for half in range(2):
        for q in range(4):
            k.last_group[k.chunk_no[("ff2", l, half, q)]] = first + half * 4 + q + 1
    k.n_groups += 8
    with ExitStack() as ctx:
        summed = nc.alloc_semaphore(f"ff2_{l}_summed")
        added = nc.alloc_semaphore(f"ff2_{l}_added")
        bank = [ctx.enter_context(nc.psum_tensor(f"ff2_{l}_bank{i}", [P, COL], F32)) for i in range(8)]
        block = ctx.enter_context(nc.Block())

        @block.sync
        def _(sp):
            load_chunks(k, sp, ("ff2", l, 1, 3))

        @block.tensor
        def _(pe):
            for half in range(2):
                for q in range(4):
                    key = ("ff2", l, half, q)
                    wait_chunk(k, pe, key)
                    (w,) = chunk_view(k, key)
                    for t in range(NT):
                        for j in range(ND):
                            mm = nc.tensor.matmul(bank[half * 4 + t][:], u[:, q * ND + j, t * P:(t + 1) * P], w[:, j, :],
                                                  start=(q == 0 and j == 0), stop=(q == 3 and j == ND - 1))
                    mm.then_inc(k.groups_done, 1)

        @block.vector
        def _(dve):
            for half in range(2):
                dve.wait_ge(k.groups_done, first + half * 4 + 4)
                for t in range(NT):
                    cols = slice(half * COL, (half + 1) * COL)
                    nc.vector.tensor_tensor(k.x[:, t, cols], k.x[:, t, cols], bank[half * 4 + t][:], ALU.add).then_inc(added, 1)


def part2(k, a):
    nc = k.nc
    for l in range(LAYERS):
        with cleared_semaphores(nc):
            layer(k, a, l)
    rms_stage(k, "final_norm", [(k.x[:, t:t + 1, :], k.x[:, t:t + 1, :], D, k.final_row[:]) for t in range(NT)])


def layer(k, a, l):
    nc = k.nc
    with nc.sbuf_tensor(f"xn2_{l}", [P, NT, D], F32) as xn:
        rms_stage(k, f"norm_a{l}", row_norm_groups(k.x, xn))
        transpose_stage(k, f"turn_a{l}", [(columns_of(xn, j * P, P), k.hT[:, j, :], k.attn_norm[:, l, j:j + 1], None) for j in range(ND)])
    with nc.sbuf_tensor(f"tok2_{l}", [P, NT, IN2_W], F32) as tok, nc.sbuf_tensor(f"nsa_o{l}", [P, NT, 512], F32) as o:
        project2_stage(k, l, tok)
        nsa_stages(k, l, tok, o)
        mla_stages(k, l, tok)
        ob = tok[:, :, H2 * DQ:H2 * DQ + 512]
        rms_stage(k, f"mix_norm{l}", row_norm_groups(o, o) + row_norm_groups(ob, ob))
        transpose_stage(k, f"turn_mix{l}", [(columns_of(o, j * P, P), k.hT[:, j, :], k.nsa_norm[:, l, j:j + 1], None) for j in range(4)] +
                        [(columns_of(ob, j * P, P), k.hT[:, 4 + j, :], k.mla_norm[:, l, j:j + 1], None) for j in range(4)])
    out_stage(k, f"out2_{l}", [("out2", l, n) for n in range(2)])
    with nc.sbuf_tensor(f"xn3_{l}", [P, NT, D], F32) as xn:
        rms_stage(k, f"norm_m{l}", row_norm_groups(k.x, xn))
        transpose_stage(k, f"turn_m{l}", [(columns_of(xn, j * P, P), k.hT[:, j, :], k.mlp_norm[:, l, j:j + 1], None) for j in range(ND)])
    mlp_stages(k, l)


def store_stage(k, out):
    nc = k.nc
    with ExitStack() as ctx:
        stored = nc.alloc_semaphore("out_stored")
        block = ctx.enter_context(nc.Block())

        @block.sync
        def _(sp):
            sp.dma_start(out[0].rearrange("(t p) d -> p t d", p=P), k.x[:]).then_inc(stored, 16)
            sp.wait_ge(stored, 16)


class Program:

    def __init__(self, nc, a, ctx):
        self.nc, self.a, self.ctx = nc, a, ctx
        self.small = []
        self.n_groups = 0
        self.next_load = 0
        self.last_group = {}
        self.plan = plan_chunks(a)
        self.chunk_no = {key: n for n, (key, _) in enumerate(self.plan)}
        self.load_end = self.chunk_no[("out1", 1)]
        self.loaded_at, count = [], [0] * SLOTS
        for n, (_, parts) in enumerate(self.plan):
            count[n % SLOTS] += 16 * len(parts)
            self.loaded_at.append(count[n % SLOTS])

    def sb(self, name, shape, dt=F32):
        return self.ctx.enter_context(self.nc.sbuf_tensor(name, shape, dt))

    def loaded(self, name, shape, *sources):
        t = self.sb(name, shape)
        if len(sources) == 1:
            self.small.append((t[:], sources[0]))
        else:
            self.small += [(t[:, i], src) for i, src in enumerate(sources)]
        return t

    def constant(self, name):
        src = self.a[f"const_{name}"]
        return self.loaded(name, list(src.shape), src)


def column(v):
    return v.rearrange("(k p) -> p k", p=P)


def row(v):
    return v.partition_broadcast(P)


def build(nc, a, out):
    h2_dram = nc.dram_tensor("h2_rows", [S, D], F32).ap()
    y_dram = nc.dram_tensor("expert_rows", [S * TOPK + P, D], F32).ap()
    with ExitStack() as ctx:
        k = Program(nc, a, ctx)
        k.x = k.sb("x", [P, NT, D])
        k.ring = k.sb("ring", [P, SLOTS * SLOT])
        k.eps = k.sb("eps", [P, 1])
        k.ones = k.sb("ones", [P, P])
        k.gated = k.sb("gated", [P, COL])
        k.ident = k.constant("ident")
        k.causal_bias = k.constant("causal_bias")
        k.upper_incl = k.constant("upper_incl")
        k.upper_strict = k.constant("upper_strict")
        k.iota = k.constant("iota")
        k.place_no = k.constant("place_no")
        k.spare_no = k.constant("spare_no")
        k.cmp_mask = k.constant("cmp_mask")
        k.cmp_bias = k.constant("cmp_bias")
        k.cos_a, k.sin_a = k.constant("cos_a"), k.constant("sin_a")
        k.cos_b, k.sin_b = k.constant("cos_b"), k.constant("sin_b")

        def layers(name):
            return [column(a[name][l]) for l in range(LAYERS)]

        k.attn_norm = k.loaded("attn_norm", [P, LAYERS, ND], *layers("attn_norm_2"))
        k.mlp_norm = k.loaded("mlp_norm", [P, LAYERS, ND], *layers("mlp_norm_2"))
        k.nsa_norm = k.loaded("nsa_norm", [P, LAYERS, 4], *layers("nsa_out_norm_2"))
        k.mla_norm = k.loaded("mla_norm", [P, LAYERS, 4], *layers("mla_out_norm_2"))
        k.q_norm = k.loaded("q_norm", [P, LAYERS, 2], *layers("mla_q_norm_2"))
        k.kv_norm = k.loaded("kv_norm", [P, LAYERS, 1], *layers("mla_kv_norm_2"))
        k.final_row = k.loaded("final_row", [P, D], row(a["final_norm_2"]))
        k.ring_loaded = [nc.alloc_semaphore(f"ring_loaded{i}") for i in range(SLOTS)]
        k.groups_done = nc.alloc_semaphore("groups_done")
        k.small_pool_loaded = nc.alloc_semaphore("small_pool_loaded")
        k.gathered = [nc.alloc_semaphore(f"moe_gathered{u}") for u in range(2)]
        k.y_stored = [nc.alloc_semaphore(f"moe_y_stored{u}") for u in range(2)]
        with cleared_semaphores(nc), ExitStack() as k.ctx:
            k.c_col = k.loaded("c_col", [P, ND], column(a["c"][0]))
            k.norm1 = k.loaded("norm1", [P, ND], column(a["norm1_g"][0]))
            k.norm2_row = k.loaded("norm2_row", [P, D], row(a["norm2_g"][0]))
            k.a_q_gain = k.loaded("a_q_gain", [P, A_DK], row(a["a_q_gain"][0]))
            k.a_k_gain = k.loaded("a_k_gain", [P, A_DK], row(a["a_k_gain"][0]))
            k.a_out_gain = k.loaded("a_out_gain", [P, A_DV], row(a["a_out_gain"][0]))
            k.b_q_gain = k.loaded("b_q_gain", [P, B_DK], row(a["b_q_gain"][0]))
            k.b_k_gain = k.loaded("b_k_gain", [P, B_DK], row(a["b_k_gain"][0]))
            k.c_out_gain = k.loaded("c_out_gain", [P, C_DV], row(a["c_out_gain"][0]))
            k.lam_q = k.loaded("lam_q", [P, 2, A_DK], row(a["a_lam_q1"][0]), row(a["a_lam_q2"][0]))
            k.lam_k = k.loaded("lam_k", [P, 2, A_DK], row(a["a_lam_k1"][0]), row(a["a_lam_k2"][0]))
            k.c_wg2 = k.loaded("c_wg2", [C_RANK, C_HEADS * C_DK], a["c_w_g2"][0])
            k.c_bg = k.loaded("c_bg", [P, 1], column(a["c_b_g"][0]))
            k.conv_w = k.loaded("conv_w", [P, CONV_W, 2], *[column(a["d_conv_w"][0][i]) for i in range(CONV_W)])
            k.conv_b = k.loaded("conv_b", [P, 2], column(a["d_conv_b"][0]))
            k.lru_b = k.loaded("lru_b", [P, 2, 2], column(a["d_b_a"][0]), column(a["d_b_x"][0]))
            k.lru_lam = k.loaded("lru_lam", [P, 2], column(a["d_lambda"][0]))
            k.lru_w = k.sb("lru_w", [P, 2, 2, P])
            k.lru_blocks = [(k.lru_w[64 * (n % 2):64 * (n % 2) + 64, i, n // 2, 64 * (n % 2):64 * (n % 2) + 64], a[name][0][n])
                            for i, name in enumerate(("d_w_a", "d_w_x")) for n in range(4)]
            k.router_w = k.loaded("router_w", [P, ND, NE], a["router_w"][0].rearrange("(k p) n -> p k n", p=P))
            k.router_b = k.loaded("router_b", [1, NE], a["router_b"])
            k.mod = k.sb("mod", [P, 4, D])
            k.scale1, k.shift1 = k.sb("scale1", [P, ND]), k.sb("shift1", [P, ND])
            k.lam = k.sb("lam", [P, 1])
            k.gla_state = k.sb("gla_state", [P, 256])
            k.gla_tile_decay = k.sb("gla_tile_decay", [P, NT])
            k.gates = k.sb("gates", [P, NT, TOPK])
            k.row_token, k.row_place = k.sb("row_token", [P, MAXB + 2], I32), k.sb("row_place", [P, MAXB], I32)
            k.owner, k.pairs = k.sb("owner", [1, MAXB], I32), k.sb("pairs", [1, 1], I32)
            with nc.sbuf_tensor("hT1", [P, ND, S], F32) as k.hT:
                load_stage(k, a)
                part1(k, a)
                second_norm_stages(k, h2_dram)
                route_stages(k, a)
            expert_stage(k, a, h2_dram, y_dram)
            combine_stage(k, y_dram)
        with nc.sbuf_tensor("hT2", [P, ND, S], F32) as k.hT:
            part2(k, a)
        store_stage(k, out)


INPUTS = ("x c ada_w ada_b norm1_g norm2_g w_in w_out a_q_gain a_k_gain a_lam_q1 a_lam_k1 a_lam_q2 a_lam_k2 a_out_gain b_q_gain "
          "b_k_gain c_w_g2 c_b_g c_out_gain d_conv_w d_conv_b d_w_a d_b_a d_w_x d_b_x d_lambda router_w router_b exp_w_up exp_b_up "
          "exp_w_down exp_b_down attn_norm_2 w_in_2 cmp_pos_k_2 cmp_w1_k_2 cmp_w2_k_2 cmp_pos_v_2 cmp_w1_v_2 cmp_w2_v_2 mla_q_norm_2 "
          "w_q_up_2 mla_kv_norm_2 w_kv_up_2 nsa_out_norm_2 mla_out_norm_2 w_out_2 mlp_norm_2 w_ff1_2 w_ff2_2 final_norm_2").split()


def kernel(**inputs):
    import concourse.bacc as bacc
    from concourse.bass_utils import run_bass_kernel_spmd

    nc = bacc.Bacc("TRN2", target_bir_lowering=False, num_devices=1)
    arrays = {n: np.ascontiguousarray(inputs[n]) for n in INPUTS}
    arrays |= {f"const_{n}": v for n, v in host_constants().items()}
    a = {n: nc.dram_tensor(f"in_{n}", v.shape, mybir.dt.from_np(v.dtype), kind="ExternalInput").ap() for n, v in arrays.items()}
    out = nc.dram_tensor("out", [1, S, D], F32, kind="ExternalOutput").ap()
    build(nc, a, out)
    result = run_bass_kernel_spmd(nc, [{f"in_{n}": v for n, v in arrays.items()}], core_ids=[0])
    return result.results[0]["out"]
```

```python
import math
from contextlib import ExitStack, contextmanager

import numpy as np

import concourse.bass as bass
from concourse import mybir

F32 = mybir.dt.float32
BF16 = mybir.dt.bfloat16
F32R = mybir.dt.float32r
I32 = mybir.dt.int32
U32 = mybir.dt.uint32
ALU = mybir.AluOpType
ACT = mybir.ActivationFunctionType
X = mybir.AxisListType.X

P = 128
S = 512
NT = S // P
D = 1024
ND = D // P
EPS = 1e-6
NEG = -1e30
COL = 512
SLOTS = 3
SLOT = ND * COL
PIECES = 4

A_HEADS, A_DK, A_DV = 4, 32, 64
B_HEADS, B_DK = 4, 64
C_HEADS, C_DK, C_DV, C_RANK, C_TAU = 4, 32, 64, 16, 16.0
SUB = 16
NSUB = P // SUB
DECAY_CLAMP = 60.0
W_D = 256
CONV_W = 4
LAM_INIT = 0.8 - 0.6 * math.exp(-0.3 * 0)
NE, TOPK, FF = 32, 4, 1024
BR = 64
MAXB = S * TOPK // BR + NE
UNITS = FF // 4
ALPHA, LIMIT = 1.702, 7.0

OUT_A, OUT_B, OUT_C = 0, 768, 1024
CR = 1792

LAYERS = 2
H2, G2, R2, DK2 = 8, 2, 4, 64
CB, CS, CHID = 32, 16, 256
NCMP = S // CS - 1
CPAD = 32
RQ, RKV, DR, DN, DV2 = 256, 128, 32, 64, 64
DQ = DN + DR
FF2 = 4096


class Job:

    def __init__(self, mm, m, n, evac, eng, chunk=None, finish=None, needs=None):
        self.mm, self.m, self.n, self.evac, self.eng, self.chunk = mm, m, n, evac, eng, chunk
        self.finish, self.needs = finish, needs


class Step:

    def __init__(self, i, q, k, v, out, gate=None):
        self.i, self.q, self.k, self.v, self.out, self.gate = i, q, k, v, out, gate


class Chain:

    def __init__(self, engine, sem):
        self.engine, self.sem, self.n = engine, sem, 0

    def __call__(self, instruction):
        self.n += 1
        instruction.then_inc(self.sem, 1)
        self.engine.wait_ge(self.sem, self.n)


def host_constants():
    p = np.arange(P)
    tok = np.arange(S)
    f32 = np.float32
    out = {}
    out["ident"] = np.eye(P, dtype=f32)
    out["causal_bias"] = np.where(p[None, :] <= p[:, None], 0.0, NEG).astype(f32)
    out["upper_incl"] = (p[:, None] <= p[None, :]).astype(f32)
    out["upper_strict"] = (p[:, None] < p[None, :]).astype(f32)
    out["iota"] = np.tile(np.arange(P, dtype=f32), (P, 1))
    out["place_no"] = (1 + TOPK * tok.reshape(NT, P).T[:, :, None] + np.arange(TOPK)).reshape(P, NT * TOPK).astype(f32)
    out["spare_no"] = (1 + TOPK * S + p[:, None] % BR).astype(f32)
    out["row_no"] = np.tile((p % BR).astype(f32), (P, 1))
    out["half_no"] = (p[:, None] // BR).astype(f32)
    n = np.arange(CPAD)
    seen = (n[None, :] * CS + CB - 1 <= tok[:, None]) & (n[None, :] < NCMP)
    seen = np.ascontiguousarray(seen.reshape(NT, P, CPAD).transpose(1, 0, 2))
    out["cmp_mask"] = seen.astype(f32)
    out["cmp_bias"] = np.where(seen, 0.0, NEG).astype(f32)
    for name, dim in (("a", DK2), ("b", DR)):
        inv = (1.0 / (np.float32(10000.0) ** (np.arange(0, dim, 2, dtype=f32) / np.float32(dim)))).astype(f32)
        ang = (tok.astype(f32)[:, None] * inv[None, :]).astype(f32)
        ang = np.concatenate([ang, ang], axis=-1)
        sign = np.where(np.arange(dim) < dim // 2, -1.0, 1.0).astype(f32)
        out[f"cos_{name}"] = np.ascontiguousarray(np.cos(ang).astype(f32).reshape(NT, P, dim).transpose(1, 0, 2))
        out[f"sin_{name}"] = np.ascontiguousarray((np.sin(ang) * sign).astype(f32).reshape(NT, P, dim).transpose(1, 0, 2))
    return out




def plan_chunks(a):
    plan = []

    def cols(key, w, c0, c1):
        plan.append((key, [(0, w.shape[0] // P * (c1 - c0), w[:, c0:c1].rearrange("(k p) n -> p k n", p=P), c1 - c0)]))

    for n in range(12):
        cols(("ada", n), a["ada_w"][0], n * COL, (n + 1) * COL)
    for n, (c0, c1) in enumerate(IN1):
        cols(("in1", n), a["w_in"][0], c0, c1)
    for n in range(2):
        cols(("out1", n), a["w_out"][0], n * COL, (n + 1) * COL)
    for l in range(LAYERS):
        for n, (c0, c1) in enumerate(IN2):
            cols(("in2", l, n), a["w_in_2"][l], c0, c1)
        for kv in "kv":
            w = a[f"cmp_w1_{kv}_2"][l].rearrange("(k p) n -> p k n", p=P)
            plan.append((("cmp", l, kv), [(0, 16 * CHID, w, CHID)]))
        plan.append((("up", l), [
            (0, 2 * H2 * DQ, a["w_q_up_2"][l].rearrange("(k p) n -> p k n", p=P), H2 * DQ),
            (2 * H2 * DQ, H2 * (DN + DV2), a["w_kv_up_2"][l].rearrange("(k p) n -> p k n", p=P), H2 * (DN + DV2)),
        ]))
        for n in range(2):
            cols(("out2", l, n), a["w_out_2"][l], n * COL, (n + 1) * COL)
        for q in range(4):
            for n in (2 * q, 2 * q + 1):
                cols(("ff1", l, n), a["w_ff1_2"][l], n * COL, (n + 1) * COL)
            for half in range(2):
                w = a["w_ff2_2"][l][q * D:(q + 1) * D, half * COL:(half + 1) * COL].rearrange("(k p) n -> p k n", p=P)
                plan.append((("ff2", l, half, q), [(0, SLOT, w, COL)]))
    return plan


IN1 = [(0, 512), (512, 1024), (1024, 1536), (1536, 2048), (2048, 2320), (2320, 2832)]
IN2 = [(0, 512), (512, 1024), (1024, 1536), (1536, 1720)]


def chunk_view(k, key):
    n = k.chunk_no[key]
    base = (n % SLOTS) * SLOT
    _, parts = k.plan[n]
    return [k.ring[:, base + off:base + off + size].rearrange("p (k n) -> p k n", n=width)
            for off, size, _, width in parts]


def wait_chunk(k, eng, key):
    n = k.chunk_no[key]
    eng.wait_ge(k.ring_loaded[n % SLOTS], k.loaded_at[n])


def load_chunks(k, sp, last_key):
    limit = k.chunk_no[last_key] + SLOTS if last_key is not None else SLOTS - 1
    while k.next_load <= min(limit, k.load_end):
        n = k.next_load
        if n >= SLOTS:
            sp.wait_ge(k.groups_done, k.last_group[n - SLOTS])
        base = (n % SLOTS) * SLOT
        for off, size, src, width in k.plan[n][1]:
            sp.dma_start(k.ring[:, base + off:base + off + size].rearrange("p (k n) -> p k n", n=width),
                         src).then_inc(k.ring_loaded[n % SLOTS], 16)
        k.next_load += 1




def gemm_stage(k, name, jobs, banks=8, last_key=None, extra=None):
    nc = k.nc
    first = k.n_groups
    for n, job in enumerate(jobs):
        if job.chunk is not None:
            k.last_group[k.chunk_no[job.chunk]] = first + n + 1
    k.n_groups += len(jobs)
    order = {"act": [n for n, j in enumerate(jobs) if j.eng == "act"],
             "dve": [n for n, j in enumerate(jobs) if j.eng == "dve"]}
    rank = {n: i for e in order for i, n in enumerate(order[e])}
    with ExitStack() as ctx:
        evac_done = {e: nc.alloc_semaphore(f"{name}_{e}_evacuated") for e in order}
        evac_step = {e: nc.alloc_semaphore(f"{name}_{e}_step") for e in order}
        bank = [ctx.enter_context(nc.psum_tensor(f"{name}_bank{i}", [P, COL], F32)) for i in range(banks)]
        block = ctx.enter_context(nc.Block())

        @block.sync
        def _(sp):
            if last_key is not None:
                load_chunks(k, sp, last_key)

        @block.tensor
        def _(pe):
            seen = None
            for n, job in enumerate(jobs):
                if job.chunk is not None and job.chunk != seen:
                    wait_chunk(k, pe, job.chunk)
                    seen = job.chunk
                if n >= banks:
                    e = jobs[n - banks].eng
                    pe.wait_ge(evac_done[e], rank[n - banks] + 1)
                out = bank[n % banks][:job.m, :job.n]
                for i, (lhsT, rhs) in enumerate(job.mm):
                    mm = nc.tensor.matmul(out, lhsT, rhs, start=(i == 0), stop=(i == len(job.mm) - 1))
                mm.then_inc(k.groups_done, 1)

        def evacuate(eng, e):
            chain = Chain(eng, evac_step[e])
            for i, n in enumerate(order[e]):
                eng.wait_ge(k.groups_done, first + n + 1)
                if i >= 1:
                    eng.wait_ge(evac_done[e], i)
                jobs[n].evac(jobs[n].eng, chain, bank[n % banks][:jobs[n].m, :jobs[n].n]).then_inc(evac_done[e], 1)

        @block.scalar
        def _(act):
            evacuate(act, "act")

        @block.vector
        def _(dve):
            evacuate(dve, "dve")




class Halves:

    def __init__(self, hi, lo):
        self.hi, self.lo = hi, lo

    def __getitem__(self, index):
        return Halves(self.hi[index], self.lo[index])


def split_chunk(k, key):
    (w,) = chunk_view(k, key)
    if key not in k.split_no:
        k.split_no[key] = len(k.split_no)
    at = k.w_split[:, k.split_no[key] % 2, :, 0:w.shape[1] * w.shape[2]].rearrange("p s (k n) -> p s k n", n=w.shape[2])
    return Halves(at[:, 0], at[:, 1])


def split_gemm_stage(k, name, jobs, banks=8, last_key=None):
    nc = k.nc
    first = k.n_groups
    for n, job in enumerate(jobs):
        k.last_group[k.chunk_no[job.chunk]] = first + n + 1
    k.n_groups += len(jobs)
    chunks = list(dict.fromkeys(job.chunk for job in jobs))
    order = {e: [n for n, j in enumerate(jobs) if j.eng == e] for e in ("act", "dve")}
    rank = {n: i for e in order for i, n in enumerate(order[e])}
    finish_rank = {n: i for i, n in enumerate(n for n, j in enumerate(jobs) if j.finish)}
    with ExitStack() as ctx:
        evac_done = {e: nc.alloc_semaphore(f"{name}_{e}_evacuated") for e in order}
        evac_step = {e: nc.alloc_semaphore(f"{name}_{e}_step") for e in order}
        hi_made, lo_made = nc.alloc_semaphore(f"{name}_hi_made"), nc.alloc_semaphore(f"{name}_lo_made")
        finished = nc.alloc_semaphore(f"{name}_finished")
        bank = [ctx.enter_context(nc.psum_tensor(f"{name}_bank{i}", [P, COL], F32)) for i in range(banks)]
        block = ctx.enter_context(nc.Block())

        def pieces(c):
            blocks = chunk_view(k, chunks[c])[0].shape[1]
            return [(c * PIECES + i, slice(blocks * i // PIECES, blocks * (i + 1) // PIECES)) for i in range(PIECES)]

        @block.sync
        def _(sp):
            load_chunks(k, sp, last_key)

        @block.tensor
        def _(pe):
            needed = 0
            for n, job in enumerate(jobs):
                if n >= banks:
                    e = jobs[n - banks].eng
                    pe.wait_ge(evac_done[e], rank[n - banks] + 1)
                opens = n == 0 or jobs[n - 1].chunk != job.chunk
                starts = {at.start: piece for piece, at in pieces(chunks.index(job.chunk))} if opens else {}
                out = bank[n % banks][:job.m, :job.n]
                for i, (lhsT, rhs) in enumerate(job.mm):
                    if i in starts:
                        pe.wait_ge(hi_made, starts[i] + 1)
                        pe.wait_ge(lo_made, starts[i] + 1)
                    if job.needs is not None and finish_rank[job.needs[i]] + 1 > needed:
                        needed = finish_rank[job.needs[i]] + 1
                        pe.wait_ge(finished, needed)
                    last = i == len(job.mm) - 1
                    nc.tensor.matmul(out, lhsT.hi, rhs.hi, start=(i == 0), stop=False)
                    nc.tensor.matmul(out, lhsT.hi, rhs.lo, start=False, stop=False)
                    mm = nc.tensor.matmul(out, lhsT.lo, rhs.hi, start=False, stop=last)
                mm.then_inc(k.groups_done, 1)

        def work(eng, e, split):
            chain = Chain(eng, evac_step[e])
            split(0)
            for n, job in enumerate(jobs):
                if n == 0 or jobs[n - 1].chunk != job.chunk:
                    c = chunks.index(job.chunk)
                    if c + 1 < len(chunks):
                        split(c + 1)
                if job.eng == e:
                    eng.wait_ge(k.groups_done, first + n + 1)
                    if rank[n] >= 1:
                        eng.wait_ge(evac_done[e], rank[n])
                    if job.finish and finish_rank[n] >= 2:
                        eng.wait_ge(finished, finish_rank[n] - 1)
                    job.evac(e, chain, bank[n % banks][:job.m, :job.n]).then_inc(evac_done[e], 1)
                if job.finish and e == "dve":
                    eng.wait_ge(evac_done["act"], rank[n] + 1)
                    if finish_rank[n] >= 2:
                        eng.wait_ge(finished, finish_rank[n] - 1)
                    job.finish(chain).then_inc(finished, 1)

        @block.scalar
        def _(act):
            def split(c):
                (w,), halves = chunk_view(k, chunks[c]), split_chunk(k, chunks[c])
                wait_chunk(k, act, chunks[c])
                if c >= 2:
                    act.wait_ge(k.groups_done, k.last_group[k.chunk_no[chunks[c - 2]]])
                for _, at in pieces(c):
                    nc.scalar.activation(halves.hi[:, at], w[:, at], ACT.Copy).then_inc(hi_made, 1)
            work(act, "act", split)

        @block.vector
        def _(dve):
            def split(c):
                (w,), halves = chunk_view(k, chunks[c]), split_chunk(k, chunks[c])
                for piece, at in pieces(c):
                    dve.wait_ge(hi_made, piece + 1)
                    nc.vector.tensor_tensor(halves.lo[:, at], w[:, at], halves.hi[:, at].bitcast(F32), ALU.subtract).then_inc(lo_made, 1)
            work(dve, "dve", split)


def copy_to(k, dst, scale=None, bias=None):
    nc = k.nc

    def evac(e, chain, psum):
        src = psum if dst.shape == psum.shape else psum
        if e == "act":
            if scale is None and bias is None:
                return nc.scalar.activation(dst, src, ACT.Copy)
            return nc.scalar.activation(dst, src, ACT.Identity, bias=bias if bias is not None else 0.0,
                                        scale=scale if scale is not None else 1.0)
        if scale is None and bias is None:
            return nc.vector.tensor_copy(dst, src)
        if scale is None:
            return nc.vector.tensor_scalar(dst, src, bias, None, ALU.add)
        if bias is None:
            return nc.vector.tensor_scalar(dst, src, scale, None, ALU.mult)
        return nc.vector.tensor_scalar(dst, src, scale, bias, ALU.mult, ALU.add)
    return evac


def engine_of(n):
    return "act" if n % 2 == 0 else "dve"




def transpose_stage(k, name, blocks, last_key=None):
    nc = k.nc
    with ExitStack() as ctx:
        turned = nc.alloc_semaphore(f"{name}_turned")
        taken = [nc.alloc_semaphore(f"{name}_taken_{e}") for e in ("act", "dve")]
        bank = [ctx.enter_context(nc.psum_tensor(f"{name}_bank{i}", [P, COL], F32)) for i in range(4)]
        block = ctx.enter_context(nc.Block())

        @block.sync
        def _(sp):
            if last_key is not None:
                load_chunks(k, sp, last_key)

        @block.tensor
        def _(pe):
            for n, (src, _, _, _) in enumerate(blocks):
                if n >= 4:
                    pe.wait_ge(taken[n % 2], (n - 4) // 2 + 1)
                w = src[0].shape[-1] if len(src[0].shape) == 2 else src[0].shape[1] * src[0].shape[2]
                for t in range(NT):
                    tr = nc.tensor.transpose(bank[n % 4][:w, t * P:(t + 1) * P], src[t], k.ident[:])
                tr.then_inc(turned, 1)

        def take(eng, e):
            for n, (src, dst, scale, bias) in enumerate(blocks):
                if n % 2 == e:
                    eng.wait_ge(turned, n + 1)
                    lo, w = (dst[1], dst[0].shape[0]) if isinstance(dst, tuple) else (0, dst.shape[0])
                    out = dst[0] if isinstance(dst, tuple) else dst
                    copy_to(k, out, scale, bias)("act" if e == 0 else "dve", None,
                                                 bank[n % 4][lo:lo + w, :]).then_inc(taken[e], 1)

        @block.scalar
        def _(act):
            take(act, 0)

        @block.vector
        def _(dve):
            take(dve, 1)


def rms_stage(k, name, groups):
    nc = k.nc
    with ExitStack() as ctx:
        squares = nc.alloc_semaphore(f"{name}_sums")
        roots = nc.alloc_semaphore(f"{name}_roots")
        step = nc.alloc_semaphore(f"{name}_step")
        sq = ctx.enter_context(nc.sbuf_tensor(f"{name}_sq", [P, 1024], F32))
        total = sum(g[0].shape[1] for g in groups)
        ss = ctx.enter_context(nc.sbuf_tensor(f"{name}_ss", [P, total], F32))
        rms = ctx.enter_context(nc.sbuf_tensor(f"{name}_rms", [P, total], F32))
        rinv = ctx.enter_context(nc.sbuf_tensor(f"{name}_rinv", [P, total], F32))
        block = ctx.enter_context(nc.Block())
        at = [sum(g[0].shape[1] for g in groups[:i]) for i in range(len(groups))]

        @block.vector
        def _(dve):
            chain = Chain(dve, step)
            for i, (src, dst, w, gain) in enumerate(groups):
                n = src.shape[1]
                tmp = sq[:, 0:n * w].rearrange("p (n w) -> p n w", w=w)
                chain(nc.vector.tensor_tensor(tmp, src, src, ALU.mult))
                nc.vector.tensor_reduce(ss[:, at[i]:at[i] + n], tmp, X, ALU.add).then_inc(squares, 1)
                dve.wait_ge(squares, i + 1)
            for i, (src, dst, w, gain) in enumerate(groups):
                n = src.shape[1]
                r = rinv[:, at[i]:at[i] + n]
                dve.wait_ge(roots, i + 1)
                chain(nc.vector.reciprocal(r, rms[:, at[i]:at[i] + n]))
                if gain is None:
                    chain(nc.vector.tensor_tensor(dst, src, r.unsqueeze(2).to_broadcast([P, n, w]), ALU.mult))
                else:
                    chain(nc.vector.tensor_tensor(dst, src, r.unsqueeze(2).to_broadcast([P, n, w]), ALU.mult))
                    chain(nc.vector.tensor_tensor(dst, dst, gain.unsqueeze(1).to_broadcast([P, n, w]), ALU.mult))

        @block.scalar
        def _(act):
            for i, (src, dst, w, gain) in enumerate(groups):
                n = src.shape[1]
                act.wait_ge(squares, i + 1)
                nc.scalar.activation(rms[:, at[i]:at[i] + n], ss[:, at[i]:at[i] + n], ACT.Sqrt,
                                     bias=k.eps[:], scale=1.0 / w).then_inc(roots, 1)


def norm_turn_stage(k, name, parts, dst, last_key=None):
    nc = k.nc
    split = isinstance(dst, Halves)
    w = parts[0][0].shape[2]
    n_parts, per = len(parts), w // P
    with ExitStack() as ctx:
        squared, rooted, inverted, scaled = (nc.alloc_semaphore(f"{name}_{s}") for s in ("squared", "rooted", "inverted", "scaled"))
        turned, taken, lo_taken = (nc.alloc_semaphore(f"{name}_{s}") for s in ("turned", "taken", "lo_taken"))
        sq = ctx.enter_context(nc.sbuf_tensor(f"{name}_sq", [P, 2, w], F32))
        ss = ctx.enter_context(nc.sbuf_tensor(f"{name}_ss", [P, NT * n_parts], F32))
        rms = ctx.enter_context(nc.sbuf_tensor(f"{name}_rms", [P, NT * n_parts], F32))
        inv = ctx.enter_context(nc.sbuf_tensor(f"{name}_inv", [P, NT * n_parts], F32))
        bank = [ctx.enter_context(nc.psum_tensor(f"{name}_bank{i}", [P, COL], F32)) for i in range(ND)]
        block = ctx.enter_context(nc.Block())
        rows = [(t, i) for t in range(NT) for i in range(n_parts)]

        def out(j):
            _, _, scale, shift = parts[j // per]
            return j % per, scale[:, j % per:j % per + 1], None if shift is None else shift[:, j % per:j % per + 1]

        @block.sync
        def _(sp):
            if last_key is not None:
                load_chunks(k, sp, last_key)

        @block.scalar
        def _(act):
            for n, (t, i) in enumerate(rows):
                if n >= 2:
                    act.wait_ge(squared, n - 1)
                nc.scalar.activation(sq[:, n % 2, :], parts[i][0][:, t, :], ACT.Square, accum_out=ss[:, n:n + 1]).then_inc(squared, 1)
            act.wait_ge(squared, len(rows))
            nc.scalar.activation(rms[:], ss[:], ACT.Sqrt, bias=k.eps[:], scale=1.0 / w).then_inc(rooted, 1)
            for j in range(ND):
                _, scale, shift = out(j)
                if split or j % 2 == 0:
                    act.wait_ge(turned, j + 1)
                    copy_to(k, dst.hi[:, j, :] if split else dst[:, j, :], scale, shift)("act", None, bank[j][:]).then_inc(taken, 1)

        @block.vector
        def _(dve):
            dve.wait_ge(rooted, 1)
            nc.vector.reciprocal(inv[:], rms[:]).then_inc(inverted, 1)
            dve.wait_ge(inverted, 1)
            for n, (t, i) in enumerate(rows):
                nc.vector.tensor_scalar(parts[i][1][:, t, :], parts[i][0][:, t, :], inv[:, n:n + 1], None, ALU.mult).then_inc(scaled, 1)
            for j in range(ND):
                _, scale, shift = out(j)
                if split:
                    dve.wait_ge(taken, j + 1)
                    nc.vector.scalar_tensor_tensor(dst.lo[:, j, :], bank[j][:], scale, dst.hi[:, j, :].bitcast(F32),
                                                   ALU.mult, ALU.subtract).then_inc(lo_taken, 1)
                elif j % 2 == 1:
                    dve.wait_ge(turned, j + 1)
                    copy_to(k, dst[:, j, :], scale, shift)("dve", None, bank[j][:]).then_inc(lo_taken, 1)

        @block.tensor
        def _(pe):
            for n, (t, i) in enumerate(rows):
                pe.wait_ge(scaled, n + 1)
                for j in range(per):
                    tr = nc.tensor.transpose(bank[i * per + j][:, t * P:(t + 1) * P], parts[i][1][:, t, j * P:(j + 1) * P], k.ident[:])
                    if t == NT - 1:
                        tr.then_inc(turned, 1)


def row_norm_groups(src, dst, gain=None):
    return [(src[:, t:t + 1, :], dst[:, t:t + 1, :], src.shape[2], gain) for t in range(NT)]


def columns_of(src, c0, w):
    return [src[:, t, c0:c0 + w] for t in range(NT)]




def attention_stage(k, name, steps, scale, pair, lam=None, gated=False, last_key=None):
    nc = k.nc
    maps = 2
    turns = 1 if pair else 2
    with ExitStack() as ctx:
        def sem(s):
            return nc.alloc_semaphore(f"{name}_{s}")

        def sb(s, shape):
            return ctx.enter_context(nc.sbuf_tensor(f"{name}_{s}", shape, F32))

        scores_ready, bias_ready, exp_ready = sem("scores"), sem("bias"), sem("exp")
        weights_ready, turned = sem("weights"), sem("turned")
        taken_act, taken_dve, values_ready, out_taken = sem("taken_act"), sem("taken_dve"), sem("values"), sem("out")
        step_dve, inverted = sem("step"), sem("inverted")
        p = sb("p", [P, 2, maps, S])
        pt = sb("pt", [P, 2, turns, S])
        w = sb("w", [P, 2, S]) if pair else None
        top = sb("top", [P, 2, maps])
        neg = sb("neg", [P, 2, maps])
        total = sb("total", [P, 4, maps])
        inv = sb("inv", [P, 4, maps])
        lam_inv = sb("lam_inv", [P, 2, 1]) if pair else None
        sc = [ctx.enter_context(nc.psum_tensor(f"{name}_s{b}", [P, maps, COL], F32)) for b in range(2)]
        tr = [ctx.enter_context(nc.psum_tensor(f"{name}_t{b}", [P, COL], F32)) for b in range(2)]
        ov = [ctx.enter_context(nc.psum_tensor(f"{name}_o{b}", [P, COL], F32)) for b in range(2)]
        block = ctx.enter_context(nc.Block())
        n_steps = len(steps)

        @block.sync
        def _(sp):
            if last_key is not None:
                load_chunks(k, sp, last_key)

        @block.tensor
        def _(pe):
            def scores(n):
                st, b = steps[n], n % 2
                nk = P * (st.i + 1)
                if n >= 2:
                    pe.wait_ge(exp_ready, maps * (n - 1))
                for m in range(maps):
                    nc.tensor.matmul(sc[b][:, m, 0:nk], st.q[m], st.k[m][:, 0:nk], start=True, stop=False)
                for m in range(maps):
                    mm = nc.tensor.matmul(sc[b][:, m, nk - P:nk], k.ident_half[:], k.causal_half[:], start=False, stop=True)
                mm.then_inc(scores_ready, 1)

            def turn(n):
                st, b = steps[n], n % 2
                for m in range(turns):
                    u = n * turns + m
                    if pair:
                        pe.wait_ge(weights_ready, n + 1)
                    else:
                        pe.wait_ge(exp_ready, maps * n + m + 1)
                    if u >= 2:
                        pe.wait_ge(taken_act if u % 2 == 0 else taken_dve, (u - 2) // 2 + 1)
                    for j in range(st.i + 1):
                        row = w[:, b, j * P:(j + 1) * P] if pair else p[:, b, m, j * P:(j + 1) * P]
                        t = nc.tensor.transpose(tr[u % 2][:, j * P:(j + 1) * P], row, k.ident[:])
                    t.then_inc(turned, 1)

            def values(n):
                st, b = steps[n], n % 2
                if n >= 2:
                    pe.wait_ge(out_taken, n - 1)
                for m in range(turns):
                    u = n * turns + m
                    pe.wait_ge(taken_act if u % 2 == 0 else taken_dve, u // 2 + 1)
                    for j in range(st.i + 1):
                        mm = nc.tensor.matmul(ov[b][:, m * 64:(m + 1) * 64], pt[:, b, m, j * P:(j + 1) * P],
                                              st.v(m, j), start=(j == 0), stop=(j == st.i))
                mm.then_inc(values_ready, 1)

            scores(0)
            scores(1)
            turn(0)
            for n in range(n_steps):
                if n + 2 < n_steps:
                    scores(n + 2)
                if n + 1 < n_steps:
                    turn(n + 1)
                values(n)

        def take_turned(eng, n, m):
            u, b = n * turns + m, n % 2
            nk = P * (steps[n].i + 1)
            if n >= 2:
                eng.wait_ge(values_ready, n - 1)
            eng.wait_ge(turned, u + 1)
            if u % 2 == 0:
                nc.scalar.activation(pt[:, b, m, 0:nk], tr[0][:, 0:nk], ACT.Copy).then_inc(taken_act, 1)
            else:
                nc.vector.tensor_copy(pt[:, b, m, 0:nk], tr[1][:, 0:nk]).then_inc(taken_dve, 1)

        @block.scalar
        def _(act):
            def exps(n):
                st, b = steps[n], n % 2
                nk = P * (st.i + 1)
                act.wait_ge(bias_ready, n + 1)
                if n >= 2:
                    if pair:
                        act.wait_ge(weights_ready, n - 1)
                    else:
                        act.wait_ge(turned, turns * (n - 1))
                if n >= 4:
                    act.wait_ge(inverted, n - 3)
                for m in range(maps):
                    nc.scalar.activation(p[:, b, m, 0:nk], sc[b][:, m, 0:nk], ACT.Exp, bias=neg[:, b, m:m + 1],
                                         scale=scale, accum_out=total[:, n % 4, m:m + 1]).then_inc(exp_ready, 1)

            def take(n):
                for m in range(turns):
                    if (n * turns + m) % 2 == 0:
                        take_turned(act, n, m)

            exps(0)
            exps(1)
            take(0)
            for n in range(n_steps):
                if n + 2 < n_steps:
                    exps(n + 2)
                if n + 1 < n_steps:
                    take(n + 1)

        @block.vector
        def _(dve):
            chain = Chain(dve, step_dve)

            def maxima(n):
                st, b = steps[n], n % 2
                nk = P * (st.i + 1)
                dve.wait_ge(scores_ready, n + 1)
                chain(nc.vector.tensor_reduce(top[:, b, :], sc[b][:, :, 0:nk], X, ALU.max))
                if n >= 2:
                    dve.wait_ge(exp_ready, maps * (n - 1))
                nc.vector.tensor_scalar(neg[:, b, :], top[:, b, :], -scale, None, ALU.mult).then_inc(bias_ready, 1)

            def inverses(n):
                st, b, c = steps[n], n % 2, n % 4
                nk = P * (st.i + 1)
                dve.wait_ge(exp_ready, maps * (n + 1))
                if n >= 4:
                    dve.wait_ge(out_taken, n - 3)
                nc.vector.reciprocal(inv[:, c, :], total[:, c, :]).then_inc(inverted, 1)
                dve.wait_ge(inverted, n + 1)
                if gated:
                    chain(nc.vector.tensor_tensor(inv[:, c, :], inv[:, c, :], st.gate, ALU.mult))
                if pair:
                    chain(nc.vector.tensor_tensor(lam_inv[:, b, :], inv[:, c, 1:2], lam, ALU.mult))
                    chain(nc.vector.tensor_scalar(p[:, b, 1, 0:nk], p[:, b, 1, 0:nk], lam_inv[:, b, :], None, ALU.mult))
                    if n >= 2:
                        dve.wait_ge(turned, n - 1)
                    nc.vector.scalar_tensor_tensor(w[:, b, 0:nk], p[:, b, 0, 0:nk], inv[:, c, 0:1], p[:, b, 1, 0:nk],
                                                   ALU.mult, ALU.subtract).then_inc(weights_ready, 1)

            def take(n):
                for m in range(turns):
                    if (n * turns + m) % 2 == 1:
                        take_turned(dve, n, m)

            def output(n):
                st, b = steps[n], n % 2
                dve.wait_ge(values_ready, n + 1)
                for m in range(turns):
                    last = st.out(chain, ov[b][:, m * 64:(m + 1) * 64], inv[:, n % 4, m:m + 1], m)
                last.then_inc(out_taken, 1)

            maxima(0)
            maxima(1)
            inverses(0)
            take(0)
            for n in range(n_steps):
                if n + 1 < n_steps:
                    inverses(n + 1)
                if n + 2 < n_steps:
                    maxima(n + 2)
                if n + 1 < n_steps:
                    take(n + 1)
                output(n)




def load_stage(k, a):
    nc = k.nc
    with ExitStack() as ctx:
        loaded = {e: nc.alloc_semaphore(f"small_{e}_loaded") for e in ("sp", "act")}
        loaded["pool"] = k.small_pool_loaded
        made = nc.alloc_semaphore("constants_made")
        block = ctx.enter_context(nc.Block())
        share = {"sp": k.small[0::3], "act": k.small[1::3], "pool": k.small[2::3]}

        def run(eng, e):
            for dst, src in share[e]:
                eng.dma_start(dst, src, allow_slow_non_contiguous=True).then_inc(loaded[e], 16)

        @block.sync
        def _(sp):
            for dst, src in k.tables:
                sp.dma_start(dst, src).then_inc(k.tables_loaded, 16)
            sp.dma_start(k.x[:], a["x"][0].rearrange("(t p) d -> p t d", p=P)).then_inc(loaded["sp"], 16)
            load_chunks(k, sp, None)
            sp.wait_ge(k.tables_loaded, 16 * len(k.tables))
            run(sp, "sp")
            sp.wait_ge(made, 3)
            for dst, src in k.lru_blocks:
                sp.dma_start(dst, src).then_inc(loaded["sp"], 16)
            sp.wait_ge(loaded["sp"], 16 * (len(share["sp"]) + 1 + len(k.lru_blocks)))

        @block.scalar
        def _(act):
            run(act, "act")
            act.wait_ge(loaded["act"], 16 * len(share["act"]))

        @block.gpsimd
        def _(pool):
            run(pool, "pool")
            pool.wait_ge(loaded["pool"], 16 * len(share["pool"]))

        @block.vector
        def _(dve):
            nc.vector.memset(k.eps[:], EPS).then_inc(made, 1)
            nc.vector.memset(k.ones[:], 1.0).then_inc(made, 1)
            nc.vector.memset(k.lru_w[:], 0.0).then_inc(made, 1)
            dve.wait_ge(k.tables_loaded, 16 * 2)
            nc.vector.tensor_copy(k.ident_half[:], k.ident[:]).then_inc(made, 1)
            nc.vector.tensor_copy(k.causal_half[:], k.causal_bias[:]).then_inc(made, 1)


def condition_stage(k, a):
    nc = k.nc
    with ExitStack() as ctx:
        cond = ctx.enter_context(nc.sbuf_tensor("cond", [P, ND], F32))
        cond_rows = ctx.enter_context(nc.sbuf_tensor("cond_rows", [P, ND, P], F32))
        ada_b = ctx.enter_context(nc.sbuf_tensor("ada_b_row", [1, 6 * D], F32))
        first = ctx.enter_context(nc.sbuf_tensor("mod_first", [P, 2, D], F32))
        with ExitStack() as inner:
            activated = nc.alloc_semaphore("cond_activated")
            spread = nc.alloc_semaphore("cond_spread")
            row_loaded = nc.alloc_semaphore("ada_b_loaded")
            block = inner.enter_context(nc.Block())

            @block.sync
            def _(sp):
                sp.dma_start(ada_b[:], a["ada_b"]).then_inc(row_loaded, 16)
                sp.wait_ge(row_loaded, 16)

            @block.scalar
            def _(act):
                nc.scalar.activation(cond[:], k.c_col[:], ACT.Silu).then_inc(activated, 1)

            @block.vector
            def _(dve):
                dve.wait_ge(activated, 1)
                nc.vector.tensor_copy(cond_rows[:], cond[:].unsqueeze(2).to_broadcast([P, ND, P])).then_inc(spread, 1)

        jobs = []
        for n in range(12):
            (w,) = chunk_view(k, ("ada", n))
            mm = [(cond_rows[:, j, :], w[:, j, :]) for j in range(ND)]
            mm.append((k.ones[0:1, :], ada_b[0:1, n * COL:(n + 1) * COL]))
            part, half = divmod(n, 2)
            dst = first[:, part, half * COL:(half + 1) * COL] if part < 2 else k.mod[:, part - 2, half * COL:(half + 1) * COL]
            jobs.append(Job(mm, P, COL, copy_to(k, dst), engine_of(n), ("ada", n)))
        gemm_stage(k, "ada", jobs, last_key=("ada", 11))

        with ExitStack() as inner:
            turned = nc.alloc_semaphore("mod_turned")
            step = nc.alloc_semaphore("mod_step")
            bank = inner.enter_context(nc.psum_tensor("mod_bank", [P, COL], F32))
            block = inner.enter_context(nc.Block())

            @block.tensor
            def _(pe):
                for part in range(2):
                    for j in range(ND):
                        mm = nc.tensor.matmul(bank[:, part * ND + j:part * ND + j + 1], first[0:1, part, j * P:(j + 1) * P],
                                              k.ones[0:1, 0:1], start=True, stop=True)
                mm.then_inc(turned, 1)

            @block.vector
            def _(dve):
                chain = Chain(dve, step)
                dve.wait_ge(turned, 1)
                chain(nc.vector.tensor_copy(k.shift1[:], bank[:, 0:ND]))
                chain(nc.vector.scalar_tensor_tensor(k.scale1[:], bank[:, ND:2 * ND], 1.0, k.norm1[:], ALU.add, ALU.mult))
                chain(nc.vector.scalar_tensor_tensor(k.mod[:, 2, :], k.mod[:, 2, :], 1.0, k.gain_row[:], ALU.add, ALU.mult))


def project1_stage(k, tok, fm, glow, dxg):
    jobs = []
    n = 0

    def token_major(key, lo, width, dst0):
        nonlocal n
        (w,) = chunk_view(k, key)
        for t in range(NT):
            mm = [(k.hT[:, j, t * P:(t + 1) * P], w[:, j, lo:lo + width]) for j in range(ND)]
            jobs.append(Job(mm, P, width, copy_to(k, tok[:, t, dst0:dst0 + width]), engine_of(n), key))
            n += 1

    def feature_major(key, lo, width, dst):
        nonlocal n
        (w,) = chunk_view(k, key)
        mm = [(w[:, j, lo:lo + width], k.hT[:, j, :]) for j in range(ND)]
        jobs.append(Job(mm, width, S, copy_to(k, dst), engine_of(n), key))
        n += 1

    for c in range(3):
        token_major(("in1", c), 0, COL, c * COL)
    feature_major(("in1", 3), 0, P, fm[:, 0, :])
    feature_major(("in1", 3), P, P, fm[:, 1, :])
    token_major(("in1", 3), 2 * P, 256, 1536)
    feature_major(("in1", 4), 0, C_RANK, glow[0:C_RANK, :])
    token_major(("in1", 4), C_RANK, 256, 1792)
    for j in range(4):
        feature_major(("in1", 5), j * P, P, dxg[:, j, :])
    gemm_stage(k, "in1", jobs, last_key=("in1", 5))


def lambda_stage(k):
    nc = k.nc
    with ExitStack() as ctx:
        dots = nc.alloc_semaphore("lam_dots")
        raised = nc.alloc_semaphore("lam_raised")
        step = nc.alloc_semaphore("lam_step")
        prod = ctx.enter_context(nc.sbuf_tensor("lam_prod", [P, 2, A_DK], F32))
        dot = ctx.enter_context(nc.sbuf_tensor("lam_dot", [P, 2], F32))
        e = ctx.enter_context(nc.sbuf_tensor("lam_exp", [P, 2], F32))
        block = ctx.enter_context(nc.Block())

        @block.vector
        def _(dve):
            chain = Chain(dve, step)
            chain(nc.vector.tensor_tensor(prod[:], k.lam_q[:], k.lam_k[:], ALU.mult))
            nc.vector.tensor_reduce(dot[:], prod[:], X, ALU.add).then_inc(dots, 1)
            dve.wait_ge(raised, 1)
            chain(nc.vector.tensor_tensor(k.lam[:], e[:, 0:1], e[:, 1:2], ALU.subtract))
            chain(nc.vector.tensor_scalar(k.lam[:], k.lam[:], LAM_INIT, None, ALU.add))

        @block.scalar
        def _(act):
            act.wait_ge(dots, 1)
            nc.scalar.activation(e[:], dot[:], ACT.Exp).then_inc(raised, 1)


def gla_stages(k, tok, fm, glow, a):
    nc = k.nc
    qs = C_DK ** -0.5
    with ExitStack() as ctx:
        def sb(s, shape):
            return ctx.enter_context(nc.sbuf_tensor(f"gla_{s}", shape, F32))

        z, b, ex = sb("z", [P, S]), sb("b", [P, S]), sb("ex", [P, S])
        qin, kout = sb("qin", [P, S]), sb("kout", [P, S])
        qsub = sb("qsub", [P, S // SUB, C_HEADS, SUB])
        gemm_stage(k, "gla_gate", [Job([(k.c_wg2[0:C_RANK, :], glow[0:C_RANK, :])], P, S,
                                       copy_to(k, z[:], bias=k.c_bg[:]), "dve")], banks=1)
        with ExitStack() as inner:
            def sem(s):
                return nc.alloc_semaphore(f"gla_{s}")

            soft, cum, raised, zeroed, step, astep = sem("soft"), sem("cum"), sem("raised"), sem("zeroed"), sem("step"), sem("astep")
            diff = inner.enter_context(nc.sbuf_tensor("gla_diff", [P, S], F32))
            end = inner.enter_context(nc.sbuf_tensor("gla_end", [P, S], F32))
            block = inner.enter_context(nc.Block())

            @block.gpsimd
            def _(pool):
                nc.gpsimd.memset(qsub[:], 0.0).then_inc(zeroed, 1)
                nc.gpsimd.memset(k.gla_state[:], 0.0).then_inc(zeroed, 1)

            @block.scalar
            def _(act):
                chain = Chain(act, astep)
                chain(nc.scalar.activation(ex[:], z[:], ACT.Abs))
                chain(nc.scalar.activation(ex[:], ex[:], ACT.Exp, scale=-1.0))
                nc.scalar.activation(ex[:], ex[:], ACT.Ln, bias=k.ones[:, 0:1]).then_inc(soft, 1)
                act.wait_ge(cum, 1)
                nc.scalar.activation(qin[:], b[:], ACT.Exp).then_inc(raised, 1)
                for t in range(NT):
                    nc.scalar.activation(kout[:, t * P:(t + 1) * P], b[:, t * P:(t + 1) * P], ACT.Exp, scale=-1.0,
                                         bias=b[:, t * P + P - 1:t * P + P]).then_inc(raised, 1)
                nc.scalar.activation(k.gla_tile_decay[:], b[:].rearrange("p (t n) -> p t n", n=P)[:, :, P - 1],
                                     ACT.Exp).then_inc(raised, 1)
                act.wait_ge(cum, 2)
                nc.scalar.activation(diff[:], diff[:], ACT.Exp).then_inc(raised, 1)

            @block.vector
            def _(dve):
                chain = Chain(dve, step)
                dve.wait_ge(soft, 1)
                chain(nc.vector.scalar_tensor_tensor(z[:], z[:], 0.0, ex[:], ALU.min, ALU.subtract))
                chain(nc.vector.tensor_scalar(z[:], z[:], 1.0 / C_TAU, None, ALU.mult))
                chain(nc.vector.memset(end[:], 1.0))
                for t in range(NT):
                    c = slice(t * P, (t + 1) * P)
                    scan = nc.vector.tensor_tensor_scan(b[:, c], end[:, c], z[:, c], 0.0, ALU.mult, ALU.add)
                    if t < NT - 1:
                        chain(scan)
                scan.then_inc(cum, 1)
                dve.wait_ge(cum, 1)
                bs = b[:].rearrange("p (n s) -> p n s", s=SUB)
                ref = bs[:, :, SUB // 2:SUB // 2 + 1].to_broadcast([P, S // SUB, SUB])
                nc.vector.tensor_tensor(diff[:].rearrange("p (n s) -> p n s", s=SUB), bs, ref, ALU.subtract).then_inc(cum, 1)
                dve.wait_ge(raised, 1 + NT + 1)
                chain(nc.vector.scalar_tensor_tensor(qin[:], fm[:, 0, :], qs, qin[:], ALU.mult, ALU.mult))
                chain(nc.vector.tensor_tensor(kout[:], fm[:, 1, :], kout[:], ALU.mult))
                dve.wait_ge(raised, 1 + NT + 2)
                dve.wait_ge(zeroed, 2)
                for h in range(C_HEADS):
                    r = slice(h * C_DK, (h + 1) * C_DK)
                    chain(nc.vector.scalar_tensor_tensor(
                        qsub[r, :, h, :], fm[r, 0, :].rearrange("p (n s) -> p n s", s=SUB), qs,
                        diff[r, :].rearrange("p (n s) -> p n s", s=SUB), ALU.mult, ALU.mult))

        with ExitStack() as inner:
            def sem(s):
                return nc.alloc_semaphore(f"gla2_{s}")

            def isb(s, shape):
                return inner.enter_context(nc.sbuf_tensor(f"gla2_{s}", shape, F32))

            def ps(s):
                return inner.enter_context(nc.psum_tensor(f"gla2_{s}", [P, COL], F32))

            spread, raised, keys, att_ready, masked, turned, copied, state_ready, updated, out_ready, out_taken, step = (
                sem(s) for s in ("spread", "raised", "keys", "att_ready", "masked", "turned", "copied", "state_ready",
                                 "updated", "out_ready", "out_taken", "step"))
            ksub = isb("ksub", [P, 2, NSUB, P])
            att = isb("att", [P, C_HEADS, P])
            kt = isb("kt", [P, P])
            att_bank, kt_bank, u_bank, o_bank = ps("att_bank"), ps("kt_bank"), ps("u_bank"), ps("o_bank")
            block = inner.enter_context(nc.Block())
            cv = 1536

            @block.scalar
            def _(act):
                for t in range(NT):
                    act.wait_ge(spread, t + 1)
                    nc.scalar.activation(ksub[:, t % 2], ksub[:, t % 2], ACT.Exp, scale=-1.0).then_inc(raised, 1)

            @block.vector
            def _(dve):
                chain = Chain(dve, step)

                def spread_tile(t):
                    if t >= 2:
                        dve.wait_ge(att_ready, t - 1)
                    bt = b[:, t * P:(t + 1) * P]
                    ref = bt.rearrange("p (n s) -> p n s", s=SUB)[:, :, SUB // 2:SUB // 2 + 1].to_broadcast([P, NSUB, P])
                    chain(nc.vector.tensor_tensor(ksub[:, t % 2], bt.unsqueeze(1).to_broadcast([P, NSUB, P]), ref, ALU.subtract))
                    nc.vector.tensor_scalar(ksub[:, t % 2], ksub[:, t % 2], -DECAY_CLAMP, None, ALU.max).then_inc(spread, 1)

                spread_tile(0)
                for t in range(NT):
                    if t + 1 < NT:
                        spread_tile(t + 1)
                    dve.wait_ge(raised, t + 1)
                    nc.vector.tensor_tensor(ksub[:, t % 2], ksub[:, t % 2],
                                            fm[:, 1, t * P:(t + 1) * P].unsqueeze(1).to_broadcast([P, NSUB, P]),
                                            ALU.mult).then_inc(keys, 1)
                    dve.wait_ge(att_ready, t + 1)
                    if t >= 1:
                        dve.wait_ge(out_ready, t)
                    for h in range(C_HEADS):
                        last = nc.vector.tensor_tensor(
                            att[:, h, :].rearrange("p (n s) -> p n s", s=SUB),
                            att_bank[:].rearrange("p (n h s) -> p n h s", h=C_HEADS, s=SUB)[:, :, h, :],
                            k.upper_incl[:].rearrange("p (n s) -> p n s", s=SUB), ALU.mult)
                        if h < C_HEADS - 1:
                            chain(last)
                    last.then_inc(masked, 1)
                    dve.wait_ge(turned, t + 1)
                    if t >= 1:
                        dve.wait_ge(state_ready, t)
                    nc.vector.tensor_copy(kt[:], kt_bank[:, 0:P]).then_inc(copied, 1)
                    dve.wait_ge(out_ready, t + 1)
                    nc.vector.tensor_copy(tok[:, t, OUT_C:OUT_C + 256], o_bank[:, 0:256]).then_inc(out_taken, 1)
                    dve.wait_ge(state_ready, t + 1)
                    for h in range(C_HEADS):
                        r, e = slice(h * C_DK, (h + 1) * C_DK), slice(h * C_DV, (h + 1) * C_DV)
                        last = nc.vector.scalar_tensor_tensor(k.gla_state[r, e], k.gla_state[r, e], k.gla_tile_decay[r, t:t + 1],
                                                              u_bank[r, e], ALU.mult, ALU.add)
                        if h < C_HEADS - 1:
                            chain(last)
                    last.then_inc(updated, 1)

            @block.tensor
            def _(pe):
                for t in range(NT):
                    c = slice(t * P, (t + 1) * P)
                    pe.wait_ge(keys, t + 1)
                    if t >= 1:
                        pe.wait_ge(masked, t)
                    for i in range(NSUB):
                        mm = nc.tensor.matmul(att_bank[:, i * 64:(i + 1) * 64], ksub[:, t % 2, i, :],
                                              qsub[:, t * NSUB + i].rearrange("p h s -> p (h s)"), start=True, stop=True)
                    mm.then_inc(att_ready, 1)
                    if t >= 1:
                        pe.wait_ge(copied, t)
                    nc.tensor.transpose(kt_bank[:, 0:P], kout[:, c], k.ident[:]).then_inc(turned, 1)
                    if t >= 1:
                        pe.wait_ge(updated, t)
                        pe.wait_ge(out_taken, t)
                    nc.tensor.matmul(o_bank[:, 0:256], qin[:, c], k.gla_state[:], start=True, stop=True)
                    pe.wait_ge(masked, t + 1)
                    for h in range(C_HEADS):
                        mm = nc.tensor.matmul(o_bank[:, h * 64:(h + 1) * 64], att[:, h, :], tok[:, t, cv + h * 64:cv + (h + 1) * 64],
                                              start=False, stop=True, skip_group_check=True)
                    mm.then_inc(out_ready, 1)
                    pe.wait_ge(copied, t + 1)
                    nc.tensor.matmul(u_bank[:, 0:256], kt[:], tok[:, t, cv:cv + 256], start=True, stop=True).then_inc(state_ready, 1)


def gla_gate_stage(k, tok):
    nc = k.nc
    with ExitStack() as ctx:
        opened = nc.alloc_semaphore("gla_opened")
        scaled = nc.alloc_semaphore("gla_scaled")
        r = ctx.enter_context(nc.sbuf_tensor("gla_silu", [P, NT, 256], F32))
        block = ctx.enter_context(nc.Block())

        @block.scalar
        def _(act):
            nc.scalar.activation(r[:], tok[:, :, CR:CR + 256], ACT.Silu).then_inc(opened, 1)

        @block.vector
        def _(dve):
            dve.wait_ge(opened, 1)
            nc.vector.tensor_tensor(tok[:, :, OUT_C:OUT_C + 256], tok[:, :, OUT_C:OUT_C + 256], r[:], ALU.mult).then_inc(scaled, 1)


def lru_stages(k, dxg):
    nc = k.nc
    with ExitStack() as ctx:
        def sb(s, shape):
            return ctx.enter_context(nc.sbuf_tensor(f"lru_{s}", shape, F32))

        xc, gates = sb("xc", [P, 2, S]), sb("gates", [P, 2, 2, S])
        with ExitStack() as inner:
            step = nc.alloc_semaphore("lru_step")
            block = inner.enter_context(nc.Block())

            @block.vector
            def _(dve):
                chain = Chain(dve, step)
                for j in range(2):
                    chain(nc.vector.tensor_scalar(xc[:, j, :], dxg[:, j, :], k.conv_w[:, CONV_W - 1, j:j + 1],
                                                  k.conv_b[:, j:j + 1], ALU.mult, ALU.add))
                    for back in range(1, CONV_W):
                        chain(nc.vector.scalar_tensor_tensor(xc[:, j, back:], dxg[:, j, :S - back],
                                                             k.conv_w[:, CONV_W - 1 - back, j:j + 1], xc[:, j, back:],
                                                             ALU.mult, ALU.add))
        jobs = [Job([(k.lru_w[:, g, j, :], xc[:, j, :])], P, S, copy_to(k, gates[:, g, j, :], bias=k.lru_b[:, g, j:j + 1]),
                    "dve") for g in range(2) for j in range(2)]
        gemm_stage(k, "lru_gates", jobs)
        with ExitStack() as inner:
            def sem(s):
                return nc.alloc_semaphore(f"lru_{s}")

            def isb(s, shape):
                return inner.enter_context(nc.sbuf_tensor(f"lru2_{s}", shape, F32))

            astep, step, opened, decayed, ready = sem("astep"), sem("step2"), sem("opened"), sem("decayed"), sem("ready")
            la, th, root = isb("la", [P, 2, S]), isb("th", [P, 2, S]), isb("root", [P, 2, S])
            lam = isb("lam", [P, 2])
            den = isb("den", [P, 2, S])
            block = inner.enter_context(nc.Block())

            @block.scalar
            def _(act):
                chain = Chain(act, astep)
                chain(nc.scalar.activation(lam[:], k.lru_lam[:], ACT.Abs))
                chain(nc.scalar.activation(lam[:], lam[:], ACT.Exp, scale=-1.0))
                nc.scalar.activation(lam[:], lam[:], ACT.Ln, bias=k.ones[:, 0:1]).then_inc(opened, 1)
                nc.scalar.activation(gates[:], gates[:], ACT.Sigmoid).then_inc(opened, 1)
                nc.scalar.activation(dxg[:, 2:4, :], dxg[:, 2:4, :], ACT.Gelu_apprx_tanh).then_inc(opened, 1)
                act.wait_ge(ready, 1)
                nc.scalar.activation(th[:], la[:], ACT.Tanh, scale=-1.0).then_inc(decayed, 1)
                nc.scalar.activation(la[:], la[:], ACT.Exp).then_inc(decayed, 1)
                act.wait_ge(ready, 2)
                nc.scalar.activation(root[:], th[:], ACT.Sqrt).then_inc(decayed, 1)

            @block.vector
            def _(dve):
                chain = Chain(dve, step)
                dve.wait_ge(opened, 3)
                chain(nc.vector.scalar_tensor_tensor(lam[:], k.lru_lam[:], 0.0, lam[:], ALU.min, ALU.subtract))
                chain(nc.vector.tensor_scalar(lam[:], lam[:], 8.0, None, ALU.mult))
                for j in range(2):
                    last = nc.vector.tensor_scalar(la[:, j, :], gates[:, 0, j, :], lam[:, j:j + 1], None, ALU.mult)
                    if j == 0:
                        chain(last)
                last.then_inc(ready, 1)
                dve.wait_ge(decayed, 1)
                chain(nc.vector.tensor_scalar(den[:], th[:], 1.0, None, ALU.add))
                chain(nc.vector.reciprocal(den[:], den[:]))
                nc.vector.scalar_tensor_tensor(th[:], th[:], 2.0, den[:], ALU.mult, ALU.mult).then_inc(ready, 1)
                chain(nc.vector.tensor_tensor(xc[:], xc[:], gates[:, 1], ALU.mult))
                dve.wait_ge(decayed, 3)
                chain(nc.vector.tensor_tensor(xc[:], xc[:], root[:], ALU.mult))
                for j in range(2):
                    chain(nc.vector.tensor_tensor_scan(den[:, j, :], la[:, j, :], xc[:, j, :], 0.0, ALU.mult, ALU.add))
                chain(nc.vector.tensor_tensor(k.hT[:, 6:8, :], den[:], dxg[:, 2:4, :], ALU.mult))


def residual(k, t, n, gate=None):
    nc = k.nc
    cols = slice(n * COL, (n + 1) * COL)

    def evac(e, chain, psum):
        if gate is None:
            return nc.vector.tensor_tensor(k.x[:, t, cols], k.x[:, t, cols], psum, ALU.add)
        chain(nc.vector.tensor_tensor(k.gated[:], psum, gate[:, cols], ALU.mult))
        return nc.vector.tensor_tensor(k.x[:, t, cols], k.x[:, t, cols], k.gated[:], ALU.add)
    return evac


def out_stage(k, name, keys, gate=None):
    jobs = []
    for n, key in enumerate(keys):
        (w,) = chunk_view(k, key)
        for t in range(NT):
            mm = [(k.hT[:, j, t * P:(t + 1) * P], w[:, j, :]) for j in range(ND)]
            jobs.append(Job(mm, P, COL, residual(k, t, n, gate), "dve", key))
    gemm_stage(k, name, jobs, last_key=keys[-1])


def part1(k, a):
    nc = k.nc
    condition_stage(k, a)
    with nc.sbuf_tensor("xn1", [P, NT, D], F32) as xn:
        norm_turn_stage(k, "norm1", [(k.x, xn, k.scale1, k.shift1)], k.hT)
    with ExitStack() as ctx:
        tok = ctx.enter_context(nc.sbuf_tensor("tok1", [P, NT, 2048], F32))
        fm = ctx.enter_context(nc.sbuf_tensor("fm1", [P, 2, S], F32))
        glow = ctx.enter_context(nc.sbuf_tensor("glow1", [P, S], F32))
        dxg = ctx.enter_context(nc.sbuf_tensor("dxg1", [P, 4, S], F32))
        project1_stage(k, tok, fm, glow, dxg)
        lru_stages(k, dxg)
        with nc.sbuf_tensor("qk1", [P, 8, S], F32) as qk:
            groups = []
            for t in range(NT):
                def heads(c0, w):
                    return tok[:, t, c0:c0 + 256].rearrange("p (n w) -> p n w", w=w)
                groups += [(heads(0, A_DK), heads(0, A_DK), A_DK, k.a_q_gain[:]),
                           (heads(256, A_DK), heads(256, A_DK), A_DK, k.a_k_gain[:]),
                           (heads(768, B_DK), heads(768, B_DK), B_DK, k.b_q_gain[:]),
                           (heads(1024, B_DK), heads(1024, B_DK), B_DK, k.b_k_gain[:])]
            rms_stage(k, "qk_norm", groups)
            lambda_stage(k)
            transpose_stage(k, "turn_qk", [(columns_of(tok, c0, P), qk[:, j, :], None, None)
                                           for j, c0 in enumerate((0, 128, 256, 384, 768, 896, 1024, 1152))])

            def diff_step(h, i):
                r = [slice(64 * (h % 2) + 32 * m, 64 * (h % 2) + 32 * m + 32) for m in range(2)]

                def out(chain, psum, inv, m):
                    return nc.vector.tensor_copy(tok[:, i, OUT_A + h * 64:OUT_A + (h + 1) * 64], psum)
                return Step(i=i, q=[qk[r[m], h // 2, i * P:(i + 1) * P] for m in range(2)],
                                       k=[qk[r[m], 2 + h // 2, :] for m in range(2)],
                                       v=lambda m, j: tok[:, j, 512 + h * 64:512 + (h + 1) * 64], out=out)

            def moba_step(g, i):
                r = [slice(64 * m, 64 * m + 64) for m in range(2)]

                def out(chain, psum, inv, m):
                    h = 2 * g + m
                    return nc.vector.tensor_scalar(tok[:, i, OUT_B + h * 64:OUT_B + (h + 1) * 64], psum, inv, None, ALU.mult)
                return Step(i=i, q=[qk[r[m], 4 + g, i * P:(i + 1) * P] for m in range(2)],
                                       k=[qk[r[m], 6 + g, :] for m in range(2)],
                                       v=lambda m, j: tok[:, j, 1280 + (2 * g + m) * 64:1280 + (2 * g + m + 1) * 64], out=out)

            attention_stage(k, "diff", [diff_step(h, i) for h in range(A_HEADS) for i in range(NT)], A_DK ** -0.5, True, k.lam[:])
            attention_stage(k, "moba", [moba_step(g, i) for g in range(2) for i in range(NT)], B_DK ** -0.5, False)
        gla_stages(k, tok, fm, glow, a)
        gla_finish = []
        for t in range(NT):
            o = tok[:, t, OUT_A:OUT_A + 256].rearrange("p (n w) -> p n w", w=A_DV)
            gla_finish.append((o, o, A_DV, k.a_out_gain[:]))
        for t in range(NT):
            o = tok[:, t, OUT_C:OUT_C + 256].rearrange("p (n w) -> p n w", w=C_DV)
            gla_finish.append((o, o, C_DV, k.c_out_gain[:]))
        rms_stage(k, "head_norm", gla_finish)
        gla_gate_stage(k, tok)
        transpose_stage(k, "turn_mix", [(columns_of(tok, c0 + j * P, P), k.hT[:, 2 * g + j, :],
                                         1.0 - LAM_INIT if g == 0 else None, None)
                                        for g, c0 in enumerate((OUT_A, OUT_B, OUT_C)) for j in range(2)])
    out_stage(k, "out1", [("out1", n) for n in range(2)], k.mod[:, 0, :])




def second_norm_stages(k, h2_dram):
    nc = k.nc
    with nc.sbuf_tensor("h2", [P, NT, D], F32) as h2:
        rms_stage(k, "norm2", row_norm_groups(k.x, h2))
        with ExitStack() as ctx:
            step = nc.alloc_semaphore("h2_step")
            tile_ready = nc.alloc_semaphore("h2_tile_ready")
            stored = nc.alloc_semaphore("h2_stored")
            block = ctx.enter_context(nc.Block())

            @block.vector
            def _(dve):
                chain = Chain(dve, step)
                for t in range(NT):
                    chain(nc.vector.tensor_tensor(h2[:, t, :], h2[:, t, :], k.mod[:, 2, :], ALU.mult))
                    nc.vector.tensor_tensor(h2[:, t, :], h2[:, t, :], k.mod[:, 1, :], ALU.add).then_inc(tile_ready, 1)

            @block.sync
            def _(sp):
                for t in range(NT):
                    sp.wait_ge(tile_ready, t + 1)
                    sp.dma_start(h2_dram[t * P:(t + 1) * P, :], h2[:, t, :]).then_inc(stored, 16)
                sp.wait_ge(stored, 16 * NT)
        transpose_stage(k, "turn2", [(columns_of(h2, j * P, P), k.hT[:, j, :], None, None) for j in range(ND)])


def route_stages(k, a):
    nc = k.nc
    with ExitStack() as ctx:
        def sb(s, shape, dt=F32):
            return ctx.enter_context(nc.sbuf_tensor(f"route_{s}", shape, dt))

        def sem(s):
            return nc.alloc_semaphore(f"route_{s}")

        def ps(s, n=COL):
            return ctx.enter_context(nc.psum_tensor(f"route_{s}", [P, n], F32))

        logits = sb("logits", [P, NT, NE])
        best, best_id = sb("best", [P, NT, 8]), sb("best_id", [P, NT, 8], U32)
        ids = sb("ids", [P, NT, TOPK])
        e, total = sb("e", [P, NT, TOPK]), sb("total", [P, NT])
        hot = sb("hot", [P, NT, TOPK, NE])
        mask = sb("mask", [P, NT, NE])
        count, blocks, ends, start = sb("count", [P, NE]), sb("blocks", [P, NE]), sb("ends", [P, NE]), sb("start", [P, NE])
        place = sb("place", [P, NT, NE])
        prod = sb("prod", [P, NT, TOPK, NE])
        dest, dest_i = sb("dest", [P, NT, TOPK]), sb("dest_i", [P, NT * TOPK], I32)
        number, spare, number_i = sb("number", [P, MAXB + 1]), sb("spare", [P, MAXB + 1]), sb("number_i", [P, MAXB + 1], I32)
        row_i, blk_i = sb("row_i", [P, NT * TOPK], I32), sb("blk_i", [P, NT * TOPK], I32)
        row_f, blk_f = sb("row_f", [P, NT * TOPK]), sb("blk_f", [P, NT * TOPK])
        row_hot, blk_hot = sb("row_hot", [P, NT * TOPK, P]), sb("blk_hot", [P, NT * TOPK, MAXB + 1])
        step, logits_ready, masked, ranked, scaled, raised, rows_ready, lists_ready = (
            sem(s) for s in ("step", "logits", "masked", "ranked", "scaled", "raised", "rows", "lists"))
        l_bank, r_bank, c_bank, t_bank = ps("l_bank"), ps("r_bank"), ps("c_bank"), ps("t_bank")
        block = ctx.enter_context(nc.Block())

        @block.sync
        def _(sp):
            for c in range(CHUNKS):
                sp.dma_start(k.expert_chunk(c, 0), expert_source(a, 0, c)).then_inc(k.expert_loaded[c], 16)

        @block.tensor
        def _(pe):
            for t in range(NT):
                out = l_bank[:, t * NE:(t + 1) * NE]
                for j in range(ND):
                    nc.tensor.matmul(out, k.hT[:, j, t * P:(t + 1) * P], k.router_w[:, j, :], start=(j == 0), stop=False)
                mm = nc.tensor.matmul(out, k.ones[0:1, :], k.router_b[0:1, :], start=False, stop=True)
            mm.then_inc(logits_ready, 1)
            pe.wait_ge(masked, 1)
            for t in range(NT):
                for s in range(t + 1):
                    nc.tensor.matmul(r_bank[:, t * NE:(t + 1) * NE], k.upper_strict[:] if s == t else k.ones[:], mask[:, s, :],
                                     start=(s == 0), stop=(s == t))
            for s in range(NT):
                mm = nc.tensor.matmul(c_bank[:, 0:NE], k.ones[:], mask[:, s, :], start=(s == 0), stop=(s == NT - 1))
            mm.then_inc(ranked, 1)
            pe.wait_ge(rows_ready, 1)
            for n in range(NT * TOPK):
                mm = nc.tensor.matmul(t_bank[:, 0:MAXB + 1], row_hot[:, n, :], blk_hot[:, n, :], start=(n == 0), stop=(n == NT * TOPK - 1))
            mm.then_inc(lists_ready, 1)

        @block.scalar
        def _(act):
            act.wait_ge(scaled, 1)
            nc.scalar.activation(e[:], e[:], ACT.Exp).then_inc(raised, 1)

        @block.vector
        def _(dve):
            chain = Chain(dve, step)
            dve.wait_ge(logits_ready, 1)
            chain(nc.vector.tensor_copy(logits[:], l_bank[:, 0:NT * NE].rearrange("p (t e) -> p t e", e=NE)))
            for t in range(NT):
                chain(nc.vector.max(best[:, t, :], logits[:, t, :]))
                chain(nc.vector.max_index(best_id[:, t, :], best[:, t, :], logits[:, t, :]))
            nc.vector.tensor_tensor(e[:], best[:, :, 0:TOPK], best[:, :, 0:1].to_broadcast([P, NT, TOPK]), ALU.subtract).then_inc(scaled, 1)
            chain(nc.vector.tensor_copy(ids[:], best_id[:, :, 0:TOPK]))
            for t in range(NT):
                chain(nc.vector.tensor_tensor(hot[:, t], k.iota[:, 0:NE].unsqueeze(1).to_broadcast([P, TOPK, NE]),
                                              ids[:, t, :].unsqueeze(2).to_broadcast([P, TOPK, NE]), ALU.is_equal))
            nc.vector.tensor_reduce(mask[:], hot[:].rearrange("p t k e -> p t e k"), X, ALU.add).then_inc(masked, 1)
            dve.wait_ge(raised, 1)
            chain(nc.vector.tensor_reduce(total[:], e[:], X, ALU.add))
            chain(nc.vector.reciprocal(total[:], total[:]))
            chain(nc.vector.tensor_tensor(k.gates[:], e[:], total[:].unsqueeze(2).to_broadcast([P, NT, TOPK]), ALU.mult))
            dve.wait_ge(ranked, 1)
            chain(nc.vector.tensor_copy(count[:], c_bank[:, 0:NE]))
            chain(nc.vector.tensor_scalar(blocks[:], count[:], 0.0, None, ALU.is_gt))
            for n in range(1, S // BR):
                chain(nc.vector.scalar_tensor_tensor(blocks[:], count[:], float(n * BR), blocks[:], ALU.is_gt, ALU.add))
            chain(nc.vector.tensor_tensor_scan(ends[:], k.ones[:, 0:NE], blocks[:], 0.0, ALU.mult, ALU.add))
            chain(nc.vector.tensor_tensor(start[:], ends[:], blocks[:], ALU.subtract))
            chain(nc.vector.tensor_copy(k.first[:, 0:NE], start[0:1, :]))
            chain(nc.vector.tensor_copy(k.first[:, NE:], ends[0:1, NE - 1:]))
            chain(nc.vector.tensor_scalar(start[:], start[:], float(BR), None, ALU.mult))
            chain(nc.vector.tensor_tensor(place[:], r_bank[:, 0:NT * NE].rearrange("p (t e) -> p t e", e=NE),
                                          start[:].unsqueeze(1).to_broadcast([P, NT, NE]), ALU.add))
            for t in range(NT):
                chain(nc.vector.tensor_tensor(prod[:, t], hot[:, t], place[:, t, :].unsqueeze(1).to_broadcast([P, TOPK, NE]), ALU.mult))
            chain(nc.vector.tensor_reduce(dest[:], prod[:], X, ALU.add))
            chain(nc.vector.tensor_copy(dest_i[:], dest[:].rearrange("p t k -> p (t k)")))
            chain(nc.vector.tensor_single_scalar(row_i[:], dest_i[:], BR - 1, ALU.bitwise_and))
            chain(nc.vector.tensor_single_scalar(blk_i[:], dest_i[:], int(math.log2(BR)), ALU.arith_shift_right))
            chain(nc.vector.tensor_copy(row_f[:], row_i[:]))
            chain(nc.vector.tensor_copy(blk_f[:], blk_i[:]))
            for n in range(NT * TOPK):
                chain(nc.vector.tensor_scalar(row_hot[:, n, :], k.row_no[:], row_f[:, n:n + 1], None, ALU.is_equal))
                last = nc.vector.tensor_scalar(blk_hot[:, n, :], k.iota[:, 0:MAXB + 1], blk_f[:, n:n + 1], k.place_no[:, n:n + 1],
                                               ALU.is_equal, ALU.mult)
                if n < NT * TOPK - 1:
                    chain(last)
            last.then_inc(rows_ready, 1)
            dve.wait_ge(lists_ready, 1)
            chain(nc.vector.tensor_copy(number[:], t_bank[:, 0:MAXB + 1]))
            chain(nc.vector.tensor_scalar(spare[:], number[:], 0.0, k.spare_no[:], ALU.is_equal, ALU.mult))
            chain(nc.vector.scalar_tensor_tensor(spare[:], spare[:], -1.0, number[:], ALU.add, ALU.add))
            chain(nc.vector.tensor_scalar(spare[:], spare[:], 2.0, k.half_no[:], ALU.mult, ALU.add))
            chain(nc.vector.tensor_copy(k.row_place[:], spare[:]))
            chain(nc.vector.tensor_scalar(number[:], number[:], -1.0, 0.0, ALU.add, ALU.max))
            chain(nc.vector.tensor_copy(number_i[:], number[:]))
            chain(nc.vector.tensor_single_scalar(number_i[:], number_i[:], 2, ALU.arith_shift_right))
            chain(nc.vector.tensor_copy(number[:], number_i[:]))
            chain(nc.vector.tensor_scalar(number[:], number[:], 2.0, k.half_no[:], ALU.mult, ALU.add))
            chain(nc.vector.tensor_copy(k.row_token[:], number[:]))


CHUNKS = 6
TWICE = 2


def expert_source(a, e, c):
    if c < 4:
        col = (c % 2) * FF + (c // 2) * COL
        src = a["exp_w_up"][0].rearrange("e (k p) n -> e p k n", p=P)[bass.ds(e, 1), :, :, col:col + COL]
    else:
        src = a["exp_w_down"][0].rearrange("e (k p) n -> e p k n", p=P)[bass.ds(e, 1), :, 4 * (c - 4):4 * (c - 3), :]
    return src.rearrange("e p k n -> (e p) k n")


def expert_stage(k, a, h2_dram, y_dram):
    nc = k.nc
    halves = [slice(BR * h, BR * h + BR) for h in range(2)]
    with ExitStack() as ctx:
        def sem(s):
            return nc.alloc_semaphore(f"moe_{s}")

        def sb(s, shape, dt=F32):
            return ctx.enter_context(nc.sbuf_tensor(f"moe_{s}", shape, dt))

        def ps(s):
            return ctx.enter_context(nc.psum_tensor(f"moe_{s}", [P, COL], F32))

        k.expert_w2 = sb("w2", [P, TWICE * SLOT])
        chunk = [[k.expert_chunk(c, u) for c in range(CHUNKS)] for u in range(2)]
        loaded = k.expert_loaded
        rows, y = k.hT[:, 0, :], k.hT[:, 1, :]
        rowsT, hidT = (k.hT[:, n, :].rearrange("p (j r) -> p j r", r=P) for n in (2, 3))
        gate, lin, sig, hid = (k.hT[:, n, :].rearrange("p (h n) -> p h n", n=UNITS) for n in range(4, 8))
        index, place = sb("index", [P, 1], U32), sb("place", [P, 1], U32)
        used_mod = k.mod[:, 0:3, :].rearrange("p n d -> p (n d)")
        bias, bias_row = sb("bias", [P, 3 * COL]), [used_mod[0:1, h * 3 * COL:(h + 1) * 3 * COL] for h in range(2)]
        bias_loaded, bias_spread, indexed, waited = (sem(s) for s in ("bias_loaded", "bias_spread", "indexed", "waited"))
        chunk_free = sem("chunk_free")
        gathered, y_stored = k.gathered, k.y_stored
        rows_turned, rows_taken = sem("rows_turned"), sem("rows_taken")
        chunk_done, gate_ready, sig_ready, hid_ready, up_taken = sem("chunk_done"), sem("gate"), sem("sig"), sem("hid"), sem("up_taken")
        hid_turned, hid_taken = sem("hid_turned"), sem("hid_taken")
        y_ready, y_free, step = sem("y_ready"), sem("y_free"), sem("step")
        up = [ps(f"up{c}") for c in range(4)]
        down = ps("down")
        turn_r, turn_h = ps("turn_rows"), [ps(f"turn_hid{c}") for c in range(2)]
        block = ctx.enter_context(nc.Block())
        b_up = a["exp_b_up"][0].rearrange("e (s h n) -> e s h n", h=2, n=UNITS)
        b_down = a["exp_b_down"][0]
        h2_halves = h2_dram.rearrange("s (h n) -> (s h) n", h=2)
        y_halves = y_dram.rearrange("s (h n) -> (s h) n", h=2)

        def first_block(eng, e):
            return eng.value_load(k.first[0:1, bass.ds(e, 1)], min_val=0, max_val=MAXB)

        @block.sync
        def _(sp):
            def load_bias(e):
                for h in range(2):
                    sp.dma_start(bias_row[h][:, 0:2 * COL].rearrange("p (s n) -> p s n", n=UNITS), b_up[bass.ds(e, 1), :, h, :]).then_inc(bias_loaded, 16)
                    sp.dma_start(bias_row[h][:, 2 * COL:], b_down[bass.ds(e, 1), h * COL:(h + 1) * COL]).then_inc(bias_loaded, 16)

            def load(e, u):
                sp.wait_ge(bias_spread, e * 2)
                load_bias(e)
                last_but_one, last = first_block(sp, e - 1), first_block(sp, e)
                for c in range(CHUNKS):
                    sp.wait_ge(chunk_done, (last_but_one if c < TWICE else last) * CHUNKS + (c + 1))
                    sp.sem_inc(chunk_free, 1)
                    sp.wait_ge(loaded[(c - 2) % CHUNKS], e * 16 + (16 if c >= 2 else 0))
                    sp.dma_start(k.expert_chunk(c, u), expert_source(a, e, c)).then_inc(loaded[c], 16)

            load_bias(0)
            with sp.Fori(0, NE // 2 - 1) as i:
                load(i * 2 + 1, 1)
                load(i * 2 + 2, 0)
            load(NE - 1, 1)

        @block.gpsimd
        def _(pool):
            def gather(b, copies):
                nc.gpsimd.tensor_copy(index[:], k.row_token[:, bass.ds(b, 1)]).then_inc(indexed, 1)
                pool.wait_ge(indexed, copies)
                pool.sem_inc(waited, 1)
                pool.indirect_dma_start(rows, None, h2_halves,
                                        bass.IndirectOffsetOnAxis(ap=index[:], axis=0)).then_inc(gathered, 16)

            def scatter(b, copies, made):
                nc.gpsimd.tensor_copy(place[:], k.row_place[:, bass.ds(b, 1)]).then_inc(indexed, 1)
                pool.wait_ge(indexed, copies)
                pool.wait_ge(y_ready, made)
                pool.sem_inc(waited, 1)
                pool.indirect_dma_start(y_halves, bass.IndirectOffsetOnAxis(ap=place[:], axis=0), y, None).then_inc(y_stored, 16)

            gather(0, 1)
            scatter(MAXB, 2, 1)
            with pool.Fori(0, NE) as e:
                pool.wait_ge(bias_loaded, e * 64 + 64)
                pool.wait_ge(y_ready, first_block(pool, e) + 1)
                pool.sem_inc(waited, 1)
                nc.gpsimd.partition_broadcast(bias[:], bias_row[1]).then_inc(bias_spread, 1)
                pool.wait_ge(bias_spread, e * 2 + 1)
                pool.sem_inc(waited, 1)
                nc.gpsimd.partition_broadcast(bias[0:BR, :], bias_row[0], channels=BR).then_inc(bias_spread, 1)
                with pool.Fori(first_block(pool, e), first_block(pool, e + 1)) as b:
                    pool.wait_ge(rows_turned, b + 1)
                    gather(b + 1, b * 2 + 3)
                    pool.wait_ge(y_stored, b * 16 + 16)
                    pool.sem_inc(y_free, 1)
                    scatter(b, b * 2 + 4, b + 2)
            blocks = first_block(pool, NE)
            pool.wait_ge(gathered, blocks * 16 + 16)
            pool.sem_inc(waited, 1)
            pool.wait_ge(y_stored, blocks * 16 + 16)
            pool.sem_inc(waited, 1)

        @block.tensor
        def _(pe):
            def turn_rows():
                for j in range(4):
                    tr = nc.tensor.transpose(turn_r[:, j * P:(j + 1) * P], rows[:, j * P:(j + 1) * P], k.ident[:])
                tr.then_inc(rows_turned, 1)

            def up_chunk(e, u, b, c):
                pe.wait_ge(loaded[c], e * 16 + 16)
                pe.wait_ge(up_taken, b * 4 + (c + 1))
                for j in range(ND):
                    for h in range(2):
                        mm = nc.tensor.matmul(up[c][halves[h], 0:UNITS], rowsT[:, j % 4, halves[j // 4]],
                                              chunk[u][c][:, j, h * UNITS:(h + 1) * UNITS], start=(j == 0), stop=(j == ND - 1))
                mm.then_inc(chunk_done, 1)

            def turn_hidden(b, half):
                pe.wait_ge(hid_ready, b * 2 + (half + 1))
                pe.wait_ge(hid_taken, b * 2 + (half + 1))
                for j in range(2):
                    tr = nc.tensor.transpose(turn_h[half][:, j * P:(j + 1) * P], hid[:, half, j * P:(j + 1) * P], k.ident[:])
                tr.then_inc(hid_turned, 1)

            def down_half(e, u, b, half):
                pe.wait_ge(hid_taken, b * 2 + (half + 3))
                if half == 0:
                    pe.wait_ge(y_ready, b + 1)
                pe.wait_ge(loaded[4 + half], e * 16 + 16)
                for j in range(4):
                    for h in range(2):
                        mm = nc.tensor.matmul(down[halves[h], :], hidT[:, 2 * half + j % 2, halves[j // 2]], chunk[u][4 + half][:, j, h * COL:(h + 1) * COL],
                                              start=(half == 0 and j == 0), stop=(half == 1 and j == 3))
                mm.then_inc(chunk_done, 1)

            pe.nop().then_inc(chunk_done, CHUNKS)
            pe.wait_ge(gathered, 16)
            turn_rows()
            with pe.Fori(0, NE // 2) as i:
                for u in range(2):
                    e = i * 2 + u
                    with pe.Fori(first_block(pe, e), first_block(pe, e + 1)) as b:
                        pe.wait_ge(rows_taken, b + 1)
                        for c in range(3):
                            up_chunk(e, u, b, c)
                        turn_hidden(b, 0)
                        up_chunk(e, u, b, 3)
                        down_half(e, u, b, 0)
                        pe.wait_ge(gathered, b * 16 + 32)
                        turn_rows()
                        turn_hidden(b, 1)
                        down_half(e, u, b, 1)

        @block.scalar
        def _(act):
            def take_rows():
                nc.scalar.activation(rowsT, turn_r[:].rearrange("p (j r) -> p j r", r=P), ACT.Copy).then_inc(rows_taken, 1)

            act.nop().then_inc(hid_taken, 2)
            act.wait_ge(rows_turned, 1)
            take_rows()
            with act.Fori(0, NE) as e:
                with act.Fori(first_block(act, e), first_block(act, e + 1)) as b:
                    for half in range(2):
                        act.wait_ge(gate_ready, b * 2 + (half + 1))
                        nc.scalar.activation(sig[:, half], gate[:, half], ACT.Sigmoid, scale=ALPHA).then_inc(sig_ready, 1)
                    for half in range(2):
                        if half == 1:
                            act.wait_ge(rows_turned, b + 2)
                            take_rows()
                        act.wait_ge(hid_turned, b * 2 + (half + 1))
                        nc.scalar.activation(hidT[:, 2 * half:2 * half + 2, :], turn_h[half][:, 0:2 * P].rearrange("p (j r) -> p j r", r=P),
                                             ACT.Copy).then_inc(hid_taken, 1)

        @block.vector
        def _(dve):
            dve.nop().then_inc(up_taken, 4)
            nc.vector.memset(y, 0.0).then_inc(y_ready, 1)
            with dve.Fori(0, NE) as e:
                dve.wait_ge(bias_spread, e * 2 + 2)
                with dve.Fori(first_block(dve, e), first_block(dve, e + 1)) as b:
                    for half in range(2):
                        g, l = gate[:, half], lin[:, half]
                        dve.wait_ge(chunk_done, b * CHUNKS + (CHUNKS + 2 * half + 1))
                        nc.vector.tensor_tensor(g, up[2 * half][:, 0:UNITS], bias[:, half * UNITS:(half + 1) * UNITS], ALU.add).then_inc(up_taken, 1)
                        dve.wait_ge(up_taken, b * 4 + (2 * half + 5))
                        nc.vector.tensor_scalar(g, g, LIMIT, None, ALU.min).then_inc(gate_ready, 1)
                        dve.wait_ge(chunk_done, b * CHUNKS + (CHUNKS + 2 * half + 2))
                        nc.vector.tensor_tensor(l, up[2 * half + 1][:, 0:UNITS], bias[:, COL + half * UNITS:COL + (half + 1) * UNITS], ALU.add).then_inc(up_taken, 1)
                        dve.wait_ge(up_taken, b * 4 + (2 * half + 6))
                        nc.vector.tensor_scalar(l, l, LIMIT, -LIMIT, ALU.min, ALU.max).then_inc(step, 1)
                        dve.wait_ge(sig_ready, b * 2 + (half + 1))
                        nc.vector.tensor_tensor(g, g, sig[:, half], ALU.mult).then_inc(step, 1)
                        dve.wait_ge(step, b * 4 + (2 * half + 2))
                        nc.vector.scalar_tensor_tensor(hid[:, half], l, 1.0, g, ALU.add, ALU.mult).then_inc(hid_ready, 1)
                    dve.wait_ge(chunk_done, b * CHUNKS + (CHUNKS + 6))
                    dve.wait_ge(y_free, b + 1)
                    nc.vector.tensor_tensor(y, down[:], bias[:, 2 * COL:], ALU.add).then_inc(y_ready, 1)


def combine_stage(k, y_dram):
    nc = k.nc
    with ExitStack() as ctx:
        rows = ctx.enter_context(nc.sbuf_tensor("combine_rows", [P, 2, TOPK, D], F32))
        acc = ctx.enter_context(nc.sbuf_tensor("combine_sum", [P, D], F32))
        loaded = [nc.alloc_semaphore(f"combine_loaded{b}") for b in range(2)]
        summed, gains_loaded = nc.alloc_semaphore("combine_summed"), nc.alloc_semaphore("final_gains_loaded")
        step = nc.alloc_semaphore("combine_step")
        block = ctx.enter_context(nc.Block())

        @block.sync
        def _(sp):
            k.load_end = len(k.plan) - 1
            sp.dma_start(k.gain_row[:], row(k.a["final_norm_2"])).then_inc(gains_loaded, 16)
            load_chunks(k, sp, ("out1", 1))
            for t in range(NT):
                if t >= 2:
                    sp.wait_ge(summed, t - 1)
                sp.dma_start(rows[:, t % 2], y_dram[t * P * TOPK:(t + 1) * P * TOPK, :].rearrange("(p k) d -> p k d", k=TOPK)).then_inc(loaded[t % 2], 16)
            sp.wait_ge(gains_loaded, 16)

        @block.vector
        def _(dve):
            chain = Chain(dve, step)
            for t in range(NT):
                dve.wait_ge(loaded[t % 2], 16 * (t // 2 + 1))
                chain(nc.vector.tensor_scalar(acc[:], rows[:, t % 2, 0, :], k.gates[:, t, 0:1], None, ALU.mult))
                for j in range(1, TOPK):
                    last = nc.vector.scalar_tensor_tensor(acc[:], rows[:, t % 2, j, :], k.gates[:, t, j:j + 1], acc[:], ALU.mult, ALU.add)
                    if j < TOPK - 1:
                        chain(last)
                last.then_inc(summed, 1)
                dve.wait_ge(summed, t + 1)
                chain(nc.vector.tensor_tensor(acc[:], acc[:], k.mod[:, 3, :], ALU.mult))
                chain(nc.vector.tensor_tensor(k.x[:, t, :], k.x[:, t, :], acc[:], ALU.add))




def rope_stage(k, name, spans, cos, sin, groups_w):
    nc = k.nc
    w = groups_w
    with ExitStack() as ctx:
        step = nc.alloc_semaphore(f"{name}_step")
        most = max(s[0].shape[1] for s in spans)
        rot = ctx.enter_context(nc.sbuf_tensor(f"{name}_rot", [P, most, w], F32))
        block = ctx.enter_context(nc.Block())

        @block.vector
        def _(dve):
            chain = Chain(dve, step)
            for n, (view, dst) in enumerate(spans):
                t = n % NT
                heads = view.shape[1]
                c = cos[:, t, :].unsqueeze(1).to_broadcast([P, heads, w])
                s = sin[:, t, :].unsqueeze(1).to_broadcast([P, heads, w])
                r = rot[:, 0:heads, :]
                half = w // 2
                nc.vector.tensor_tensor(r[:, :, 0:half], view[:, :, half:], s[:, :, 0:half], ALU.mult)
                chain(nc.vector.tensor_tensor(r[:, :, half:], view[:, :, 0:half], s[:, :, half:], ALU.mult))
                chain(nc.vector.tensor_tensor(view, view, c, ALU.mult))
                chain(nc.vector.tensor_tensor(dst, by_group(view, dst), by_group(r, dst), ALU.add))


def by_group(view, dst):
    return view if len(dst.shape) == 3 else view.rearrange("p (g r) w -> p r g w", g=G2)


@contextmanager
def cleared_semaphores(nc):
    held = nc.snapshot_sems()
    yield
    nc.clear_and_free_semaphores(nc.allocated_since(held))
    nc.all_engine_barrier()


def in_place(views):
    return [(v, v) for v in views]


KC, VC, KS, VS, KW, VW, GA, CQ, CKV, KR = 512, 640, 768, 896, 1024, 1152, 1280, 1304, 1560, 1688
IN2_W = 1720


def project2_stage(k, l, tok):
    jobs = []
    n = 0
    for c, (c0, c1) in enumerate(IN2):
        w = split_chunk(k, ("in2", l, c))
        for t in range(NT):
            mm = [(k.hT[:, j, t * P:(t + 1) * P], w[:, j, :]) for j in range(ND)]
            jobs.append(Job(mm, P, c1 - c0, copy_to(k, tok[:, t, c0:c1]), engine_of(n), ("in2", l, c)))
            n += 1
    split_gemm_stage(k, f"in2_{l}", jobs, last_key=("in2", l, 3))


def compress_stages(k, l, tok, kcmp, vbd):
    nc = k.nc
    with ExitStack() as ctx:
        def sb(s, shape):
            return ctx.enter_context(nc.sbuf_tensor(f"cmp{l}_{s}", shape, F32))

        pairs = [sb(f"pair_{kv}", [P, G2, S // 2]) for kv in "kv"]
        hid = [sb(f"hid_{kv}", [P, 2, G2 * CPAD]) for kv in "kv"]
        hid4 = sb("hid4", [P, 2, G2, 4, CPAD])
        posb = sb("posb", [P, 2, 2])
        w2k = sb("w2k", [P, 2, 2, DK2])
        w2v = sb("w2v", [P, 2, DK2])
        pos = sb("pos", [P, 2, CB // 2])
        with ExitStack() as inner:
            turned = nc.alloc_semaphore(f"cmp{l}_turned")
            taken = nc.alloc_semaphore(f"cmp{l}_taken")
            w2_loaded = nc.alloc_semaphore(f"cmp{l}_w2_loaded")
            zeroed = nc.alloc_semaphore(f"cmp{l}_zeroed")
            bank = [inner.enter_context(nc.psum_tensor(f"cmp{l}_t{i}", [P, COL], F32)) for i in range(2)]
            block = inner.enter_context(nc.Block())

            @block.sync
            def _(sp):
                for copy in range(2):
                    sp.dma_start(w2k[:, :, copy, :], k.a["cmp_w2_k_2"][l].rearrange("(k p) n -> p k n", p=P)).then_inc(w2_loaded, 16)
                sp.dma_start(w2v[:], k.a["cmp_w2_v_2"][l].rearrange("(k p) n -> p k n", p=P)).then_inc(w2_loaded, 16)
                for i, kv in enumerate("kv"):
                    sp.dma_start(pos[:, i, :], k.a[f"cmp_pos_{kv}_2"][l].rearrange("(u a) d -> (a d) u", a=2),
                                 allow_slow_non_contiguous=True).then_inc(w2_loaded, 16)
                sp.wait_ge(w2_loaded, 16 * 5)

            @block.gpsimd
            def _(pool):
                for i in range(2):
                    nc.gpsimd.memset(hid[i][:], 0.0).then_inc(zeroed, 1)
                nc.gpsimd.memset(vbd[:], 0.0).then_inc(zeroed, 1)

            @block.tensor
            def _(pe):
                for i, c0 in enumerate((KC, VC)):
                    for t in range(NT):
                        tr = nc.tensor.transpose(bank[i][:, t * P:(t + 1) * P], tok[:, t, c0:c0 + P], k.ident[:])
                    tr.then_inc(turned, 1)

            @block.vector
            def _(dve):
                for i in range(2):
                    dve.wait_ge(turned, i + 1)
                    for g in range(G2):
                        for parity in range(2):
                            nc.vector.tensor_copy(pairs[i][64 * parity:64 * parity + 64, g, :],
                                                  bank[i][64 * g:64 * g + 64, :].rearrange("p (n a) -> p n a", a=2)[:, :, parity]).then_inc(taken, 1)
        jobs = []
        for i, kv in enumerate("kv"):
            (w1,) = chunk_view(k, ("cmp", l, kv))
            for m in range(2):
                mm = [(w1[:, u, m * P:(m + 1) * P], pos[:, i, u:u + 1]) for u in range(CB // 2)]
                jobs.append(Job(mm, P, 1, copy_to(k, posb[:, i, m:m + 1]), "act", ("cmp", l, kv)))

                def silu(e, chain, psum, i=i, m=m):
                    return nc.scalar.activation(hid[i][:, m, :].rearrange("p (g n) -> p g n", n=CPAD)[:, :, 0:NCMP],
                                                psum.rearrange("p (g n) -> p g n", n=NCMP), ACT.Silu, bias=posb[:, i, m:m + 1])

                def after_bias(e, chain, psum, f=silu):
                    return f(e, chain, psum)
                mm = [(w1[:, u, m * P:(m + 1) * P], pairs[i][:, :, u:u + 8 * (NCMP - 1) + 1:8]) for u in range(CB // 2)]
                jobs.append(Job(mm, P, G2 * NCMP, after_bias, "act", ("cmp", l, kv)))
        gemm_stage(k, f"cmp1_{l}", jobs, last_key=("cmp", l, "v"))

        with ExitStack() as inner:
            step = nc.alloc_semaphore(f"cmp{l}_spread")
            block = inner.enter_context(nc.Block())

            @block.vector
            def _(dve):
                for m in range(2):
                    for g in range(G2):
                        nc.vector.tensor_copy(hid4[:, m, g], hid[1][:, m, g * CPAD:(g + 1) * CPAD].unsqueeze(1).to_broadcast([P, 4, CPAD])).then_inc(step, 1)

        jobs = []

        def keys(e, chain, psum):
            chain(nc.vector.tensor_copy(kcmp[0:64, :], psum[0:64, 0:CPAD]))
            return nc.vector.tensor_copy(kcmp[64:128, :], psum[64:128, CPAD:2 * CPAD])
        jobs.append(Job([(w2k[:, m].rearrange("p a n -> p (a n)"), hid[0][:, m, :]) for m in range(2)], P, G2 * CPAD, keys, "dve"))
        for g in range(G2):
            def values(e, chain, psum, g=g):
                for r in range(4):
                    last = nc.vector.tensor_copy(vbd[32 * r:32 * r + 32, g, 64 * r:64 * r + 64], psum[32 * r:32 * r + 32, :])
                    if r < 3:
                        chain(last)
                return last
            jobs.append(Job([(hid4[:, m, g].rearrange("p r n -> p (r n)"), w2v[:, m, :]) for m in range(2)], P, DK2, values, "dve"))
        gemm_stage(k, f"cmp2_{l}", jobs)


def compressed_attention_stage(k, l, qT, kcmp, vbd, gates, o):
    nc = k.nc
    scale = DK2 ** -0.5
    with ExitStack() as ctx:
        def sem(s):
            return nc.alloc_semaphore(f"ca{l}_{s}")

        def sb(s, shape):
            return ctx.enter_context(nc.sbuf_tensor(f"ca{l}_{s}", shape, F32))

        scored, shifted, raised, weighed, turned, taken, valued, done, step = (
            sem(s) for s in ("scored", "shifted", "raised", "weighed", "turned", "taken", "valued", "done", "step"))
        s = sb("s", [P, 2, H2, CPAD])
        top, inv = sb("top", [P, H2]), sb("inv", [P, 2, H2])
        pT = sb("pT", [P, 2, G2, P])
        sc = [ctx.enter_context(nc.psum_tensor(f"ca{l}_s{i}", [P, G2, COL], F32)) for i in range(2)]
        tr = [ctx.enter_context(nc.psum_tensor(f"ca{l}_t{i}", [P, COL], F32)) for i in range(2)]
        ov = [ctx.enter_context(nc.psum_tensor(f"ca{l}_o{i}", [P, COL], F32)) for i in range(2)]
        block = ctx.enter_context(nc.Block())

        @block.tensor
        def _(pe):
            def scores(t):
                if t >= 2:
                    pe.wait_ge(shifted, t - 1)
                for g in range(G2):
                    for r in range(R2):
                        mm = nc.tensor.matmul(sc[t % 2][:, g, r * CPAD:(r + 1) * CPAD], qT[64 * g:64 * g + 64, r, t * P:(t + 1) * P],
                                              kcmp[64 * g:64 * g + 64, :], start=True, stop=True)
                mm.then_inc(scored, 1)

            scores(0)
            for t in range(NT):
                if t + 1 < NT:
                    scores(t + 1)
                pe.wait_ge(weighed, t + 1)
                if t >= 2:
                    pe.wait_ge(done, t - 1)
                for g in range(G2):
                    x = nc.tensor.transpose(tr[t % 2][:, g * P:(g + 1) * P], s[:, t % 2, g * R2:(g + 1) * R2, :].rearrange("p r n -> p (r n)"), k.ident[:])
                x.then_inc(turned, 1)
                pe.wait_ge(taken, t + 1)
                for g in range(G2):
                    mm = nc.tensor.matmul(ov[t % 2][:, g * 256:(g + 1) * 256], pT[:, t % 2, g, :], vbd[:, g, :], start=True, stop=True)
                mm.then_inc(valued, 1)

        @block.scalar
        def _(act):
            for t in range(NT):
                act.wait_ge(shifted, t + 1)
                nc.scalar.activation(s[:, t % 2], s[:, t % 2], ACT.Exp).then_inc(raised, 1)
                act.wait_ge(turned, t + 1)
                if t >= 2:
                    act.wait_ge(valued, t - 1)
                nc.scalar.activation(pT[:, t % 2].rearrange("p g n -> p (g n)"), tr[t % 2][:, 0:G2 * P], ACT.Copy).then_inc(taken, 1)

        @block.vector
        def _(dve):
            chain = Chain(dve, step)
            for t in range(NT):
                b = t % 2
                dve.wait_ge(scored, t + 1)
                if t >= 2:
                    dve.wait_ge(turned, t - 1)
                for g in range(G2):
                    chain(nc.vector.scalar_tensor_tensor(
                        s[:, b, g * R2:(g + 1) * R2, :], sc[b][:, g, 0:R2 * CPAD].rearrange("p (r n) -> p r n", n=CPAD), scale,
                        k.cmp_bias[:, t, :].unsqueeze(1).to_broadcast([P, R2, CPAD]), ALU.mult, ALU.add))
                chain(nc.vector.tensor_reduce(top[:], s[:, b], X, ALU.max))
                nc.vector.tensor_tensor(s[:, b], s[:, b], top[:].unsqueeze(2).to_broadcast([P, H2, CPAD]), ALU.subtract).then_inc(shifted, 1)
                dve.wait_ge(raised, t + 1)
                nc.vector.tensor_tensor(s[:, b], s[:, b], k.cmp_mask[:, t, :].unsqueeze(1).to_broadcast([P, H2, CPAD]), ALU.mult).then_inc(weighed, 1)
                dve.wait_ge(weighed, t + 1)
                chain(nc.vector.tensor_reduce(inv[:, b, :], s[:, b], X, ALU.add))
                chain(nc.vector.tensor_scalar(inv[:, b, :], inv[:, b, :], 1e-30, None, ALU.max))
                chain(nc.vector.reciprocal(inv[:, b, :], inv[:, b, :]))
                chain(nc.vector.tensor_tensor(inv[:, b, :], inv[:, b, :], gates[:, t, :, 0], ALU.mult))
                dve.wait_ge(valued, t + 1)
                nc.vector.tensor_tensor(o[:, t, :].rearrange("p (h d) -> p h d", d=DK2), ov[b][:, :].rearrange("p (h d) -> p h d", d=DK2),
                                        inv[:, b, :].unsqueeze(2).to_broadcast([P, H2, DK2]), ALU.mult).then_inc(done, 1)


def nsa_stages(k, l, tok, o):
    nc = k.nc
    with ExitStack() as ctx:
        def sb(s, shape):
            return ctx.enter_context(nc.sbuf_tensor(f"nsa{l}_{s}", shape, F32))

        gates = sb("gates", [P, NT, H2, 3])
        qT = sb("qT", [P, R2, S])
        ksT = sb("ksT", [P, 2, S])
        kcmp, vbd = sb("kcmp", [P, CPAD]), sb("vbd", [P, G2, 256])
        with ExitStack() as inner:
            opened = nc.alloc_semaphore(f"nsa{l}_opened")
            block = inner.enter_context(nc.Block())

            @block.scalar
            def _(act):
                nc.scalar.activation(gates[:].rearrange("p t h n -> p t (h n)"), tok[:, :, GA:GA + 24], ACT.Sigmoid).then_inc(opened, 1)
        with nc.sbuf_tensor(f"nsa{l}_q", [P, NT, R2, G2, DK2], F32) as q:
            spans = [(tok[:, t, 0:512].rearrange("p (n w) -> p n w", w=DK2), q[:, t]) for t in range(NT)]
            for c0 in (KC, KS, KW):
                spans += in_place([tok[:, t, c0:c0 + P].rearrange("p (n w) -> p n w", w=DK2) for t in range(NT)])
            rope_stage(k, f"rope{l}", spans, k.cos_a, k.sin_a, DK2)
            blocks = [([q[:, t, r].rearrange("p g d -> p (g d)") for t in range(NT)], qT[:, r, :], None, None) for r in range(R2)]
            blocks += [(columns_of(tok, c0, P), ksT[:, j, :], None, None) for j, c0 in enumerate((KS, KW))]
            transpose_stage(k, f"turn_nsa{l}", blocks)
        compress_stages(k, l, tok, kcmp, vbd)
        compressed_attention_stage(k, l, qT, kcmp, vbd, gates, o)

        def step(branch, r, i):
            v0 = (VS, VW)[branch]
            part = [slice(64 * g, 64 * g + 64) for g in range(G2)]

            def out(chain, psum, inv, m):
                h = m * R2 + r
                dst = o[:, i, h * DK2:(h + 1) * DK2]
                return nc.vector.scalar_tensor_tensor(dst, psum, inv, dst, ALU.mult, ALU.add)
            return Step(i=i, q=[qT[part[m], r, i * P:(i + 1) * P] for m in range(2)],
                        k=[ksT[part[m], branch, :] for m in range(2)],
                        v=lambda m, j: tok[:, j, v0 + m * DK2:v0 + (m + 1) * DK2], out=out,
                        gate=gates[:, i, r:H2:R2, 1 + branch])
        attention_stage(k, f"nsa{l}", [step(br, r, i) for br in range(2) for r in range(R2) for i in range(NT)],
                        DK2 ** -0.5, False, gated=True)


def mla_stages(k, l, tok):
    nc = k.nc
    OUT = H2 * DQ
    with ExitStack() as ctx:
        def sb(s, shape):
            return ctx.enter_context(nc.sbuf_tensor(f"mla{l}_{s}", shape, F32))

        qT = sb("qT", [DQ, H2, S])
        v = sb("v", [P, NT, H2 * DV2])
        kT = sb("kT", [DQ, H2, S])
        rms_stage(k, f"mla_norm{l}", [(tok[:, t:t + 1, CQ:CQ + RQ], tok[:, t:t + 1, CQ:CQ + RQ], RQ, None) for t in range(NT)] +
                  [(tok[:, t:t + 1, CKV:CKV + RKV], tok[:, t:t + 1, CKV:CKV + RKV], RKV, None) for t in range(NT)])
        rope_stage(k, f"rope_k{l}", in_place([tok[:, t, KR:KR + DR].rearrange("p (n w) -> p n w", w=DR) for t in range(NT)]), k.cos_b, k.sin_b, DR)
        with nc.sbuf_tensor(f"mla{l}_lat", [P, 3, S], F32) as lat:
            kpe = [(qT[64:64 + DR, 0, :], 64)]
            blocks = [(columns_of(tok, CQ + j * P, P), lat[:, j, :], k.q_norm[:, l, j:j + 1], None) for j in range(2)]
            blocks.append((columns_of(tok, CKV, P), lat[:, 2, :], k.kv_norm[:, l, :], None))
            blocks += [(columns_of(tok, KR - DN, DQ), (kT[DN:DQ, h, :], DN), None, None) for h in range(H2)]
            transpose_stage(k, f"turn_lat{l}", blocks)
            wq, wkv = chunk_view(k, ("up", l))
            key = ("up", l)
            jobs = []
            for t in range(NT):
                c = slice(t * P, (t + 1) * P)
                for c0, c1 in ((0, COL), (COL, H2 * DQ)):
                    jobs.append(Job([(lat[:, j, c], wq[:, j, c0:c1]) for j in range(2)], P, c1 - c0, copy_to(k, tok[:, t, c0:c1]),
                                    engine_of(len(jobs)), key))
                wv = wkv[:, 0, :].rearrange("p (h n) -> p h n", n=DN + DV2)[:, :, DN:]
                jobs.append(Job([(lat[:, 2, c], wv)], P, H2 * DV2, copy_to(k, v[:, t, :]), engine_of(len(jobs)), key))
            for h in range(H2):
                jobs.append(Job([(wkv[:, 0, h * (DN + DV2):h * (DN + DV2) + DN], lat[:, 2, :])], DN, S, copy_to(k, kT[0:DN, h, :]),
                                engine_of(len(jobs)), key))
            gemm_stage(k, f"up{l}", jobs, last_key=key)
        rope_stage(k, f"rope_q{l}", in_place([tok[:, t, 0:H2 * DQ].rearrange("p (n w) -> p n w", w=DQ)[:, :, DN:] for t in range(NT)]), k.cos_b, k.sin_b, DR)
        transpose_stage(k, f"turn_q{l}", [(columns_of(tok, h * DQ, DQ), qT[:, h, :], None, None) for h in range(H2)])

        def step(pair, i):
            def out(chain, psum, inv, m):
                h = 2 * pair + m
                return nc.vector.tensor_scalar(tok[:, i, OUT + h * DV2:OUT + (h + 1) * DV2], psum, inv, None, ALU.mult)
            return Step(i=i, q=[qT[:, 2 * pair + m, i * P:(i + 1) * P] for m in range(2)],
                                   k=[kT[:, 2 * pair + m, :] for m in range(2)],
                                   v=lambda m, j: v[:, j, (2 * pair + m) * DV2:(2 * pair + m + 1) * DV2], out=out)
        attention_stage(k, f"mla{l}", [step(pair, i) for pair in range(H2 // 2) for i in range(NT)], DQ ** -0.5, False)


def mlp_stage(k, l):
    nc = k.nc
    quarter = FF2 // 4 // P
    with nc.sbuf_tensor(f"mlp{l}_u_hi", [P, quarter, S], F32R) as u_hi, nc.sbuf_tensor(f"mlp{l}_u_lo", [P, quarter, S], F32R) as u_lo, \
            nc.sbuf_tensor(f"mlp{l}_relu", [P, 2, S], F32) as relu:
        u = Halves(u_hi, u_lo)
        jobs = []

        def hidden(f, w, cols, key):
            r = relu[:, f % 2, :]

            def evac(e, chain, psum):
                chain(nc.scalar.activation(r, psum, ACT.Relu))
                return nc.scalar.activation(u.hi[:, f, :], r, ACT.Square)

            def finish(chain):
                chain(nc.vector.tensor_tensor(r, r, r, ALU.mult))
                return nc.vector.tensor_tensor(u.lo[:, f, :], r, u.hi[:, f, :].bitcast(F32), ALU.subtract)
            mm = [(w[:, j, cols], k.hT[:, j, :]) for j in range(ND)]
            jobs.append(Job(mm, P, S, evac, "act", key, finish=finish))

        for q in range(4):
            made = len(jobs)
            for c in range(2):
                key = ("ff1", l, 2 * q + c)
                w = split_chunk(k, key)
                for i in range(4):
                    hidden(4 * c + i, w, slice(i * P, (i + 1) * P), key)
            for n in range(2):
                key = ("ff2", l, n, q)
                w = split_chunk(k, key)
                for t in range(NT):
                    mm = [(u[:, f, t * P:(t + 1) * P], w[:, f, :]) for f in range(quarter)]
                    jobs.append(Job(mm, P, COL, residual(k, t, n), "dve", key, needs=[made + f for f in range(quarter)]))
        split_gemm_stage(k, f"mlp{l}", jobs, last_key=key)


def part2(k, a):
    nc = k.nc
    for l in range(LAYERS):
        with cleared_semaphores(nc):
            layer(k, a, l)
    rms_stage(k, "final_norm", [(k.x[:, t:t + 1, :], k.x[:, t:t + 1, :], D, k.gain_row[:]) for t in range(NT)])


def layer(k, a, l):
    nc = k.nc
    with nc.sbuf_tensor(f"xn2_{l}", [P, NT, D], F32) as xn:
        norm_turn_stage(k, f"norm_a{l}", [(k.x, xn, k.attn_norm[:, l, :], None)], k.hT)
    with nc.sbuf_tensor(f"tok2_{l}", [P, NT, IN2_W], F32) as tok, nc.sbuf_tensor(f"nsa_o{l}", [P, NT, 512], F32) as o:
        with nc.sbuf_tensor(f"in2_w{l}", [P, 2, 2, SLOT], F32R) as k.w_split:
            project2_stage(k, l, tok)
        nsa_stages(k, l, tok, o)
        mla_stages(k, l, tok)
        ob = tok[:, :, H2 * DQ:H2 * DQ + 512]
        norm_turn_stage(k, f"mix_norm{l}", [(o, o, k.nsa_norm[:, l, :], None), (ob, ob, k.mla_norm[:, l, :], None)], k.hT)
    with nc.sbuf_tensor(f"mlp_w{l}", [P, 2, 2, SLOT], F32R) as k.w_split:
        jobs = []
        for n in range(2):
            key = ("out2", l, n)
            w = split_chunk(k, key)
            for t in range(NT):
                mm = [(k.hT[:, j, t * P:(t + 1) * P], w[:, j, :]) for j in range(ND)]
                jobs.append(Job(mm, P, COL, residual(k, t, n), "dve", key))
        split_gemm_stage(k, f"out2_{l}", jobs, last_key=key)
        with nc.sbuf_tensor(f"xn3_{l}", [P, NT, D], F32) as xn:
            norm_turn_stage(k, f"norm_m{l}", [(k.x, xn, k.mlp_norm[:, l, :], None)], k.hT)
        mlp_stage(k, l)


def store_stage(k, out):
    nc = k.nc
    with ExitStack() as ctx:
        stored = nc.alloc_semaphore("out_stored")
        block = ctx.enter_context(nc.Block())

        @block.sync
        def _(sp):
            sp.dma_start(out[0].rearrange("(t p) d -> p t d", p=P), k.x[:]).then_inc(stored, 16)
            sp.wait_ge(stored, 16)


class Program:

    def __init__(self, nc, a, ctx):
        self.nc, self.a, self.ctx = nc, a, ctx
        self.small = []
        self.n_groups = 0
        self.next_load = 0
        self.last_group = {}
        self.plan = plan_chunks(a)
        self.chunk_no = {key: n for n, (key, _) in enumerate(self.plan)}
        self.load_end = self.chunk_no[("out1", 1)]
        self.loaded_at, count = [], [0] * SLOTS
        for n, (_, parts) in enumerate(self.plan):
            count[n % SLOTS] += 16 * len(parts)
            self.loaded_at.append(count[n % SLOTS])

    def sb(self, name, shape, dt=F32):
        return self.ctx.enter_context(self.nc.sbuf_tensor(name, shape, dt))

    def loaded(self, name, shape, *sources):
        t = self.sb(name, shape)
        if len(sources) == 1:
            self.small.append((t[:], sources[0]))
        else:
            self.small += [(t[:, i], src) for i, src in enumerate(sources)]
        return t

    def expert_chunk(self, c, u):
        if u == 1 and c < TWICE:
            where, at = self.expert_w2, c
        else:
            where, at = (self.ring, c) if c < SLOTS else (self.expert_w, c - SLOTS)
        return where[:, at * SLOT:(at + 1) * SLOT].rearrange("p (k n) -> p k n", n=COL if c < 4 else D)

    def constant(self, name):
        src = self.a[f"const_{name}"]
        return self.loaded(name, list(src.shape), src)


def column(v):
    return v.rearrange("(k p) -> p k", p=P)


def row(v):
    return v.partition_broadcast(P)


def build(nc, a, out):
    h2_dram = nc.dram_tensor("h2_rows", [S, D], F32).ap()
    y_dram = nc.dram_tensor("expert_rows", [S * TOPK + P, D], F32).ap()
    with ExitStack() as ctx:
        k = Program(nc, a, ctx)
        k.x = k.sb("x", [P, NT, D])
        k.ring = k.sb("ring", [P, SLOTS * SLOT])
        k.eps = k.sb("eps", [P, 1])
        k.ones = k.sb("ones", [P, P])
        k.ident, k.causal_bias = k.sb("ident", [P, P]), k.sb("causal_bias", [P, P])
        k.tables = [(k.ident[:], a["const_ident"]), (k.causal_bias[:], a["const_causal_bias"])]
        k.tables_loaded = nc.alloc_semaphore("tables_loaded")
        k.ident_half, k.causal_half = k.sb("ident_half", [P, P], BF16), k.sb("causal_half", [P, P], BF16)
        k.cmp_mask = k.constant("cmp_mask")
        k.cmp_bias = k.constant("cmp_bias")
        k.cos_a, k.sin_a = k.constant("cos_a"), k.constant("sin_a")
        k.cos_b, k.sin_b = k.constant("cos_b"), k.constant("sin_b")

        def layers(name):
            return [column(a[name][l]) for l in range(LAYERS)]

        k.attn_norm = k.loaded("attn_norm", [P, LAYERS, ND], *layers("attn_norm_2"))
        k.mlp_norm = k.loaded("mlp_norm", [P, LAYERS, ND], *layers("mlp_norm_2"))
        k.nsa_norm = k.loaded("nsa_norm", [P, LAYERS, 4], *layers("nsa_out_norm_2"))
        k.mla_norm = k.loaded("mla_norm", [P, LAYERS, 4], *layers("mla_out_norm_2"))
        k.q_norm = k.loaded("q_norm", [P, LAYERS, 2], *layers("mla_q_norm_2"))
        k.kv_norm = k.loaded("kv_norm", [P, LAYERS, 1], *layers("mla_kv_norm_2"))
        k.gain_row = k.loaded("gain_row", [P, D], row(a["norm2_g"][0]))
        k.ring_loaded = [nc.alloc_semaphore(f"ring_loaded{i}") for i in range(SLOTS)]
        k.groups_done = nc.alloc_semaphore("groups_done")
        k.small_pool_loaded = nc.alloc_semaphore("small_pool_loaded")
        k.gathered, k.y_stored = nc.alloc_semaphore("moe_gathered"), nc.alloc_semaphore("moe_y_stored")
        with cleared_semaphores(nc), ExitStack() as k.ctx:
            k.gated = k.sb("gated", [P, COL])
            k.upper_incl = k.constant("upper_incl")
            k.upper_strict = k.constant("upper_strict")
            k.iota = k.constant("iota")
            k.place_no = k.constant("place_no")
            k.spare_no = k.constant("spare_no")
            k.row_no, k.half_no = k.constant("row_no"), k.constant("half_no")
            k.c_col = k.loaded("c_col", [P, ND], column(a["c"][0]))
            k.norm1 = k.loaded("norm1", [P, ND], column(a["norm1_g"][0]))
            k.a_q_gain = k.loaded("a_q_gain", [P, A_DK], row(a["a_q_gain"][0]))
            k.a_k_gain = k.loaded("a_k_gain", [P, A_DK], row(a["a_k_gain"][0]))
            k.a_out_gain = k.loaded("a_out_gain", [P, A_DV], row(a["a_out_gain"][0]))
            k.b_q_gain = k.loaded("b_q_gain", [P, B_DK], row(a["b_q_gain"][0]))
            k.b_k_gain = k.loaded("b_k_gain", [P, B_DK], row(a["b_k_gain"][0]))
            k.c_out_gain = k.loaded("c_out_gain", [P, C_DV], row(a["c_out_gain"][0]))
            k.lam_q = k.loaded("lam_q", [P, 2, A_DK], row(a["a_lam_q1"][0]), row(a["a_lam_q2"][0]))
            k.lam_k = k.loaded("lam_k", [P, 2, A_DK], row(a["a_lam_k1"][0]), row(a["a_lam_k2"][0]))
            k.c_wg2 = k.loaded("c_wg2", [C_RANK, C_HEADS * C_DK], a["c_w_g2"][0])
            k.c_bg = k.loaded("c_bg", [P, 1], column(a["c_b_g"][0]))
            k.conv_w = k.loaded("conv_w", [P, CONV_W, 2], *[column(a["d_conv_w"][0][i]) for i in range(CONV_W)])
            k.conv_b = k.loaded("conv_b", [P, 2], column(a["d_conv_b"][0]))
            k.lru_b = k.loaded("lru_b", [P, 2, 2], column(a["d_b_a"][0]), column(a["d_b_x"][0]))
            k.lru_lam = k.loaded("lru_lam", [P, 2], column(a["d_lambda"][0]))
            k.lru_w = k.sb("lru_w", [P, 2, 2, P])
            k.lru_blocks = [(k.lru_w[64 * (n % 2):64 * (n % 2) + 64, i, n // 2, 64 * (n % 2):64 * (n % 2) + 64], a[name][0][n])
                            for i, name in enumerate(("d_w_a", "d_w_x")) for n in range(4)]
            k.router_w = k.loaded("router_w", [P, ND, NE], a["router_w"][0].rearrange("(k p) n -> p k n", p=P))
            k.router_b = k.loaded("router_b", [1, NE], a["router_b"])
            k.mod = k.sb("mod", [P, 4, D])
            k.scale1, k.shift1 = k.sb("scale1", [P, ND]), k.sb("shift1", [P, ND])
            k.lam = k.sb("lam", [P, 1])
            k.gla_state = k.sb("gla_state", [P, 256])
            k.gla_tile_decay = k.sb("gla_tile_decay", [P, NT])
            k.gates = k.sb("gates", [P, NT, TOPK])
            k.row_token, k.row_place = k.sb("row_token", [P, MAXB + 1], I32), k.sb("row_place", [P, MAXB + 1], I32)
            k.first = k.sb("first_block", [1, NE + 1], I32)
            k.expert_loaded = [nc.alloc_semaphore(f"expert_loaded{c}") for c in range(CHUNKS)]
            with nc.sbuf_tensor("hT1", [P, ND, S], F32) as k.hT:
                load_stage(k, a)
                part1(k, a)
                second_norm_stages(k, h2_dram)
                with nc.sbuf_tensor("expert_w", [P, (CHUNKS - SLOTS) * SLOT], F32) as k.expert_w:
                    route_stages(k, a)
                    expert_stage(k, a, h2_dram, y_dram)
            combine_stage(k, y_dram)
        with nc.sbuf_tensor("hT2_hi", [P, ND, S], F32R) as hi, nc.sbuf_tensor("hT2_lo", [P, ND, S], F32R) as lo:
            k.hT, k.split_no = Halves(hi, lo), {}
            part2(k, a)
        store_stage(k, out)


INPUTS = ("x c ada_w ada_b norm1_g norm2_g w_in w_out a_q_gain a_k_gain a_lam_q1 a_lam_k1 a_lam_q2 a_lam_k2 a_out_gain b_q_gain "
          "b_k_gain c_w_g2 c_b_g c_out_gain d_conv_w d_conv_b d_w_a d_b_a d_w_x d_b_x d_lambda router_w router_b exp_w_up exp_b_up "
          "exp_w_down exp_b_down attn_norm_2 w_in_2 cmp_pos_k_2 cmp_w1_k_2 cmp_w2_k_2 cmp_pos_v_2 cmp_w1_v_2 cmp_w2_v_2 mla_q_norm_2 "
          "w_q_up_2 mla_kv_norm_2 w_kv_up_2 nsa_out_norm_2 mla_out_norm_2 w_out_2 mlp_norm_2 w_ff1_2 w_ff2_2 final_norm_2").split()


def kernel(**inputs):
    import concourse.bacc as bacc
    from concourse.bass_utils import run_bass_kernel_spmd

    nc = bacc.Bacc("TRN2", target_bir_lowering=False, num_devices=1)
    arrays = {n: np.ascontiguousarray(inputs[n]) for n in INPUTS}
    arrays |= {f"const_{n}": v for n, v in host_constants().items()}
    a = {n: nc.dram_tensor(f"in_{n}", v.shape, mybir.dt.from_np(v.dtype), kind="ExternalInput").ap() for n, v in arrays.items()}
    out = nc.dram_tensor("out", [1, S, D], F32, kind="ExternalOutput").ap()
    build(nc, a, out)
    result = run_bass_kernel_spmd(nc, [{f"in_{n}": v for n, v in arrays.items()}], core_ids=[0])
    return result.results[0]["out"]
```

```python
import math
from contextlib import ExitStack, contextmanager

import numpy as np

import concourse.bass as bass
from concourse import mybir

F32 = mybir.dt.float32
BF16 = mybir.dt.bfloat16
F32R = mybir.dt.float32r
I32 = mybir.dt.int32
U32 = mybir.dt.uint32
ALU = mybir.AluOpType
ACT = mybir.ActivationFunctionType
X = mybir.AxisListType.X

P = 128
S = 512
NT = S // P
D = 1024
ND = D // P
EPS = 1e-6
NEG = -1e30
COL = 512
SLOTS = 3
SLOT = ND * COL
PIECES = 4

A_HEADS, A_DK, A_DV = 4, 32, 64
B_HEADS, B_DK = 4, 64
C_HEADS, C_DK, C_DV, C_RANK, C_TAU = 4, 32, 64, 16, 16.0
SUB = 16
NSUB = P // SUB
DECAY_CLAMP = 60.0
W_D = 256
CONV_W = 4
LAM_INIT = 0.8 - 0.6 * math.exp(-0.3 * 0)
NE, TOPK, FF = 32, 4, 1024
BR = 64
MAXB = S * TOPK // BR + NE
UNITS = FF // 4
ALPHA, LIMIT = 1.702, 7.0

OUT_A, OUT_B, OUT_C = 0, 768, 1024
CR = 1792

LAYERS = 2
H2, G2, R2, DK2 = 8, 2, 4, 64
CB, CS, CHID = 32, 16, 256
NCMP = S // CS - 1
CPAD = 32
RQ, RKV, DR, DN, DV2 = 256, 128, 32, 64, 64
DQ = DN + DR
FF2 = 4096


class Job:

    def __init__(self, mm, m, n, evac, eng, chunk=None, finish=None, needs=None):
        self.mm, self.m, self.n, self.evac, self.eng, self.chunk = mm, m, n, evac, eng, chunk
        self.finish, self.needs = finish, needs


def tiles(n):
    return range(NT) if n % 2 else range(NT - 1, -1, -1)


class Step:

    def __init__(self, i, q, k, v, out, gate=None):
        self.i, self.q, self.k, self.v, self.out, self.gate = i, q, k, v, out, gate


class Chain:

    def __init__(self, engine, sem):
        self.engine, self.sem, self.n = engine, sem, 0

    def __call__(self, instruction):
        self.n += 1
        instruction.then_inc(self.sem, 1)
        self.engine.wait_ge(self.sem, self.n)


def host_constants():
    p = np.arange(P)
    tok = np.arange(S)
    f32 = np.float32
    out = {}
    out["ident"] = np.eye(P, dtype=f32)
    out["causal_bias"] = np.where(p[None, :] <= p[:, None], 0.0, NEG).astype(f32)
    out["upper_incl"] = (p[:, None] <= p[None, :]).astype(f32)
    out["upper_strict"] = (p[:, None] < p[None, :]).astype(f32)
    out["iota"] = np.tile(np.arange(P, dtype=f32), (P, 1))
    out["place_no"] = (1 + TOPK * tok.reshape(NT, P).T[:, :, None] + np.arange(TOPK)).reshape(P, NT * TOPK).astype(f32)
    out["spare_no"] = (1 + TOPK * S + p[:, None] % BR).astype(f32)
    out["row_no"] = np.tile((p % BR).astype(f32), (P, 1))
    out["half_no"] = (p[:, None] // BR).astype(f32)
    n = np.arange(CPAD)
    seen = (n[None, :] * CS + CB - 1 <= tok[:, None]) & (n[None, :] < NCMP)
    seen = np.ascontiguousarray(seen.reshape(NT, P, CPAD).transpose(1, 0, 2))
    out["cmp_mask"] = seen.astype(f32)
    out["cmp_bias"] = np.where(seen, 0.0, NEG).astype(f32)
    for name, dim in (("a", DK2), ("b", DR)):
        inv = (1.0 / (np.float32(10000.0) ** (np.arange(0, dim, 2, dtype=f32) / np.float32(dim)))).astype(f32)
        ang = (tok.astype(f32)[:, None] * inv[None, :]).astype(f32)
        ang = np.concatenate([ang, ang], axis=-1)
        sign = np.where(np.arange(dim) < dim // 2, -1.0, 1.0).astype(f32)
        out[f"cos_{name}"] = np.ascontiguousarray(np.cos(ang).astype(f32).reshape(NT, P, dim).transpose(1, 0, 2))
        out[f"sin_{name}"] = np.ascontiguousarray((np.sin(ang) * sign).astype(f32).reshape(NT, P, dim).transpose(1, 0, 2))
    return out




def plan_chunks(a):
    plan = []

    def cols(key, w, c0, c1):
        plan.append((key, [(0, w.shape[0] // P * (c1 - c0), w[:, c0:c1].rearrange("(k p) n -> p k n", p=P), c1 - c0)]))

    def modulation(n0, n1):
        for n in range(n0, n1):
            cols(("ada", n), a["ada_w"][0], n * COL, (n + 1) * COL)

    modulation(0, FIRST_MOD)
    for n, (c0, c1) in enumerate(IN1):
        cols(("in1", n), a["w_in"][0], c0, c1)
    modulation(FIRST_MOD, 6 * D // COL)
    for n in range(D // NARROW):
        cols(("out1", n), a["w_out"][0], n * NARROW, (n + 1) * NARROW)
    for l in range(LAYERS):
        for n, (c0, c1) in enumerate(IN2):
            cols(("in2", l, n), a["w_in_2"][l], c0, c1)
        for kv in "kv":
            w = a[f"cmp_w1_{kv}_2"][l].rearrange("(k p) n -> p k n", p=P)
            plan.append((("cmp", l, kv), [(0, 16 * CHID, w, CHID)]))
        plan.append((("up", l), [
            (0, 2 * H2 * DQ, a["w_q_up_2"][l].rearrange("(k p) n -> p k n", p=P), H2 * DQ),
            (2 * H2 * DQ, H2 * (DN + DV2), a["w_kv_up_2"][l].rearrange("(k p) n -> p k n", p=P), H2 * (DN + DV2)),
        ]))
        for n in range(2):
            cols(("out2", l, n), a["w_out_2"][l], n * COL, (n + 1) * COL)
        for q in range(4):
            for n in (2 * q, 2 * q + 1):
                cols(("ff1", l, n), a["w_ff1_2"][l], n * COL, (n + 1) * COL)
            for half in range(2):
                w = a["w_ff2_2"][l][q * D:(q + 1) * D, half * COL:(half + 1) * COL].rearrange("(k p) n -> p k n", p=P)
                plan.append((("ff2", l, half, q), [(0, SLOT, w, COL)]))
    return plan


FIRST_MOD = 2 * D // COL
NARROW = 256
IN1 = [(c, c + NARROW) for c in range(0, 2048, NARROW)] + [(2048, 2176), (2176, 2320), (2320, 2576), (2576, 2832)]
IN2 = [(0, 512), (512, 1024), (1024, 1536), (1536, 1720)]


def chunk_view(k, key):
    n = k.chunk_no[key]
    base = (n % SLOTS) * SLOT
    _, parts = k.plan[n]
    return [k.ring[:, base + off:base + off + size].rearrange("p (k n) -> p k n", n=width)
            for off, size, _, width in parts]


def wait_chunk(k, eng, key):
    n = k.chunk_no[key]
    eng.wait_ge(k.ring_loaded[n % SLOTS], k.loaded_at[n])


def load_chunks(k, sp, last_key):
    limit = k.chunk_no[last_key] + SLOTS if last_key is not None else SLOTS - 1
    while k.next_load <= min(limit, k.load_end):
        n = k.next_load
        if n >= SLOTS:
            sp.wait_ge(k.groups_done, k.last_group[n - SLOTS])
        base = (n % SLOTS) * SLOT
        for off, size, src, width in k.plan[n][1]:
            sp.dma_start(k.ring[:, base + off:base + off + size].rearrange("p (k n) -> p k n", n=width),
                         src).then_inc(k.ring_loaded[n % SLOTS], 16)
        k.next_load += 1




def gemm_stage(k, name, jobs, banks=8, last_key=None, extra=None):
    nc = k.nc
    first = k.n_groups
    for n, job in enumerate(jobs):
        if job.chunk is not None:
            k.last_group[k.chunk_no[job.chunk]] = first + n + 1
    k.n_groups += len(jobs)
    order = {"act": [n for n, j in enumerate(jobs) if j.eng == "act"],
             "dve": [n for n, j in enumerate(jobs) if j.eng == "dve"]}
    rank = {n: i for e in order for i, n in enumerate(order[e])}
    with ExitStack() as ctx:
        evac_done = {e: nc.alloc_semaphore(f"{name}_{e}_evacuated") for e in order}
        evac_step = {e: nc.alloc_semaphore(f"{name}_{e}_step") for e in order}
        bank = [ctx.enter_context(nc.psum_tensor(f"{name}_bank{i}", [P, COL], F32)) for i in range(banks)]
        block = ctx.enter_context(nc.Block())

        @block.sync
        def _(sp):
            if last_key is not None:
                load_chunks(k, sp, last_key)

        @block.tensor
        def _(pe):
            seen = None
            for n, job in enumerate(jobs):
                if job.chunk is not None and job.chunk != seen:
                    wait_chunk(k, pe, job.chunk)
                    seen = job.chunk
                if n >= banks:
                    e = jobs[n - banks].eng
                    pe.wait_ge(evac_done[e], rank[n - banks] + 1)
                out = bank[n % banks][:job.m, :job.n]
                for i, (lhsT, rhs) in enumerate(job.mm):
                    mm = nc.tensor.matmul(out, lhsT, rhs, start=(i == 0), stop=(i == len(job.mm) - 1))
                mm.then_inc(k.groups_done, 1)

        def evacuate(eng, e):
            chain = Chain(eng, evac_step[e])
            for i, n in enumerate(order[e]):
                eng.wait_ge(k.groups_done, first + n + 1)
                if i >= 1:
                    eng.wait_ge(evac_done[e], i)
                jobs[n].evac(jobs[n].eng, chain, bank[n % banks][:jobs[n].m, :jobs[n].n]).then_inc(evac_done[e], 1)

        @block.scalar
        def _(act):
            evacuate(act, "act")

        @block.vector
        def _(dve):
            evacuate(dve, "dve")




class Halves:

    def __init__(self, hi, lo):
        self.hi, self.lo = hi, lo

    def __getitem__(self, index):
        return Halves(self.hi[index], self.lo[index])


def split_chunk(k, key):
    (w,) = chunk_view(k, key)
    if key not in k.split_no:
        k.split_no[key] = len(k.split_no)
    at = k.w_split[:, k.split_no[key] % 2, :, 0:w.shape[1] * w.shape[2]].rearrange("p s (k n) -> p s k n", n=w.shape[2])
    return Halves(at[:, 0], at[:, 1])


def split_gemm_stage(k, name, jobs, banks=8, last_key=None, norm=None, room=None):
    nc = k.nc
    first = k.n_groups
    for n, job in enumerate(jobs):
        k.last_group[k.chunk_no[job.chunk]] = first + n + 1
    k.n_groups += len(jobs)
    chunks = list(dict.fromkeys(job.chunk for job in jobs))
    order = {e: [n for n, j in enumerate(jobs) if j.eng == e] for e in ("act", "dve")}
    rank = {n: i for e in order for i, n in enumerate(order[e])}
    finish_rank = {n: i for i, n in enumerate(n for n, j in enumerate(jobs) if j.finish)}
    with ExitStack() as ctx:
        evac_done = {e: nc.alloc_semaphore(f"{name}_{e}_evacuated") for e in order}
        evac_step = {e: nc.alloc_semaphore(f"{name}_{e}_step") for e in order}
        hi_made, lo_made = nc.alloc_semaphore(f"{name}_hi_made"), nc.alloc_semaphore(f"{name}_lo_made")
        finished = nc.alloc_semaphore(f"{name}_finished")
        bank = [ctx.enter_context(nc.psum_tensor(f"{name}_bank{i}", [P, COL], F32)) for i in range(banks)]
        opening = NormTurn(k, f"{name}_norm", norm, k.hT, ctx, bank, room) if norm is not None else None
        block = ctx.enter_context(nc.Block())

        def pieces(c):
            blocks = chunk_view(k, chunks[c])[0].shape[1]
            return [(c * PIECES + i, slice(blocks * i // PIECES, blocks * (i + 1) // PIECES)) for i in range(PIECES)]

        @block.sync
        def _(sp):
            load_chunks(k, sp, last_key)

        @block.tensor
        def _(pe):
            needed = 0
            if opening:
                opening.tensor(pe)
            for n, job in enumerate(jobs):
                if n >= banks:
                    e = jobs[n - banks].eng
                    pe.wait_ge(evac_done[e], rank[n - banks] + 1)
                opens = n == 0 or jobs[n - 1].chunk != job.chunk
                starts = {at.start: piece for piece, at in pieces(chunks.index(job.chunk))} if opens else {}
                out = bank[n % banks][:job.m, :job.n]
                for i, (lhsT, rhs) in enumerate(job.mm):
                    if opening and n == 0:
                        opening.wait_block(pe, i)
                    if i in starts:
                        pe.wait_ge(hi_made, starts[i] + 1)
                        pe.wait_ge(lo_made, starts[i] + 1)
                    if job.needs is not None and finish_rank[job.needs[i]] + 1 > needed:
                        needed = finish_rank[job.needs[i]] + 1
                        pe.wait_ge(finished, needed)
                    last = i == len(job.mm) - 1
                    nc.tensor.matmul(out, lhsT.hi, rhs.hi, start=(i == 0), stop=False)
                    nc.tensor.matmul(out, lhsT.hi, rhs.lo, start=False, stop=False)
                    mm = nc.tensor.matmul(out, lhsT.lo, rhs.hi, start=False, stop=last)
                mm.then_inc(k.groups_done, 1)

        def work(eng, e, split):
            chain = Chain(eng, evac_step[e])
            if opening:
                opening.scalar_sums(eng) if e == "act" else opening.vector_diagonals(eng)
            split(0)
            if opening:
                opening.scalar_halves(eng) if e == "act" else opening.vector_halves(eng)
            for n, job in enumerate(jobs):
                if n == 0 or jobs[n - 1].chunk != job.chunk:
                    c = chunks.index(job.chunk)
                    if c + 1 < len(chunks):
                        split(c + 1)
                if job.eng == e:
                    eng.wait_ge(k.groups_done, first + n + 1)
                    if rank[n] >= 1:
                        eng.wait_ge(evac_done[e], rank[n])
                    if job.finish and finish_rank[n] >= 2:
                        eng.wait_ge(finished, finish_rank[n] - 1)
                    job.evac(e, chain, bank[n % banks][:job.m, :job.n]).then_inc(evac_done[e], 1)
                if job.finish and e == "dve":
                    eng.wait_ge(evac_done["act"], rank[n] + 1)
                    if finish_rank[n] >= 2:
                        eng.wait_ge(finished, finish_rank[n] - 1)
                    job.finish(chain).then_inc(finished, 1)

        @block.scalar
        def _(act):
            def split(c):
                (w,), halves = chunk_view(k, chunks[c]), split_chunk(k, chunks[c])
                wait_chunk(k, act, chunks[c])
                if c >= 2:
                    act.wait_ge(k.groups_done, k.last_group[k.chunk_no[chunks[c - 2]]])
                for _, at in pieces(c):
                    nc.scalar.activation(halves.hi[:, at], w[:, at], ACT.Copy).then_inc(hi_made, 1)
            work(act, "act", split)

        @block.vector
        def _(dve):
            def split(c):
                (w,), halves = chunk_view(k, chunks[c]), split_chunk(k, chunks[c])
                for piece, at in pieces(c):
                    dve.wait_ge(hi_made, piece + 1)
                    nc.vector.tensor_tensor(halves.lo[:, at], w[:, at], halves.hi[:, at].bitcast(F32), ALU.subtract).then_inc(lo_made, 1)
            work(dve, "dve", split)


def copy_to(k, dst, scale=None, bias=None):
    nc = k.nc

    def evac(e, chain, psum):
        src = psum if dst.shape == psum.shape else psum
        if e == "act":
            if scale is None and bias is None:
                return nc.scalar.activation(dst, src, ACT.Copy)
            return nc.scalar.activation(dst, src, ACT.Identity, bias=bias if bias is not None else 0.0,
                                        scale=scale if scale is not None else 1.0)
        if scale is None and bias is None:
            return nc.vector.tensor_copy(dst, src)
        if scale is None:
            return nc.vector.tensor_scalar(dst, src, bias, None, ALU.add)
        if bias is None:
            return nc.vector.tensor_scalar(dst, src, scale, None, ALU.mult)
        return nc.vector.tensor_scalar(dst, src, scale, bias, ALU.mult, ALU.add)
    return evac


def engine_of(n):
    return "act" if n % 2 == 0 else "dve"




def transpose_stage(k, name, blocks, last_key=None):
    nc = k.nc
    with ExitStack() as ctx:
        turned = nc.alloc_semaphore(f"{name}_turned")
        taken = [nc.alloc_semaphore(f"{name}_taken_{e}") for e in ("act", "dve")]
        bank = [ctx.enter_context(nc.psum_tensor(f"{name}_bank{i}", [P, COL], F32)) for i in range(4)]
        block = ctx.enter_context(nc.Block())

        @block.sync
        def _(sp):
            if last_key is not None:
                load_chunks(k, sp, last_key)

        @block.tensor
        def _(pe):
            for n, (src, _, _, _) in enumerate(blocks):
                if n >= 4:
                    pe.wait_ge(taken[n % 2], (n - 4) // 2 + 1)
                w = src[0].shape[-1] if len(src[0].shape) == 2 else src[0].shape[1] * src[0].shape[2]
                for t in range(NT):
                    tr = nc.tensor.transpose(bank[n % 4][:w, t * P:(t + 1) * P], src[t], k.ident[:])
                tr.then_inc(turned, 1)

        def take(eng, e):
            for n, (src, dst, scale, bias) in enumerate(blocks):
                if n % 2 == e:
                    eng.wait_ge(turned, n + 1)
                    lo, w = (dst[1], dst[0].shape[0]) if isinstance(dst, tuple) else (0, dst.shape[0])
                    out = dst[0] if isinstance(dst, tuple) else dst
                    copy_to(k, out, scale, bias)("act" if e == 0 else "dve", None,
                                                 bank[n % 4][lo:lo + w, :]).then_inc(taken[e], 1)

        @block.scalar
        def _(act):
            take(act, 0)

        @block.vector
        def _(dve):
            take(dve, 1)


def split_transpose_stage(k, name, blocks, ready):
    nc = k.nc
    with ExitStack() as ctx:
        turned, hi_made, lo_made = (nc.alloc_semaphore(f"{name}_{s}") for s in ("turned", "hi_made", "lo_made"))
        bank = [ctx.enter_context(nc.psum_tensor(f"{name}_bank{i}", [P, COL], F32)) for i in range(8)]
        block = ctx.enter_context(nc.Block())
        sources = [(src, dst, 1.0) for src, dst in ready] + [(bank[n][:], dst, factor) for n, (_, dst, factor) in enumerate(blocks)]

        @block.tensor
        def _(pe):
            for n, (src, _, _) in enumerate(blocks):
                for t in range(NT):
                    tr = nc.tensor.transpose(bank[n][:, t * P:(t + 1) * P], src[t], k.ident[:])
                tr.then_inc(turned, 1)

        @block.scalar
        def _(act):
            for n, (src, dst, factor) in enumerate(sources):
                if n >= len(ready):
                    act.wait_ge(turned, n - len(ready) + 1)
                nc.scalar.activation(dst.hi, src, ACT.Copy, scale=factor).then_inc(hi_made, 1)

        @block.vector
        def _(dve):
            for n, (src, dst, factor) in enumerate(sources):
                dve.wait_ge(hi_made, n + 1)
                nc.vector.scalar_tensor_tensor(dst.lo, src, factor, dst.hi.bitcast(F32), ALU.mult, ALU.subtract).then_inc(lo_made, 1)


def idle_engines(block, beside):
    block.sync(beside.sync)
    block.tensor(beside.tensor)
    block.gpsimd(beside.gpsimd)


def rms_stage(k, name, groups, beside=None):
    nc = k.nc
    with ExitStack() as ctx:
        squared, summed, rooted, step = (nc.alloc_semaphore(f"{name}_{s}") for s in ("squared", "summed", "rooted", "step"))
        most = max(v.shape[1] * v.shape[2] * v.shape[3] for v, _ in groups)
        sq = ctx.enter_context(nc.sbuf_tensor(f"{name}_sq", [P, 2, most], F32))
        count = [v.shape[1] * v.shape[2] for v, _ in groups]
        at = [sum(count[:i]) for i in range(len(groups) + 1)]
        ss, rms, inv = (ctx.enter_context(nc.sbuf_tensor(f"{name}_{s}", [P, at[-1]], F32)) for s in ("ss", "rms", "inv"))
        opened = beside and beside(ctx)
        block = ctx.enter_context(nc.Block())
        if opened:
            idle_engines(block, opened)
        widths = list(dict.fromkeys(v.shape[3] for v, _ in groups))
        spans = [[i for i, (v, _) in enumerate(groups) if v.shape[3] == w] for w in widths]

        def as_rows(flat, v):
            return flat.rearrange("p (t n) -> p t n", t=v.shape[1])

        def square_of(i):
            v = groups[i][0]
            return sq[:, i % 2, 0:count[i] * v.shape[3]].rearrange("p (t n w) -> p t n w", t=v.shape[1], w=v.shape[3])

        @block.scalar
        def _(act):
            for i, (v, _) in enumerate(groups):
                if i >= 2:
                    act.wait_ge(summed, i - 1)
                nc.scalar.activation(square_of(i), v, ACT.Square).then_inc(squared, 1)
            for w, span in zip(widths, spans):
                c = slice(at[span[0]], at[span[-1] + 1])
                act.wait_ge(summed, span[-1] + 1)
                nc.scalar.activation(rms[:, c], ss[:, c], ACT.Sqrt, bias=k.eps[:], scale=1.0 / w).then_inc(rooted, 1)
            if opened:
                opened.scalar(act)

        @block.vector
        def _(dve):
            chain = Chain(dve, step)
            for i, (v, _) in enumerate(groups):
                dve.wait_ge(squared, i + 1)
                nc.vector.tensor_reduce(as_rows(ss[:, at[i]:at[i + 1]], v), square_of(i), X, ALU.add).then_inc(summed, 1)
            dve.wait_ge(rooted, len(widths))
            chain(nc.vector.reciprocal(inv[:], rms[:]))
            for i, (v, _) in enumerate(groups):
                shape = list(v.shape)
                nc.vector.tensor_tensor(v, v, as_rows(inv[:, at[i]:at[i + 1]], v).unsqueeze(3).to_broadcast(shape), ALU.mult).then_inc(step, 1)
            for i, (v, gain) in enumerate(groups):
                if gain is not None:
                    dve.wait_ge(step, 1 + i + 1)
                    nc.vector.tensor_tensor(v, v, gain.unsqueeze(1).unsqueeze(1).to_broadcast(list(v.shape)), ALU.mult)


class NormTurn:

    def __init__(self, k, name, parts, dst, ctx, bank, room):
        self.k, self.parts, self.dst, self.bank = k, parts, dst, bank
        nc = k.nc
        self.w = w = parts[0][0].shape[2]
        self.per = w // P
        self.rows = [(t, i) for t in range(NT) for i in range(len(parts))]
        n = len(self.rows)
        self.squared, self.rooted, self.inverted, self.spread = (
            nc.alloc_semaphore(f"{name}_{s}") for s in ("squared", "rooted", "inverted", "spread"))
        self.turned, self.whole, self.hi_made, self.lo_made = (
            nc.alloc_semaphore(f"{name}_{s}") for s in ("turned", "whole", "hi_made", "lo_made"))
        self.ss, self.rms, self.inv = (ctx.enter_context(nc.sbuf_tensor(f"{name}_{s}", [P, n], F32)) for s in ("ss", "rms", "inv"))
        self.shifts = parts[0][2] is not None
        self.squares = room[:, 0, 0:w // 2].bitcast(BF16)
        self.diagonal = [room[:, 1 + r * P // S, r * P % S:r * P % S + P] for r in range(n)]
        if self.shifts:
            self.y = [room[:, i, :] for i in range(2)]
            self.diagonal[-1] = ctx.enter_context(nc.sbuf_tensor(f"{name}_diagonal", [P, P], F32))[:]

    def columns(self, j):
        _, scale, shift = self.parts[j // self.per]
        c = slice(j % self.per, j % self.per + 1)
        return scale[:, c], None if shift is None else shift[:, c]

    def scalar_sums(self, act):
        k, nc = self.k, self.k.nc

        def root(n):
            act.wait_ge(self.squared, n + 1)
            nc.scalar.activation(self.rms[:, n:n + 1], self.ss[:, n:n + 1], ACT.Sqrt, bias=k.eps[:], scale=1.0 / self.w).then_inc(self.rooted, 1)

        for n, (t, i) in enumerate(self.rows):
            if n >= 1:
                act.wait_ge(self.squared, n)
            nc.scalar.activation(self.squares, self.parts[i][0][:, t, :], ACT.Square, accum_out=self.ss[:, n:n + 1]).then_inc(self.squared, 1)
            if n >= 1:
                root(n - 1)
        root(len(self.rows) - 1)

    def vector_diagonals(self, dve):
        k, nc = self.k, self.k.nc
        for n in range(len(self.rows)):
            dve.wait_ge(self.rooted, n + 1)
            nc.vector.reciprocal(self.inv[:, n:n + 1], self.rms[:, n:n + 1]).then_inc(self.inverted, 1)
            dve.wait_ge(self.inverted, n + 1)
            nc.vector.tensor_scalar(self.diagonal[n], k.ident[:], self.inv[:, n:n + 1], None, ALU.mult).then_inc(self.spread, 1)

    def tensor(self, pe):
        nc = self.k.nc
        for n, (t, i) in enumerate(self.rows):
            pe.wait_ge(self.spread, n + 1)
            for j in range(self.per):
                mm = nc.tensor.matmul(self.bank[i * self.per + j][:, t * P:(t + 1) * P], self.parts[i][0][:, t, j * P:(j + 1) * P],
                                      self.diagonal[n], start=True, stop=True)
                if t == NT - 1:
                    mm.then_inc(self.turned, 1)

    def scalar_halves(self, act):
        nc = self.k.nc
        for j in range(ND):
            scale, shift = self.columns(j)
            act.wait_ge(self.turned, j + 1)
            if self.shifts:
                if j >= 2:
                    act.wait_ge(self.lo_made, j - 1)
                nc.scalar.activation(self.y[j % 2], self.bank[j][:], ACT.Identity, scale=scale, bias=shift).then_inc(self.whole, 1)
                nc.scalar.activation(self.dst.hi[:, j, :], self.bank[j][:], ACT.Identity, scale=scale, bias=shift).then_inc(self.hi_made, 1)
            else:
                nc.scalar.activation(self.dst.hi[:, j, :], self.bank[j][:], ACT.Copy, scale=scale).then_inc(self.hi_made, 1)

    def vector_halves(self, dve):
        nc = self.k.nc

        for j in range(ND):
            scale, _ = self.columns(j)
            hi = self.dst.hi[:, j, :].bitcast(F32)
            dve.wait_ge(self.hi_made, j + 1)
            if self.shifts:
                dve.wait_ge(self.whole, j + 1)
                nc.vector.tensor_tensor(self.dst.lo[:, j, :], self.y[j % 2], hi, ALU.subtract).then_inc(self.lo_made, 1)
            else:
                nc.vector.scalar_tensor_tensor(self.dst.lo[:, j, :], self.bank[j][:], scale, hi, ALU.mult, ALU.subtract).then_inc(self.lo_made, 1)

    def wait_block(self, pe, j):
        pe.wait_ge(self.lo_made, j + 1)


def norm_rows_stage(k, name, src, dst, gain, shift, store, hT=None):
    nc = k.nc
    with ExitStack() as ctx:
        squared, rooted, inverted, gained, made = (nc.alloc_semaphore(f"{name}_{s}") for s in ("squared", "rooted", "inverted", "gained", "made"))
        turned, stored = nc.alloc_semaphore(f"{name}_turned"), nc.alloc_semaphore(f"{name}_stored")
        squares = ctx.enter_context(nc.sbuf_tensor(f"{name}_squares", [P, 2, D], BF16))
        ss, rms, inv = (ctx.enter_context(nc.sbuf_tensor(f"{name}_{s}", [P, NT], F32)) for s in ("ss", "rms", "inv"))
        bank = [ctx.enter_context(nc.psum_tensor(f"{name}_bank{i}", [P, COL], F32)) for i in range(ND)]
        block = ctx.enter_context(nc.Block())

        @block.sync
        def _(sp):
            for t in range(NT):
                sp.wait_ge(made, t + 1)
                sp.dma_start(store[t * P:(t + 1) * P, :], dst[:, t, :]).then_inc(stored, 16)
            sp.wait_ge(stored, 16 * NT)

        @block.scalar
        def _(act):
            for t in range(NT):
                if t >= 2:
                    act.wait_ge(squared, t - 1)
                nc.scalar.activation(squares[:, t % 2, :], src[:, t, :], ACT.Square, accum_out=ss[:, t:t + 1]).then_inc(squared, 1)
            act.wait_ge(squared, NT)
            nc.scalar.activation(rms[:], ss[:], ACT.Sqrt, bias=k.eps[:], scale=1.0 / D).then_inc(rooted, 1)
            for j in range(0, ND if hT is not None else 0, 2):
                act.wait_ge(turned, j + 1)
                nc.scalar.activation(hT[:, j, :], bank[j][:], ACT.Copy)

        @block.vector
        def _(dve):
            def shifted(t):
                dve.wait_ge(gained, t + 1)
                nc.vector.tensor_tensor(dst[:, t, :], dst[:, t, :], shift, ALU.add).then_inc(made, 1)

            dve.wait_ge(rooted, 1)
            nc.vector.reciprocal(inv[:], rms[:]).then_inc(inverted, 1)
            dve.wait_ge(inverted, 1)
            for t in range(NT):
                nc.vector.scalar_tensor_tensor(dst[:, t, :], src[:, t, :], inv[:, t:t + 1], gain, ALU.mult,
                                               ALU.mult).then_inc(made if shift is None else gained, 1)
                if shift is not None and t >= 1:
                    shifted(t - 1)
            if shift is not None:
                shifted(NT - 1)
            for j in range(1, ND if hT is not None else 0, 2):
                dve.wait_ge(turned, j + 1)
                nc.vector.tensor_copy(hT[:, j, :], bank[j][:])

        @block.tensor
        def _(pe):
            for t in range(NT if hT is not None else 0):
                pe.wait_ge(made, t + 1)
                for j in range(ND):
                    tr = nc.tensor.transpose(bank[j][:, t * P:(t + 1) * P], dst[:, t, j * P:(j + 1) * P], k.ident[:])
                    if t == NT - 1:
                        tr.then_inc(turned, 1)


def columns_of(src, c0, w):
    return [src[:, t, c0:c0 + w] for t in range(NT)]




def attention_stage(k, name, steps, scale, pair, lam=None, gated=False, last_key=None):
    nc = k.nc
    maps = 2
    turns = 1 if pair else 2
    with ExitStack() as ctx:
        def sem(s):
            return nc.alloc_semaphore(f"{name}_{s}")

        def sb(s, shape):
            return ctx.enter_context(nc.sbuf_tensor(f"{name}_{s}", shape, F32))

        scores_ready, bias_ready, exp_ready = sem("scores"), sem("bias"), sem("exp")
        weights_ready, turned = sem("weights"), sem("turned")
        taken_act, taken_dve, values_ready, out_taken = sem("taken_act"), sem("taken_dve"), sem("values"), sem("out")
        step_dve, inverted = sem("step"), sem("inverted")
        p = sb("p", [P, 2, maps, S])
        pt = sb("pt", [P, 2, turns, S])
        w = sb("w", [P, 2, S]) if pair else None
        top = sb("top", [P, 2, maps])
        neg = sb("neg", [P, 2, maps])
        total = sb("total", [P, 4, maps])
        inv = sb("inv", [P, 4, maps])
        lam_inv = sb("lam_inv", [P, 2, 1]) if pair else None
        sc = [ctx.enter_context(nc.psum_tensor(f"{name}_s{b}", [P, maps, COL], F32)) for b in range(2)]
        tr = [ctx.enter_context(nc.psum_tensor(f"{name}_t{b}", [P, COL], F32)) for b in range(2)]
        ov = [ctx.enter_context(nc.psum_tensor(f"{name}_o{b}", [P, COL], F32)) for b in range(2)]
        block = ctx.enter_context(nc.Block())
        n_steps = len(steps)

        @block.sync
        def _(sp):
            if last_key is not None:
                load_chunks(k, sp, last_key)

        @block.tensor
        def _(pe):
            def scores(n):
                st, b = steps[n], n % 2
                nk = P * (st.i + 1)
                if n >= 2:
                    pe.wait_ge(exp_ready, maps * (n - 1))
                for m in range(maps):
                    nc.tensor.matmul(sc[b][:, m, 0:nk], st.q[m], st.k[m][:, 0:nk], start=True, stop=False)
                for m in range(maps):
                    mm = nc.tensor.matmul(sc[b][:, m, nk - P:nk], k.ident_half[:], k.causal_half[:], start=False, stop=True)
                mm.then_inc(scores_ready, 1)

            def turn(n):
                st, b = steps[n], n % 2
                for m in range(turns):
                    u = n * turns + m
                    if pair:
                        pe.wait_ge(weights_ready, n + 1)
                    else:
                        pe.wait_ge(exp_ready, maps * n + m + 1)
                    if u >= 2:
                        pe.wait_ge(taken_act if u % 2 == 0 else taken_dve, (u - 2) // 2 + 1)
                    for j in range(st.i + 1):
                        row = w[:, b, j * P:(j + 1) * P] if pair else p[:, b, m, j * P:(j + 1) * P]
                        t = nc.tensor.transpose(tr[u % 2][:, j * P:(j + 1) * P], row, k.ident[:])
                    t.then_inc(turned, 1)

            def values(n):
                st, b = steps[n], n % 2
                if n >= 2:
                    pe.wait_ge(out_taken, n - 1)
                for m in range(turns):
                    u = n * turns + m
                    pe.wait_ge(taken_act if u % 2 == 0 else taken_dve, u // 2 + 1)
                    for j in range(st.i + 1):
                        mm = nc.tensor.matmul(ov[b][:, m * 64:(m + 1) * 64], pt[:, b, m, j * P:(j + 1) * P],
                                              st.v(m, j), start=(j == 0), stop=(j == st.i))
                mm.then_inc(values_ready, 1)

            scores(0)
            scores(1)
            turn(0)
            for n in range(n_steps):
                if n + 2 < n_steps:
                    scores(n + 2)
                if n + 1 < n_steps:
                    turn(n + 1)
                values(n)

        def take_turned(eng, n, m):
            u, b = n * turns + m, n % 2
            nk = P * (steps[n].i + 1)
            if n >= 2:
                eng.wait_ge(values_ready, n - 1)
            eng.wait_ge(turned, u + 1)
            if u % 2 == 0:
                nc.scalar.activation(pt[:, b, m, 0:nk], tr[0][:, 0:nk], ACT.Copy).then_inc(taken_act, 1)
            else:
                nc.vector.tensor_copy(pt[:, b, m, 0:nk], tr[1][:, 0:nk]).then_inc(taken_dve, 1)

        @block.scalar
        def _(act):
            def exps(n):
                st, b = steps[n], n % 2
                nk = P * (st.i + 1)
                act.wait_ge(bias_ready, n + 1)
                if n >= 2:
                    if pair:
                        act.wait_ge(weights_ready, n - 1)
                    else:
                        act.wait_ge(turned, turns * (n - 1))
                if n >= 4:
                    act.wait_ge(inverted, n - 3)
                for m in range(maps):
                    nc.scalar.activation(p[:, b, m, 0:nk], sc[b][:, m, 0:nk], ACT.Exp, bias=neg[:, b, m:m + 1],
                                         scale=scale, accum_out=total[:, n % 4, m:m + 1]).then_inc(exp_ready, 1)

            def take(n):
                for m in range(turns):
                    if (n * turns + m) % 2 == 0:
                        take_turned(act, n, m)

            exps(0)
            exps(1)
            take(0)
            for n in range(n_steps):
                if n + 2 < n_steps:
                    exps(n + 2)
                if n + 1 < n_steps:
                    take(n + 1)

        @block.vector
        def _(dve):
            chain = Chain(dve, step_dve)

            def maxima(n):
                st, b = steps[n], n % 2
                nk = P * (st.i + 1)
                dve.wait_ge(scores_ready, n + 1)
                chain(nc.vector.tensor_reduce(top[:, b, :], sc[b][:, :, 0:nk], X, ALU.max))
                if n >= 2:
                    dve.wait_ge(exp_ready, maps * (n - 1))
                nc.vector.tensor_scalar(neg[:, b, :], top[:, b, :], -scale, None, ALU.mult).then_inc(bias_ready, 1)

            def inverses(n):
                st, b, c = steps[n], n % 2, n % 4
                nk = P * (st.i + 1)
                dve.wait_ge(exp_ready, maps * (n + 1))
                if n >= 4:
                    dve.wait_ge(out_taken, n - 3)
                nc.vector.reciprocal(inv[:, c, :], total[:, c, :]).then_inc(inverted, 1)
                dve.wait_ge(inverted, n + 1)
                if gated:
                    chain(nc.vector.tensor_tensor(inv[:, c, :], inv[:, c, :], st.gate, ALU.mult))
                if pair:
                    chain(nc.vector.tensor_tensor(lam_inv[:, b, :], inv[:, c, 1:2], lam, ALU.mult))
                    chain(nc.vector.tensor_scalar(p[:, b, 1, 0:nk], p[:, b, 1, 0:nk], lam_inv[:, b, :], None, ALU.mult))
                    if n >= 2:
                        dve.wait_ge(turned, n - 1)
                    nc.vector.scalar_tensor_tensor(w[:, b, 0:nk], p[:, b, 0, 0:nk], inv[:, c, 0:1], p[:, b, 1, 0:nk],
                                                   ALU.mult, ALU.subtract).then_inc(weights_ready, 1)

            def take(n):
                for m in range(turns):
                    if (n * turns + m) % 2 == 1:
                        take_turned(dve, n, m)

            def output(n):
                st, b = steps[n], n % 2
                dve.wait_ge(values_ready, n + 1)
                for m in range(turns):
                    last = st.out(chain, ov[b][:, m * 64:(m + 1) * 64], inv[:, n % 4, m:m + 1], m)
                last.then_inc(out_taken, 1)

            maxima(0)
            maxima(1)
            inverses(0)
            take(0)
            for n in range(n_steps):
                if n + 1 < n_steps:
                    inverses(n + 1)
                if n + 2 < n_steps:
                    maxima(n + 2)
                if n + 1 < n_steps:
                    take(n + 1)
                output(n)




def condition_stage(k, a):
    nc = k.nc
    half, width = P // 2, COL // 2
    chunks = FIRST_MOD
    first_group = k.n_groups
    for n in range(chunks):
        k.last_group[k.chunk_no[("ada", n)]] = first_group + n + 1
    k.n_groups += chunks
    with ExitStack() as ctx:
        def sb(s, shape):
            return ctx.enter_context(nc.sbuf_tensor(s, shape, F32))

        def sem(s):
            return nc.alloc_semaphore(s)

        cond = k.cond
        c_col, cond_rows = sb("c_col", [P, ND]), sb("cond_rows", [P, ND, half])
        ada_b, first = sb("ada_b_row", [1, 2 * D]), sb("mod_first", [1, 2, D])
        loaded = {e: sem(f"small_{e}_loaded") for e in ("sp", "act")}
        loaded["pool"] = k.small_pool_loaded
        made, c_loaded, x_loaded = sem("constants_made"), sem("c_loaded"), sem("x_loaded")
        activated, spread = sem("cond_activated"), sem("cond_spread")
        taken = {e: sem(f"mod_taken_{e}") for e in ("act", "dve")}
        turned, step = sem("mod_turned"), sem("mod_step")
        bank = [ctx.enter_context(nc.psum_tensor(f"mod_bank{i}", [P, COL], F32)) for i in range(chunks)]
        turn_bank = ctx.enter_context(nc.psum_tensor("mod_turn_bank", [P, COL], F32))
        block = ctx.enter_context(nc.Block())
        share = {"sp": k.small[0::3], "act": k.small[1::3], "pool": k.small[2::3]}
        sp_loads = len(share["sp"]) + len(k.lru_blocks)

        def run(eng, e):
            for dst, src in share[e]:
                eng.dma_start(dst, src, allow_slow_non_contiguous=True).then_inc(loaded[e], 16)

        def outputs(n):
            part, at = n * COL // D, n * COL % D
            return first[:, part, at:at + width], first[:, part, at + width:at + COL]

        @block.sync
        def _(sp):
            sp.dma_start(c_col[:], column(a["c"][0]), allow_slow_non_contiguous=True).then_inc(c_loaded, 16)
            sp.dma_start(ada_b[:], a["ada_b"][:, 0:2 * D]).then_inc(c_loaded, 16)
            load_chunks(k, sp, None)
            sp.wait_ge(made, 3)
            for dst, src in k.lru_blocks:
                sp.dma_start(dst, src).then_inc(loaded["sp"], 16)
            load_chunks(k, sp, ("ada", 0))
            sp.dma_start(k.x[:], a["x"][0].rearrange("(t p) d -> p t d", p=P)).then_inc(x_loaded, 16)
            run(sp, "sp")
            load_chunks(k, sp, ("ada", chunks - 1))
            sp.wait_ge(loaded["sp"], 16 * sp_loads)
            sp.wait_ge(x_loaded, 16)

        @block.gpsimd
        def _(pool):
            run(pool, "pool")
            pool.wait_ge(loaded["pool"], 16 * len(share["pool"]))

        @block.tensor
        def _(pe):
            pe.wait_ge(made, 2)
            pe.wait_ge(spread, 1)
            for n in range(chunks):
                wait_chunk(k, pe, ("ada", n))
                (w,) = chunk_view(k, ("ada", n))
                for j in range(ND):
                    for h in range(2):
                        nc.tensor.matmul(bank[n][half * h:half * h + half, 0:width], cond_rows[:, j, :], w[:, j, width * h:width * h + width],
                                         start=(j == 0), stop=False)
                for h in range(2):
                    c0 = n * COL + width * h
                    mm = nc.tensor.matmul(bank[n][half * h:half * h + half, 0:width], k.ones[0:1, 0:half], ada_b[0:1, c0:c0 + width],
                                          start=False, stop=True)
                mm.then_inc(k.groups_done, 1)
            for e in taken:
                pe.wait_ge(taken[e], chunks)
            for part in range(2):
                for j in range(ND):
                    mm = nc.tensor.matmul(turn_bank[:, part * ND + j:part * ND + j + 1], first[0:1, part, j * P:(j + 1) * P],
                                          k.ones[0:1, 0:1], start=True, stop=True)
            mm.then_inc(turned, 1)

        def take(eng, e, h, copy):
            for n in range(chunks):
                eng.wait_ge(k.groups_done, first_group + n + 1)
                copy(outputs(n)[h], bank[n][half * h:half * h + 1, 0:width]).then_inc(taken[e], 1)

        @block.scalar
        def _(act):
            act.wait_ge(c_loaded, 32)
            nc.scalar.activation(cond[:], c_col[:], ACT.Silu).then_inc(activated, 1)
            run(act, "act")
            take(act, "act", 0, lambda dst, src: nc.scalar.activation(dst, src, ACT.Copy))
            act.wait_ge(loaded["act"], 16 * len(share["act"]))

        @block.vector
        def _(dve):
            chain = Chain(dve, step)
            nc.vector.memset(k.eps[:], EPS).then_inc(made, 1)
            nc.vector.memset(k.ones[:], 1.0).then_inc(made, 1)
            nc.vector.memset(k.lru_w[:], 0.0).then_inc(made, 1)
            dve.wait_ge(activated, 1)
            nc.vector.tensor_copy(cond_rows[:], cond[:].unsqueeze(2).to_broadcast([P, ND, half])).then_inc(spread, 1)
            take(dve, "dve", 1, nc.vector.tensor_copy)
            for e, count in (("sp", sp_loads), ("act", len(share["act"])), ("pool", len(share["pool"]))):
                dve.wait_ge(loaded[e], 16 * count)
            nc.vector.tensor_copy(k.ident_half[:], k.ident[:])
            nc.vector.tensor_copy(k.causal_half[:], k.causal_bias[:])
            dve.wait_ge(turned, 1)
            chain(nc.vector.tensor_copy(k.shift1[:], turn_bank[:, 0:ND]))
            chain(nc.vector.scalar_tensor_tensor(k.scale1[:], turn_bank[:, ND:2 * ND], 1.0, k.norm1[:], ALU.add, ALU.mult))


class Modulation:

    def __init__(self, k, a, ctx):
        nc = k.nc
        self.k, self.a, self.half, self.width = k, a, P // 2, COL // 2
        self.cond_rows, self.ada_b, self.norm2_row = (
            ctx.enter_context(nc.sbuf_tensor(n, shape, F32))
            for n, shape in (("cond_rows2", [P, ND, self.half]), ("ada_b_row2", [1, 4 * D]), ("norm2_row", [P, D])))
        self.rows_loaded, self.spread = nc.alloc_semaphore("mod2_rows_loaded"), nc.alloc_semaphore("mod2_spread")

    def beside(self, n0, n1, ctx):
        k, self.n0, self.n1 = self.k, n0, n1
        self.first_group = k.n_groups
        for n in range(n0, n1):
            k.last_group[k.chunk_no[("ada", n)]] = self.first_group + n - n0 + 1
        k.n_groups += n1 - n0
        self.bank = [ctx.enter_context(k.nc.psum_tensor(f"mod2_{n0}_bank{i}", [P, COL], F32)) for i in range(n1 - n0)]
        return self

    def sync(self, sp):
        if self.n0 == FIRST_MOD:
            sp.dma_start(self.ada_b[:], self.a["ada_b"][:, 2 * D:]).then_inc(self.rows_loaded, 16)
            sp.dma_start(self.norm2_row[:], row(self.a["norm2_g"][0])).then_inc(self.rows_loaded, 16)
        load_chunks(self.k, sp, ("ada", self.n1 - 1))

    def tensor(self, pe):
        k, nc, half, width = self.k, self.k.nc, self.half, self.width
        pe.wait_ge(self.rows_loaded, 32)
        pe.wait_ge(self.spread, 1)
        for n in range(self.n0, self.n1):
            wait_chunk(k, pe, ("ada", n))
            (w,) = chunk_view(k, ("ada", n))
            bank = self.bank[n - self.n0]
            for j in range(ND):
                for h in range(2):
                    nc.tensor.matmul(bank[half * h:half * h + half, 0:width], self.cond_rows[:, j, :], w[:, j, width * h:width * h + width],
                                     start=(j == 0), stop=False)
            for h in range(2):
                c0 = (n - FIRST_MOD) * COL + width * h
                mm = nc.tensor.matmul(bank[half * h:half * h + half, 0:width], k.ones[0:1, 0:half], self.ada_b[0:1, c0:c0 + width],
                                      start=False, stop=True)
            mm.then_inc(k.groups_done, 1)

    def gpsimd(self, pool):
        if self.n0 == FIRST_MOD:
            self.k.nc.gpsimd.tensor_copy(self.cond_rows[:], self.k.cond[:].unsqueeze(2).to_broadcast([P, ND, self.half])).then_inc(self.spread, 1)

    def scalar(self, act):
        k = self.k
        for n in range(self.n0, self.n1):
            act.wait_ge(k.groups_done, self.first_group + n - self.n0 + 1)
            part, at = (n - FIRST_MOD) * COL // D, n * COL % D
            for h in range(2):
                src = self.bank[n - self.n0][self.half * h:self.half * h + self.half, 0:self.width]
                for to in range(2):
                    k.nc.scalar.activation(k.mod[self.half * to:self.half * to + self.half, part, at + self.width * h:at + self.width * (h + 1)],
                                           src, ACT.Copy)


def project1_stage(k, tok, fm, glow, dxg):
    jobs = []

    def token_major(n, lo, width, dst0):
        w = split_chunk(k, ("in1", n))
        for t in range(NT):
            mm = [(k.hT[:, j, t * P:(t + 1) * P], w[:, j, lo:lo + width]) for j in range(ND)]
            jobs.append(Job(mm, P, width, copy_to(k, tok[:, t, dst0:dst0 + width]), engine_of(len(jobs)), ("in1", n)))

    def feature_major(n, lo, dst, rows=P):
        w = split_chunk(k, ("in1", n))
        mm = [(w[:, j, lo:lo + P], k.hT[:, j, :]) for j in range(ND)]

        def evac(e, chain, psum):
            return copy_to(k, dst)(e, chain, psum[0:rows, :])
        jobs.append(Job(mm, P, S, evac, engine_of(len(jobs)), ("in1", n)))

    for n in range(6):
        token_major(n, 0, NARROW, n * NARROW)
    feature_major(6, 0, fm[:, 0, :])
    feature_major(6, P, fm[:, 1, :])
    token_major(7, 0, NARROW, 1536)
    feature_major(8, 0, glow[0:C_RANK, :], C_RANK)
    token_major(8, C_RANK, P - C_RANK, CR)
    token_major(9, 0, P + C_RANK, CR + P - C_RANK)
    for j in range(4):
        feature_major(10 + j // 2, j % 2 * P, dxg[:, j, :])
    split_gemm_stage(k, "in1", jobs, last_key=("in1", len(IN1) - 1), norm=[(k.x, k.scale1, k.shift1)],
                     room=dxg[:, 2:4, :])


def lambda_stage(k, norm2_row):
    nc = k.nc
    with ExitStack() as ctx:
        dots = nc.alloc_semaphore("lam_dots")
        raised = nc.alloc_semaphore("lam_raised")
        step = nc.alloc_semaphore("lam_step")
        prod = ctx.enter_context(nc.sbuf_tensor("lam_prod", [P, 2, A_DK], F32))
        dot = ctx.enter_context(nc.sbuf_tensor("lam_dot", [P, 2], F32))
        e = ctx.enter_context(nc.sbuf_tensor("lam_exp", [P, 2], F32))
        block = ctx.enter_context(nc.Block())

        @block.vector
        def _(dve):
            chain = Chain(dve, step)
            chain(nc.vector.tensor_tensor(prod[:], k.lam_q[:], k.lam_k[:], ALU.mult))
            nc.vector.tensor_reduce(dot[:], prod[:], X, ALU.add).then_inc(dots, 1)
            chain(nc.vector.scalar_tensor_tensor(k.mod[:, 2, :], k.mod[:, 2, :], 1.0, norm2_row[:], ALU.add, ALU.mult))
            dve.wait_ge(raised, 1)
            chain(nc.vector.tensor_tensor(k.lam[:], e[:, 0:1], e[:, 1:2], ALU.subtract))
            chain(nc.vector.tensor_scalar(k.lam[:], k.lam[:], LAM_INIT, None, ALU.add))

        @block.scalar
        def _(act):
            act.wait_ge(dots, 1)
            nc.scalar.activation(e[:], dot[:], ACT.Exp).then_inc(raised, 1)


def gla_stages(k, tok, fm, glow, a):
    nc = k.nc
    qs = C_DK ** -0.5
    with ExitStack() as ctx:
        def sb(s, shape):
            return ctx.enter_context(nc.sbuf_tensor(f"gla_{s}", shape, F32))

        z, b, ex = sb("z", [P, S]), sb("b", [P, S]), sb("ex", [P, S])
        qin, kout = sb("qin", [P, S]), sb("kout", [P, S])
        qsub = sb("qsub", [P, S // SUB, C_HEADS, SUB])
        gemm_stage(k, "gla_gate", [Job([(k.c_wg2[0:C_RANK, :], glow[0:C_RANK, :])], P, S,
                                       copy_to(k, z[:], bias=k.c_bg[:]), "dve")], banks=1)
        with ExitStack() as inner:
            def sem(s):
                return nc.alloc_semaphore(f"gla_{s}")

            soft, cum, raised, zeroed, step, astep = sem("soft"), sem("cum"), sem("raised"), sem("zeroed"), sem("step"), sem("astep")
            diff = inner.enter_context(nc.sbuf_tensor("gla_diff", [P, S], F32))
            end = inner.enter_context(nc.sbuf_tensor("gla_end", [P, S], F32))
            block = inner.enter_context(nc.Block())

            @block.gpsimd
            def _(pool):
                nc.gpsimd.memset(qsub[:], 0.0).then_inc(zeroed, 1)
                nc.gpsimd.memset(k.gla_state[:], 0.0).then_inc(zeroed, 1)

            @block.scalar
            def _(act):
                chain = Chain(act, astep)
                chain(nc.scalar.activation(ex[:], z[:], ACT.Abs))
                chain(nc.scalar.activation(ex[:], ex[:], ACT.Exp, scale=-1.0))
                nc.scalar.activation(ex[:], ex[:], ACT.Ln, bias=k.ones[:, 0:1]).then_inc(soft, 1)
                act.wait_ge(cum, 1)
                nc.scalar.activation(qin[:], b[:], ACT.Exp).then_inc(raised, 1)
                for t in range(NT):
                    nc.scalar.activation(kout[:, t * P:(t + 1) * P], b[:, t * P:(t + 1) * P], ACT.Exp, scale=-1.0,
                                         bias=b[:, t * P + P - 1:t * P + P]).then_inc(raised, 1)
                nc.scalar.activation(k.gla_tile_decay[:], b[:].rearrange("p (t n) -> p t n", n=P)[:, :, P - 1],
                                     ACT.Exp).then_inc(raised, 1)
                act.wait_ge(cum, 2)
                nc.scalar.activation(diff[:], diff[:], ACT.Exp).then_inc(raised, 1)

            @block.vector
            def _(dve):
                chain = Chain(dve, step)
                dve.wait_ge(soft, 1)
                chain(nc.vector.scalar_tensor_tensor(z[:], z[:], 0.0, ex[:], ALU.min, ALU.subtract))
                chain(nc.vector.tensor_scalar(z[:], z[:], 1.0 / C_TAU, None, ALU.mult))
                chain(nc.vector.memset(end[:], 1.0))
                for t in range(NT):
                    c = slice(t * P, (t + 1) * P)
                    scan = nc.vector.tensor_tensor_scan(b[:, c], end[:, c], z[:, c], 0.0, ALU.mult, ALU.add)
                    if t < NT - 1:
                        chain(scan)
                scan.then_inc(cum, 1)
                dve.wait_ge(cum, 1)
                bs = b[:].rearrange("p (n s) -> p n s", s=SUB)
                ref = bs[:, :, SUB // 2:SUB // 2 + 1].to_broadcast([P, S // SUB, SUB])
                nc.vector.tensor_tensor(diff[:].rearrange("p (n s) -> p n s", s=SUB), bs, ref, ALU.subtract).then_inc(cum, 1)
                dve.wait_ge(raised, 1 + NT + 1)
                chain(nc.vector.scalar_tensor_tensor(qin[:], fm[:, 0, :], qs, qin[:], ALU.mult, ALU.mult))
                chain(nc.vector.tensor_tensor(kout[:], fm[:, 1, :], kout[:], ALU.mult))
                dve.wait_ge(raised, 1 + NT + 2)
                dve.wait_ge(zeroed, 2)
                for h in range(C_HEADS):
                    r = slice(h * C_DK, (h + 1) * C_DK)
                    chain(nc.vector.scalar_tensor_tensor(
                        qsub[r, :, h, :], fm[r, 0, :].rearrange("p (n s) -> p n s", s=SUB), qs,
                        diff[r, :].rearrange("p (n s) -> p n s", s=SUB), ALU.mult, ALU.mult))

        with ExitStack() as inner:
            def sem(s):
                return nc.alloc_semaphore(f"gla2_{s}")

            def isb(s, shape):
                return inner.enter_context(nc.sbuf_tensor(f"gla2_{s}", shape, F32))

            def ps(s):
                return inner.enter_context(nc.psum_tensor(f"gla2_{s}", [P, COL], F32))

            spread, raised, keys, att_ready, masked, turned, copied, state_ready, updated, out_ready, out_taken, step = (
                sem(s) for s in ("spread", "raised", "keys", "att_ready", "masked", "turned", "copied", "state_ready",
                                 "updated", "out_ready", "out_taken", "step"))
            ksub = isb("ksub", [P, 2, NSUB, P])
            att = isb("att", [P, 2, C_HEADS, P])
            kt = isb("kt", [P, 2, P])
            att_bank, kt_bank, o_bank = ([ps(f"{s}_bank{i}") for i in range(2)] for s in ("att", "kt", "o"))
            u_bank = ps("u_bank")
            block = inner.enter_context(nc.Block())
            cv = 1536

            @block.scalar
            def _(act):
                def raise_tile(t):
                    act.wait_ge(spread, t + 1)
                    nc.scalar.activation(ksub[:, t % 2], ksub[:, t % 2], ACT.Exp, scale=-1.0).then_inc(raised, 1)

                raise_tile(0)
                raise_tile(1)
                for t in range(NT):
                    if t + 2 < NT:
                        raise_tile(t + 2)
                    act.wait_ge(out_ready, t + 1)
                    nc.scalar.activation(tok[:, t, OUT_C:OUT_C + 256], o_bank[t % 2][:, 0:256], ACT.Copy).then_inc(out_taken, 1)

            @block.vector
            def _(dve):
                chain = Chain(dve, step)

                def spread_tile(t):
                    if t >= 2:
                        dve.wait_ge(att_ready, t - 1)
                    bt = b[:, t * P:(t + 1) * P]
                    ref = bt.rearrange("p (n s) -> p n s", s=SUB)[:, :, SUB // 2:SUB // 2 + 1].to_broadcast([P, NSUB, P])
                    chain(nc.vector.tensor_tensor(ksub[:, t % 2], bt.unsqueeze(1).to_broadcast([P, NSUB, P]), ref, ALU.subtract))
                    nc.vector.tensor_scalar(ksub[:, t % 2], ksub[:, t % 2], -DECAY_CLAMP, None, ALU.max).then_inc(spread, 1)

                def key_tile(t):
                    dve.wait_ge(raised, t + 1)
                    nc.vector.tensor_tensor(ksub[:, t % 2], ksub[:, t % 2],
                                            fm[:, 1, t * P:(t + 1) * P].unsqueeze(1).to_broadcast([P, NSUB, P]),
                                            ALU.mult).then_inc(keys, 1)

                spread_tile(0)
                spread_tile(1)
                key_tile(0)
                for t in range(NT):
                    if t + 1 < NT:
                        key_tile(t + 1)
                    dve.wait_ge(att_ready, t + 1)
                    if t >= 2:
                        dve.wait_ge(out_ready, t - 1)
                    for h in range(C_HEADS):
                        nc.vector.tensor_tensor(
                            att[:, t % 2, h, :].rearrange("p (n s) -> p n s", s=SUB),
                            att_bank[t % 2][:].rearrange("p (n h s) -> p n h s", h=C_HEADS, s=SUB)[:, :, h, :],
                            k.upper_incl[:].rearrange("p (n s) -> p n s", s=SUB), ALU.mult).then_inc(masked, 1)
                    dve.wait_ge(turned, t + 1)
                    if t >= 2:
                        dve.wait_ge(state_ready, t - 1)
                    nc.vector.tensor_copy(kt[:, t % 2], kt_bank[t % 2][:, 0:P]).then_inc(copied, 1)
                    if t + 2 < NT:
                        spread_tile(t + 2)
                    dve.wait_ge(state_ready, t + 1)
                    dve.wait_ge(out_ready, t + 1)
                    for h in range(C_HEADS):
                        r, e = slice(h * C_DK, (h + 1) * C_DK), slice(h * C_DV, (h + 1) * C_DV)
                        nc.vector.scalar_tensor_tensor(k.gla_state[r, e], k.gla_state[r, e], k.gla_tile_decay[r, t:t + 1],
                                                       u_bank[r, e], ALU.mult, ALU.add).then_inc(updated, 1)

            @block.tensor
            def _(pe):
                def att_tile(t):
                    pe.wait_ge(keys, t + 1)
                    if t >= 2:
                        pe.wait_ge(masked, C_HEADS * (t - 1))
                    for i in range(NSUB):
                        mm = nc.tensor.matmul(att_bank[t % 2][:, i * 64:(i + 1) * 64], ksub[:, t % 2, i, :],
                                              qsub[:, t * NSUB + i].rearrange("p h s -> p (h s)"), start=True, stop=True)
                    mm.then_inc(att_ready, 1)
                    if t >= 2:
                        pe.wait_ge(copied, t - 1)
                    nc.tensor.transpose(kt_bank[t % 2][:, 0:P], kout[:, t * P:(t + 1) * P], k.ident[:]).then_inc(turned, 1)

                att_tile(0)
                for t in range(NT):
                    if t + 1 < NT:
                        att_tile(t + 1)
                    o = o_bank[t % 2]
                    if t >= 2:
                        pe.wait_ge(out_taken, t - 1)
                    if t >= 1:
                        pe.wait_ge(updated, C_HEADS * t)
                    nc.tensor.matmul(o[:, 0:256], qin[:, t * P:(t + 1) * P], k.gla_state[:], start=True, stop=True)
                    for h in range(C_HEADS):
                        pe.wait_ge(masked, C_HEADS * t + h + 1)
                        mm = nc.tensor.matmul(o[:, h * 64:(h + 1) * 64], att[:, t % 2, h, :], tok[:, t, cv + h * 64:cv + (h + 1) * 64],
                                              start=False, stop=True, skip_group_check=True)
                    mm.then_inc(out_ready, 1)
                    pe.wait_ge(copied, t + 1)
                    nc.tensor.matmul(u_bank[:, 0:256], kt[:, t % 2], tok[:, t, cv:cv + 256], start=True, stop=True).then_inc(state_ready, 1)


def gla_gate_stage(k, tok):
    nc = k.nc
    with ExitStack() as ctx:
        opened = nc.alloc_semaphore("gla_opened")
        scaled = nc.alloc_semaphore("gla_scaled")
        r = ctx.enter_context(nc.sbuf_tensor("gla_silu", [P, NT, 256], F32))
        block = ctx.enter_context(nc.Block())

        @block.scalar
        def _(act):
            nc.scalar.activation(r[:], tok[:, :, CR:CR + 256], ACT.Silu).then_inc(opened, 1)

        @block.vector
        def _(dve):
            dve.wait_ge(opened, 1)
            nc.vector.tensor_tensor(tok[:, :, OUT_C:OUT_C + 256], tok[:, :, OUT_C:OUT_C + 256], r[:], ALU.mult).then_inc(scaled, 1)


def lru_stages(k, dxg, beside):
    nc = k.nc
    with ExitStack() as ctx:
        def sb(s, shape):
            return ctx.enter_context(nc.sbuf_tensor(f"lru_{s}", shape, F32))

        xc, gates = sb("xc", [P, 2, S]), sb("gates", [P, 2, 2, S])
        with ExitStack() as inner:
            step = nc.alloc_semaphore("lru_step")
            block = inner.enter_context(nc.Block())

            @block.vector
            def _(dve):
                chain = Chain(dve, step)
                for j in range(2):
                    chain(nc.vector.tensor_scalar(xc[:, j, :], dxg[:, j, :], k.conv_w[:, CONV_W - 1, j:j + 1],
                                                  k.conv_b[:, j:j + 1], ALU.mult, ALU.add))
                    for back in range(1, CONV_W):
                        chain(nc.vector.scalar_tensor_tensor(xc[:, j, back:], dxg[:, j, :S - back],
                                                             k.conv_w[:, CONV_W - 1 - back, j:j + 1], xc[:, j, back:],
                                                             ALU.mult, ALU.add))
        jobs = [Job([(k.lru_w[:, g, j, :], xc[:, j, :])], P, S, copy_to(k, gates[:, g, j, :], bias=k.lru_b[:, g, j:j + 1]),
                    "dve") for g in range(2) for j in range(2)]
        gemm_stage(k, "lru_gates", jobs)
        with ExitStack() as inner:
            def sem(s):
                return nc.alloc_semaphore(f"lru_{s}")

            def isb(s, shape):
                return inner.enter_context(nc.sbuf_tensor(f"lru2_{s}", shape, F32))

            astep, step, opened, logged, decayed, lost, rooted = (
                sem(s) for s in ("astep", "step2", "opened", "logged", "decayed", "lost", "rooted"))
            la, th, root = isb("la", [P, 2, S]), isb("th", [P, 2, S]), isb("root", [P, 2, S])
            lam = isb("lam", [P, 2])
            den = isb("den", [P, 2, S])
            opened_beside = beside(inner)
            block = inner.enter_context(nc.Block())
            idle_engines(block, opened_beside)

            @block.scalar
            def _(act):
                chain = Chain(act, astep)
                chain(nc.scalar.activation(lam[:], k.lru_lam[:], ACT.Abs))
                chain(nc.scalar.activation(lam[:], lam[:], ACT.Exp, scale=-1.0))
                nc.scalar.activation(lam[:], lam[:], ACT.Ln, bias=k.ones[:, 0:1]).then_inc(opened, 1)
                for g in range(2):
                    nc.scalar.activation(gates[:, g], gates[:, g], ACT.Sigmoid).then_inc(opened, 1)
                for j in range(2):
                    act.wait_ge(logged, j + 1)
                    nc.scalar.activation(th[:, j, :], la[:, j, :], ACT.Tanh, scale=-1.0).then_inc(decayed, 1)
                for j in range(2):
                    nc.scalar.activation(la[:, j, :], la[:, j, :], ACT.Exp).then_inc(decayed, 1)
                nc.scalar.activation(dxg[:, 2:4, :], dxg[:, 2:4, :], ACT.Gelu_apprx_tanh).then_inc(decayed, 1)
                for j in range(2):
                    act.wait_ge(lost, j + 1)
                    nc.scalar.activation(root[:, j, :], th[:, j, :], ACT.Sqrt).then_inc(rooted, 1)
                opened_beside.scalar(act)

            @block.vector
            def _(dve):
                chain = Chain(dve, step)
                dve.wait_ge(opened, 1)
                chain(nc.vector.scalar_tensor_tensor(lam[:], k.lru_lam[:], 0.0, lam[:], ALU.min, ALU.subtract))
                chain(nc.vector.tensor_scalar(lam[:], lam[:], 8.0, None, ALU.mult))
                dve.wait_ge(opened, 2)
                for j in range(2):
                    nc.vector.tensor_scalar(la[:, j, :], gates[:, 0, j, :], lam[:, j:j + 1], None, ALU.mult).then_inc(logged, 1)
                dve.wait_ge(opened, 3)
                chain(nc.vector.tensor_tensor(xc[:], xc[:], gates[:, 1], ALU.mult))
                for j in range(2):
                    dve.wait_ge(decayed, j + 1)
                    chain(nc.vector.tensor_scalar(den[:, j, :], th[:, j, :], 1.0, None, ALU.add))
                    chain(nc.vector.reciprocal(den[:, j, :], den[:, j, :]))
                    nc.vector.scalar_tensor_tensor(th[:, j, :], th[:, j, :], 2.0, den[:, j, :], ALU.mult, ALU.mult).then_inc(lost, 1)
                dve.wait_ge(decayed, 5)
                for j in range(2):
                    dve.wait_ge(rooted, j + 1)
                    chain(nc.vector.tensor_tensor(xc[:, j, :], xc[:, j, :], root[:, j, :], ALU.mult))
                    chain(nc.vector.tensor_tensor_scan(th[:, j, :], la[:, j, :], xc[:, j, :], 0.0, ALU.mult, ALU.add))
                    chain(nc.vector.tensor_tensor(dxg[:, 2 + j, :], th[:, j, :], dxg[:, 2 + j, :], ALU.mult))


def residual(k, t, n, gate=None, width=COL):
    nc = k.nc
    cols = slice(n * width, (n + 1) * width)

    def evac(e, chain, psum):
        if gate is None:
            return nc.vector.tensor_tensor(k.x[:, t, cols], k.x[:, t, cols], psum, ALU.add)
        chain(nc.vector.tensor_tensor(k.gated[:, 0:width], psum, gate[:, cols], ALU.mult))
        return nc.vector.tensor_tensor(k.x[:, t, cols], k.x[:, t, cols], k.gated[:, 0:width], ALU.add)
    return evac


def out_stage(k, name, keys, width, gate=None, norm=None, room=None):
    jobs = []
    for n, key in enumerate(keys):
        w = split_chunk(k, key)
        for t in range(NT):
            mm = [(k.hT[:, j, t * P:(t + 1) * P], w[:, j, :]) for j in range(ND)]
            jobs.append(Job(mm, P, width, residual(k, t, n, gate, width), "dve", key))
    split_gemm_stage(k, name, jobs, last_key=keys[-1], norm=norm, room=room)


@contextmanager
def split_hT(k, name):
    with k.nc.sbuf_tensor(f"{name}_hi", [P, ND, S], F32R) as hi, k.nc.sbuf_tensor(f"{name}_lo", [P, ND, S], F32R) as lo:
        k.hT = Halves(hi, lo)
        yield


def part1(k, a):
    nc = k.nc
    condition_stage(k, a)
    narrow = [P, 2, 2, ND * NARROW]
    with ExitStack() as ctx:
        tok = ctx.enter_context(nc.sbuf_tensor("tok1", [P, NT, 2048], F32))
        fm = ctx.enter_context(nc.sbuf_tensor("fm1", [P, 2, S], F32))
        glow = ctx.enter_context(nc.sbuf_tensor("glow1", [P, S], F32))
        dxg = ctx.enter_context(nc.sbuf_tensor("dxg1", [P, 4, S], F32))
        with split_hT(k, "hT_in1"):
            with nc.sbuf_tensor("in1_w", narrow, F32R) as k.w_split:
                project1_stage(k, tok, fm, glow, dxg)
        with ExitStack() as rest:
            modulation = Modulation(k, a, rest)
            lru_stages(k, dxg, lambda ctx: modulation.beside(FIRST_MOD, FIRST_MOD + 4, ctx))

            def heads(c0, w):
                return tok[:, :, c0:c0 + 256].rearrange("p t (n w) -> p t n w", w=w)
            groups = [(heads(0, A_DK), k.a_q_gain[:]), (heads(256, A_DK), k.a_k_gain[:]),
                      (heads(768, B_DK), k.b_q_gain[:]), (heads(1024, B_DK), k.b_k_gain[:])]
            rms_stage(k, "qk_norm", groups, lambda ctx: modulation.beside(FIRST_MOD + 4, 6 * D // COL, ctx))
            lambda_stage(k, modulation.norm2_row)
        with nc.sbuf_tensor("qk1", [P, 8, S], F32) as qk:
            transpose_stage(k, "turn_qk", [(columns_of(tok, c0, P), qk[:, j, :], None, None)
                                           for j, c0 in enumerate((0, 128, 256, 384, 768, 896, 1024, 1152))])

            def diff_step(h, i):
                r = [slice(64 * (h % 2) + 32 * m, 64 * (h % 2) + 32 * m + 32) for m in range(2)]

                def out(chain, psum, inv, m):
                    return nc.vector.tensor_copy(tok[:, i, OUT_A + h * 64:OUT_A + (h + 1) * 64], psum)
                return Step(i=i, q=[qk[r[m], h // 2, i * P:(i + 1) * P] for m in range(2)],
                                       k=[qk[r[m], 2 + h // 2, :] for m in range(2)],
                                       v=lambda m, j: tok[:, j, 512 + h * 64:512 + (h + 1) * 64], out=out)

            def moba_step(g, i):
                r = [slice(64 * m, 64 * m + 64) for m in range(2)]

                def out(chain, psum, inv, m):
                    h = 2 * g + m
                    return nc.vector.tensor_scalar(tok[:, i, OUT_B + h * 64:OUT_B + (h + 1) * 64], psum, inv, None, ALU.mult)
                return Step(i=i, q=[qk[r[m], 4 + g, i * P:(i + 1) * P] for m in range(2)],
                                       k=[qk[r[m], 6 + g, :] for m in range(2)],
                                       v=lambda m, j: tok[:, j, 1280 + (2 * g + m) * 64:1280 + (2 * g + m + 1) * 64], out=out)

            attention_stage(k, "diff", [diff_step(h, i) for h in range(A_HEADS) for i in tiles(h)], A_DK ** -0.5, True, k.lam[:])
            attention_stage(k, "moba", [moba_step(g, i) for g in range(2) for i in tiles(g)], B_DK ** -0.5, False)
        gla_stages(k, tok, fm, glow, a)
        rms_stage(k, "head_norm", [(tok[:, :, c0:c0 + 256].rearrange("p t (n w) -> p t n w", w=w), gain[:])
                                   for c0, w, gain in ((OUT_A, A_DV, k.a_out_gain), (OUT_C, C_DV, k.c_out_gain))])
        gla_gate_stage(k, tok)
        with split_hT(k, "hT_out1"):
            split_transpose_stage(k, "turn_mix", [(columns_of(tok, c0 + j * P, P), k.hT[:, 2 * g + j, :], 1.0 - LAM_INIT if g == 0 else 1.0)
                                                  for g, c0 in enumerate((OUT_A, OUT_B, OUT_C)) for j in range(2)],
                                  [(dxg[:, 2 + j, :], k.hT[:, 6 + j, :]) for j in range(2)])
            with nc.sbuf_tensor("out1_w", narrow, F32R) as k.w_split, nc.sbuf_tensor("gated", [P, NARROW], F32) as k.gated:
                out_stage(k, "out1", [("out1", n) for n in range(D // NARROW)], NARROW, k.mod[:, 0, :])




def second_norm_stages(k, h2_dram):
    nc = k.nc
    with nc.sbuf_tensor("h2", [P, NT, D], F32) as h2:
        norm_rows_stage(k, "norm2", k.x, h2, k.mod[:, 2, :], k.mod[:, 1, :], h2_dram, k.hT)


def route_stages(k, a):
    nc = k.nc
    with ExitStack() as ctx:
        def sb(s, shape, dt=F32):
            return ctx.enter_context(nc.sbuf_tensor(f"route_{s}", shape, dt))

        def sem(s):
            return nc.alloc_semaphore(f"route_{s}")

        def ps(s, n=COL):
            return ctx.enter_context(nc.psum_tensor(f"route_{s}", [P, n], F32))

        logits = sb("logits", [P, NT, NE])
        best, best_id = sb("best", [P, NT, 8]), sb("best_id", [P, NT, 8], U32)
        ids = sb("ids", [P, NT, TOPK])
        e, total = sb("e", [P, NT, TOPK]), sb("total", [P, NT])
        hot = sb("hot", [P, NT, TOPK, NE])
        mask = sb("mask", [P, NT, NE])
        count, blocks, ends, start = sb("count", [P, NE]), sb("blocks", [P, NE]), sb("ends", [P, NE]), sb("start", [P, NE])
        place = sb("place", [P, NT, NE])
        prod = sb("prod", [P, NT, TOPK, NE])
        dest, dest_i = sb("dest", [P, NT, TOPK]), sb("dest_i", [P, NT * TOPK], I32)
        number, spare, number_i = sb("number", [P, MAXB + 1]), sb("spare", [P, MAXB + 1]), sb("number_i", [P, MAXB + 1], I32)
        row_i, blk_i = sb("row_i", [P, NT * TOPK], I32), sb("blk_i", [P, NT * TOPK], I32)
        row_f, blk_f = sb("row_f", [P, NT * TOPK]), sb("blk_f", [P, NT * TOPK])
        row_hot, blk_hot = sb("row_hot", [P, NT * TOPK, P]), sb("blk_hot", [P, NT * TOPK, MAXB + 1])
        step, logits_ready, masked, ranked, scaled, raised, rows_ready, lists_ready = (
            sem(s) for s in ("step", "logits", "masked", "ranked", "scaled", "raised", "rows", "lists"))
        l_bank, r_bank, c_bank, t_bank = ps("l_bank"), ps("r_bank"), ps("c_bank"), ps("t_bank")
        block = ctx.enter_context(nc.Block())

        @block.sync
        def _(sp):
            for c in range(CHUNKS):
                sp.dma_start(k.expert_chunk(c, 0), expert_source(a, 0, c)).then_inc(k.expert_loaded[c], 16)

        @block.tensor
        def _(pe):
            for t in range(NT):
                out = l_bank[:, t * NE:(t + 1) * NE]
                for j in range(ND):
                    nc.tensor.matmul(out, k.hT[:, j, t * P:(t + 1) * P], k.router_w[:, j, :], start=(j == 0), stop=False)
                mm = nc.tensor.matmul(out, k.ones[0:1, :], k.router_b[0:1, :], start=False, stop=True)
            mm.then_inc(logits_ready, 1)
            pe.wait_ge(masked, 1)
            for t in range(NT):
                for s in range(t + 1):
                    nc.tensor.matmul(r_bank[:, t * NE:(t + 1) * NE], k.upper_strict[:] if s == t else k.ones[:], mask[:, s, :],
                                     start=(s == 0), stop=(s == t))
            for s in range(NT):
                mm = nc.tensor.matmul(c_bank[:, 0:NE], k.ones[:], mask[:, s, :], start=(s == 0), stop=(s == NT - 1))
            mm.then_inc(ranked, 1)
            for n in range(NT * TOPK):
                pe.wait_ge(rows_ready, 2 * n + 2)
                mm = nc.tensor.matmul(t_bank[:, 0:MAXB + 1], row_hot[:, n, :], blk_hot[:, n, :], start=(n == 0), stop=(n == NT * TOPK - 1))
            mm.then_inc(lists_ready, 1)

        @block.scalar
        def _(act):
            act.wait_ge(scaled, 1)
            nc.scalar.activation(e[:], e[:], ACT.Exp).then_inc(raised, 1)

        @block.vector
        def _(dve):
            chain = Chain(dve, step)
            dve.wait_ge(logits_ready, 1)
            chain(nc.vector.tensor_copy(logits[:], l_bank[:, 0:NT * NE].rearrange("p (t e) -> p t e", e=NE)))
            for t in range(NT):
                chain(nc.vector.max(best[:, t, :], logits[:, t, :]))
                chain(nc.vector.max_index(best_id[:, t, :], best[:, t, :], logits[:, t, :]))
            nc.vector.tensor_tensor(e[:], best[:, :, 0:TOPK], best[:, :, 0:1].to_broadcast([P, NT, TOPK]), ALU.subtract).then_inc(scaled, 1)
            chain(nc.vector.tensor_copy(ids[:], best_id[:, :, 0:TOPK]))
            for t in range(NT):
                chain(nc.vector.tensor_tensor(hot[:, t], k.iota[:, 0:NE].unsqueeze(1).to_broadcast([P, TOPK, NE]),
                                              ids[:, t, :].unsqueeze(2).to_broadcast([P, TOPK, NE]), ALU.is_equal))
            nc.vector.tensor_reduce(mask[:], hot[:].rearrange("p t k e -> p t e k"), X, ALU.add).then_inc(masked, 1)
            dve.wait_ge(raised, 1)
            chain(nc.vector.tensor_reduce(total[:], e[:], X, ALU.add))
            chain(nc.vector.reciprocal(total[:], total[:]))
            chain(nc.vector.tensor_tensor(k.gates[:], e[:], total[:].unsqueeze(2).to_broadcast([P, NT, TOPK]), ALU.mult))
            dve.wait_ge(ranked, 1)
            chain(nc.vector.tensor_copy(count[:], c_bank[:, 0:NE]))
            chain(nc.vector.tensor_scalar(blocks[:], count[:], 0.0, None, ALU.is_gt))
            for n in range(1, S // BR):
                chain(nc.vector.scalar_tensor_tensor(blocks[:], count[:], float(n * BR), blocks[:], ALU.is_gt, ALU.add))
            chain(nc.vector.tensor_tensor_scan(ends[:], k.ones[:, 0:NE], blocks[:], 0.0, ALU.mult, ALU.add))
            chain(nc.vector.tensor_tensor(start[:], ends[:], blocks[:], ALU.subtract))
            chain(nc.vector.tensor_copy(k.first[:, 0:NE], start[0:1, :]))
            chain(nc.vector.tensor_copy(k.first[:, NE:], ends[0:1, NE - 1:]))
            chain(nc.vector.tensor_scalar(start[:], start[:], float(BR), None, ALU.mult))
            chain(nc.vector.tensor_tensor(place[:], r_bank[:, 0:NT * NE].rearrange("p (t e) -> p t e", e=NE),
                                          start[:].unsqueeze(1).to_broadcast([P, NT, NE]), ALU.add))
            for t in range(NT):
                chain(nc.vector.tensor_tensor(prod[:, t], hot[:, t], place[:, t, :].unsqueeze(1).to_broadcast([P, TOPK, NE]), ALU.mult))
            chain(nc.vector.tensor_reduce(dest[:], prod[:], X, ALU.add))
            chain(nc.vector.tensor_copy(dest_i[:], dest[:].rearrange("p t k -> p (t k)")))
            chain(nc.vector.tensor_single_scalar(row_i[:], dest_i[:], BR - 1, ALU.bitwise_and))
            chain(nc.vector.tensor_single_scalar(blk_i[:], dest_i[:], int(math.log2(BR)), ALU.arith_shift_right))
            chain(nc.vector.tensor_copy(row_f[:], row_i[:]))
            chain(nc.vector.tensor_copy(blk_f[:], blk_i[:]))
            for n in range(NT * TOPK):
                nc.vector.tensor_scalar(row_hot[:, n, :], k.row_no[:], row_f[:, n:n + 1], None, ALU.is_equal).then_inc(rows_ready, 1)
                nc.vector.tensor_scalar(blk_hot[:, n, :], k.iota[:, 0:MAXB + 1], blk_f[:, n:n + 1], k.place_no[:, n:n + 1],
                                        ALU.is_equal, ALU.mult).then_inc(rows_ready, 1)
            dve.wait_ge(lists_ready, 1)
            chain(nc.vector.tensor_copy(number[:], t_bank[:, 0:MAXB + 1]))
            chain(nc.vector.tensor_scalar(spare[:], number[:], 0.0, k.spare_no[:], ALU.is_equal, ALU.mult))
            chain(nc.vector.scalar_tensor_tensor(spare[:], spare[:], -1.0, number[:], ALU.add, ALU.add))
            chain(nc.vector.tensor_scalar(spare[:], spare[:], 2.0, k.half_no[:], ALU.mult, ALU.add))
            chain(nc.vector.tensor_copy(k.row_place[:], spare[:]))
            chain(nc.vector.tensor_scalar(number[:], number[:], -1.0, 0.0, ALU.add, ALU.max))
            chain(nc.vector.tensor_copy(number_i[:], number[:]))
            chain(nc.vector.tensor_single_scalar(number_i[:], number_i[:], 2, ALU.arith_shift_right))
            chain(nc.vector.tensor_copy(number[:], number_i[:]))
            chain(nc.vector.tensor_scalar(number[:], number[:], 2.0, k.half_no[:], ALU.mult, ALU.add))
            chain(nc.vector.tensor_copy(k.row_token[:], number[:]))


CHUNKS = 6
TWICE = 2


def expert_source(a, e, c):
    if c < 4:
        col = (c % 2) * FF + (c // 2) * COL
        src = a["exp_w_up"][0].rearrange("e (k p) n -> e p k n", p=P)[bass.ds(e, 1), :, :, col:col + COL]
    else:
        src = a["exp_w_down"][0].rearrange("e (k p) n -> e p k n", p=P)[bass.ds(e, 1), :, 4 * (c - 4):4 * (c - 3), :]
    return src.rearrange("e p k n -> (e p) k n")


def expert_stage(k, a, h2_dram, y_dram):
    nc = k.nc
    halves = [slice(BR * h, BR * h + BR) for h in range(2)]
    with ExitStack() as ctx:
        def sem(s):
            return nc.alloc_semaphore(f"moe_{s}")

        def sb(s, shape, dt=F32):
            return ctx.enter_context(nc.sbuf_tensor(f"moe_{s}", shape, dt))

        def ps(s):
            return ctx.enter_context(nc.psum_tensor(f"moe_{s}", [P, COL], F32))

        k.expert_w2 = sb("w2", [P, TWICE * SLOT])
        chunk = [[k.expert_chunk(c, u) for c in range(CHUNKS)] for u in range(2)]
        loaded = k.expert_loaded
        rows, y = k.hT[:, 0, :], k.hT[:, 1, :]
        rowsT, hidT = (k.hT[:, n, :].rearrange("p (j r) -> p j r", r=P) for n in (2, 3))
        gate, lin, sig, hid = (k.hT[:, n, :].rearrange("p (h n) -> p h n", n=UNITS) for n in range(4, 8))
        index, place = sb("index", [P, 1], U32), sb("place", [P, 1], U32)
        used_mod = k.mod[:, 0:3, :].rearrange("p n d -> p (n d)")
        bias, bias_row = sb("bias", [P, 3 * COL]), [used_mod[0:1, h * 3 * COL:(h + 1) * 3 * COL] for h in range(2)]
        bias_loaded, bias_spread, indexed, waited = (sem(s) for s in ("bias_loaded", "bias_spread", "indexed", "waited"))
        chunk_free = sem("chunk_free")
        gathered, y_stored = k.gathered, k.y_stored
        rows_turned, rows_taken = sem("rows_turned"), sem("rows_taken")
        chunk_done, gate_ready, sig_ready, hid_ready, up_taken = sem("chunk_done"), sem("gate"), sem("sig"), sem("hid"), sem("up_taken")
        hid_turned, hid_taken = sem("hid_turned"), sem("hid_taken")
        y_ready, y_free, step = sem("y_ready"), sem("y_free"), sem("step")
        up = [ps(f"up{c}") for c in range(4)]
        down = ps("down")
        turn_r, turn_h = ps("turn_rows"), [ps(f"turn_hid{c}") for c in range(2)]
        block = ctx.enter_context(nc.Block())
        b_up = a["exp_b_up"][0].rearrange("e (s h n) -> e s h n", h=2, n=UNITS)
        b_down = a["exp_b_down"][0]
        h2_halves = h2_dram.rearrange("s (h n) -> (s h) n", h=2)
        y_halves = y_dram.rearrange("s (h n) -> (s h) n", h=2)

        def first_block(eng, e):
            return eng.value_load(k.first[0:1, bass.ds(e, 1)], min_val=0, max_val=MAXB)

        @block.sync
        def _(sp):
            def load_bias(e):
                for h in range(2):
                    sp.dma_start(bias_row[h][:, 0:2 * COL].rearrange("p (s n) -> p s n", n=UNITS), b_up[bass.ds(e, 1), :, h, :]).then_inc(bias_loaded, 16)
                    sp.dma_start(bias_row[h][:, 2 * COL:], b_down[bass.ds(e, 1), h * COL:(h + 1) * COL]).then_inc(bias_loaded, 16)

            def load(e, u):
                sp.wait_ge(bias_spread, e * 2)
                load_bias(e)
                last_but_one, last = first_block(sp, e - 1), first_block(sp, e)
                for c in range(CHUNKS):
                    sp.wait_ge(chunk_done, (last_but_one if c < TWICE else last) * CHUNKS + (c + 1))
                    sp.sem_inc(chunk_free, 1)
                    sp.wait_ge(loaded[(c - 2) % CHUNKS], e * 16 + (16 if c >= 2 else 0))
                    sp.dma_start(k.expert_chunk(c, u), expert_source(a, e, c)).then_inc(loaded[c], 16)

            load_bias(0)
            with sp.Fori(0, NE // 2 - 1) as i:
                load(i * 2 + 1, 1)
                load(i * 2 + 2, 0)
            load(NE - 1, 1)

        @block.gpsimd
        def _(pool):
            def gather(b, copies):
                nc.gpsimd.tensor_copy(index[:], k.row_token[:, bass.ds(b, 1)]).then_inc(indexed, 1)
                pool.wait_ge(indexed, copies)
                pool.sem_inc(waited, 1)
                pool.indirect_dma_start(rows, None, h2_halves,
                                        bass.IndirectOffsetOnAxis(ap=index[:], axis=0)).then_inc(gathered, 16)

            def scatter(b, copies, made):
                nc.gpsimd.tensor_copy(place[:], k.row_place[:, bass.ds(b, 1)]).then_inc(indexed, 1)
                pool.wait_ge(indexed, copies)
                pool.wait_ge(y_ready, made)
                pool.sem_inc(waited, 1)
                pool.indirect_dma_start(y_halves, bass.IndirectOffsetOnAxis(ap=place[:], axis=0), y, None).then_inc(y_stored, 16)

            gather(0, 1)
            scatter(MAXB, 2, 1)
            with pool.Fori(0, NE) as e:
                pool.wait_ge(bias_loaded, e * 64 + 64)
                pool.wait_ge(y_ready, first_block(pool, e) + 1)
                pool.sem_inc(waited, 1)
                nc.gpsimd.partition_broadcast(bias[:], bias_row[1]).then_inc(bias_spread, 1)
                pool.wait_ge(bias_spread, e * 2 + 1)
                pool.sem_inc(waited, 1)
                nc.gpsimd.partition_broadcast(bias[0:BR, :], bias_row[0], channels=BR).then_inc(bias_spread, 1)
                with pool.Fori(first_block(pool, e), first_block(pool, e + 1)) as b:
                    pool.wait_ge(rows_turned, b + 1)
                    gather(b + 1, b * 2 + 3)
                    pool.wait_ge(y_stored, b * 16 + 16)
                    pool.sem_inc(y_free, 1)
                    scatter(b, b * 2 + 4, b + 2)
            blocks = first_block(pool, NE)
            pool.wait_ge(gathered, blocks * 16 + 16)
            pool.sem_inc(waited, 1)
            pool.wait_ge(y_stored, blocks * 16 + 16)
            pool.sem_inc(waited, 1)

        @block.tensor
        def _(pe):
            def turn_rows():
                for j in range(4):
                    tr = nc.tensor.transpose(turn_r[:, j * P:(j + 1) * P], rows[:, j * P:(j + 1) * P], k.ident[:])
                tr.then_inc(rows_turned, 1)

            def up_chunk(e, u, b, c):
                pe.wait_ge(loaded[c], e * 16 + 16)
                pe.wait_ge(up_taken, b * 4 + (c + 1))
                for j in range(ND):
                    for h in range(2):
                        mm = nc.tensor.matmul(up[c][halves[h], 0:UNITS], rowsT[:, j % 4, halves[j // 4]],
                                              chunk[u][c][:, j, h * UNITS:(h + 1) * UNITS], start=(j == 0), stop=(j == ND - 1))
                mm.then_inc(chunk_done, 1)

            def turn_hidden(b, half):
                pe.wait_ge(hid_ready, b * 2 + (half + 1))
                pe.wait_ge(hid_taken, b * 2 + (half + 1))
                for j in range(2):
                    tr = nc.tensor.transpose(turn_h[half][:, j * P:(j + 1) * P], hid[:, half, j * P:(j + 1) * P], k.ident[:])
                tr.then_inc(hid_turned, 1)

            def down_half(e, u, b, half):
                pe.wait_ge(hid_taken, b * 2 + (half + 3))
                if half == 0:
                    pe.wait_ge(y_ready, b + 1)
                pe.wait_ge(loaded[4 + half], e * 16 + 16)
                for j in range(4):
                    for h in range(2):
                        mm = nc.tensor.matmul(down[halves[h], :], hidT[:, 2 * half + j % 2, halves[j // 2]], chunk[u][4 + half][:, j, h * COL:(h + 1) * COL],
                                              start=(half == 0 and j == 0), stop=(half == 1 and j == 3))
                mm.then_inc(chunk_done, 1)

            pe.nop().then_inc(chunk_done, CHUNKS)
            pe.wait_ge(gathered, 16)
            turn_rows()
            with pe.Fori(0, NE // 2) as i:
                for u in range(2):
                    e = i * 2 + u
                    with pe.Fori(first_block(pe, e), first_block(pe, e + 1)) as b:
                        pe.wait_ge(rows_taken, b + 1)
                        for c in range(3):
                            up_chunk(e, u, b, c)
                        turn_hidden(b, 0)
                        up_chunk(e, u, b, 3)
                        down_half(e, u, b, 0)
                        pe.wait_ge(gathered, b * 16 + 32)
                        turn_rows()
                        turn_hidden(b, 1)
                        down_half(e, u, b, 1)

        @block.scalar
        def _(act):
            def take_rows():
                nc.scalar.activation(rowsT, turn_r[:].rearrange("p (j r) -> p j r", r=P), ACT.Copy).then_inc(rows_taken, 1)

            act.nop().then_inc(hid_taken, 2)
            act.wait_ge(rows_turned, 1)
            take_rows()
            with act.Fori(0, NE) as e:
                with act.Fori(first_block(act, e), first_block(act, e + 1)) as b:
                    for half in range(2):
                        act.wait_ge(gate_ready, b * 2 + (half + 1))
                        nc.scalar.activation(sig[:, half], gate[:, half], ACT.Sigmoid, scale=ALPHA).then_inc(sig_ready, 1)
                    for half in range(2):
                        if half == 1:
                            act.wait_ge(rows_turned, b + 2)
                            take_rows()
                        act.wait_ge(hid_turned, b * 2 + (half + 1))
                        nc.scalar.activation(hidT[:, 2 * half:2 * half + 2, :], turn_h[half][:, 0:2 * P].rearrange("p (j r) -> p j r", r=P),
                                             ACT.Copy).then_inc(hid_taken, 1)

        @block.vector
        def _(dve):
            dve.nop().then_inc(up_taken, 4)
            nc.vector.memset(y, 0.0).then_inc(y_ready, 1)
            with dve.Fori(0, NE) as e:
                dve.wait_ge(bias_spread, e * 2 + 2)
                with dve.Fori(first_block(dve, e), first_block(dve, e + 1)) as b:
                    for half in range(2):
                        g, l = gate[:, half], lin[:, half]
                        dve.wait_ge(chunk_done, b * CHUNKS + (CHUNKS + 2 * half + 1))
                        nc.vector.tensor_tensor(g, up[2 * half][:, 0:UNITS], bias[:, half * UNITS:(half + 1) * UNITS], ALU.add).then_inc(up_taken, 1)
                        dve.wait_ge(up_taken, b * 4 + (2 * half + 5))
                        nc.vector.tensor_scalar(g, g, LIMIT, None, ALU.min).then_inc(gate_ready, 1)
                        dve.wait_ge(chunk_done, b * CHUNKS + (CHUNKS + 2 * half + 2))
                        nc.vector.tensor_tensor(l, up[2 * half + 1][:, 0:UNITS], bias[:, COL + half * UNITS:COL + (half + 1) * UNITS], ALU.add).then_inc(up_taken, 1)
                        dve.wait_ge(up_taken, b * 4 + (2 * half + 6))
                        nc.vector.tensor_scalar(l, l, LIMIT, -LIMIT, ALU.min, ALU.max).then_inc(step, 1)
                        dve.wait_ge(sig_ready, b * 2 + (half + 1))
                        nc.vector.tensor_tensor(g, g, sig[:, half], ALU.mult).then_inc(step, 1)
                        dve.wait_ge(step, b * 4 + (2 * half + 2))
                        nc.vector.scalar_tensor_tensor(hid[:, half], l, 1.0, g, ALU.add, ALU.mult).then_inc(hid_ready, 1)
                    dve.wait_ge(chunk_done, b * CHUNKS + (CHUNKS + 6))
                    dve.wait_ge(y_free, b + 1)
                    nc.vector.tensor_tensor(y, down[:], bias[:, 2 * COL:], ALU.add).then_inc(y_ready, 1)


def combine_stage(k, y_dram):
    nc = k.nc
    with ExitStack() as ctx:
        rows = ctx.enter_context(nc.sbuf_tensor("combine_rows", [P, NT, TOPK, D], F32))
        acc = ctx.enter_context(nc.sbuf_tensor("combine_sum", [P, NT, D], F32))
        loaded = [nc.alloc_semaphore(f"combine_loaded{t}") for t in range(NT)]
        begun, added, summed, scaled = (nc.alloc_semaphore(f"combine_{s}") for s in ("begun", "added", "summed", "scaled"))
        block = ctx.enter_context(nc.Block())

        @block.sync
        def _(sp):
            for t in range(NT):
                sp.dma_start(rows[:, t], y_dram[t * P * TOPK:(t + 1) * P * TOPK, :].rearrange("(p k) d -> p k d", k=TOPK)).then_inc(loaded[t], 16)
            k.load_end = len(k.plan) - 1
            load_chunks(k, sp, ("out1", D // NARROW - 1))

        @block.scalar
        def _(act):
            for t in range(NT):
                act.wait_ge(loaded[t], 16)
                nc.scalar.activation(acc[:, t, :], rows[:, t, 0, :], ACT.Copy, scale=k.gates[:, t, 0:1]).then_inc(begun, 1)

        @block.vector
        def _(dve):
            for t in range(NT):
                dve.wait_ge(begun, t + 1)
                for j in range(1, TOPK):
                    if j >= 2:
                        dve.wait_ge(added, (TOPK - 2) * t + j - 1)
                    nc.vector.scalar_tensor_tensor(acc[:, t, :], rows[:, t, j, :], k.gates[:, t, j:j + 1], acc[:, t, :], ALU.mult,
                                                   ALU.add).then_inc(added if j < TOPK - 1 else summed, 1)

        @block.gpsimd
        def _(pool):
            for t in range(NT):
                pool.wait_ge(summed, t + 1)
                nc.gpsimd.tensor_tensor(acc[:, t, :], acc[:, t, :], k.mod[:, 3, :], ALU.mult).then_inc(scaled, 1)
                pool.wait_ge(scaled, t + 1)
                nc.gpsimd.tensor_tensor(k.x[:, t, :], k.x[:, t, :], acc[:, t, :], ALU.add)




def rope_stage(k, name, spans, cos, sin):
    nc = k.nc
    with ExitStack() as ctx:
        step = {e: nc.alloc_semaphore(f"{name}_{e}_step") for e in ("dve", "pool")}
        rot = [ctx.enter_context(nc.sbuf_tensor(f"{name}_rot{i}", list(v.shape), F32)) for i, (_, v, _) in enumerate(spans)]
        block = ctx.enter_context(nc.Block())

        def turn(eng, ops, e):
            mine = [(v, dst, r) for (engine, v, dst), r in zip(spans, rot) if engine == e]
            done = 0
            for v, _, r in mine:
                shape, half = list(v.shape), v.shape[3] // 2
                c, s = (x[:].unsqueeze(2).to_broadcast(shape) for x in (cos, sin))
                ops.tensor_tensor(r[:, :, :, 0:half], v[:, :, :, half:], s[:, :, :, 0:half], ALU.mult).then_inc(step[e], 1)
                ops.tensor_tensor(r[:, :, :, half:], v[:, :, :, 0:half], s[:, :, :, half:], ALU.mult).then_inc(step[e], 1)
                done += 2
                eng.wait_ge(step[e], done)
                ops.tensor_tensor(v, v, c, ALU.mult).then_inc(step[e], 1)
                done += 1
            for n, (v, dst, r) in enumerate(mine):
                eng.wait_ge(step[e], 3 * (n + 1))
                if dst is None:
                    ops.tensor_tensor(v, v, r[:], ALU.add)
                else:
                    for t in range(NT):
                        ops.tensor_tensor(dst[t], by_group(v[:, t], dst[t]), by_group(r[:, t], dst[t]), ALU.add)

        @block.vector
        def _(dve):
            turn(dve, nc.vector, "dve")

        @block.gpsimd
        def _(pool):
            turn(pool, nc.gpsimd, "pool")


def by_group(view, dst):
    return view if len(dst.shape) == 3 else view.rearrange("p (g r) w -> p r g w", g=G2)


@contextmanager
def cleared_semaphores(nc):
    held = nc.snapshot_sems()
    yield
    nc.clear_and_free_semaphores(nc.allocated_since(held))
    nc.all_engine_barrier()


KC, VC, KS, VS, KW, VW, GA, CQ, CKV, KR = 512, 640, 768, 896, 1024, 1152, 1280, 1304, 1560, 1688
IN2_W = 1720


def project2_stage(k, l, tok, room):
    jobs = []
    n = 0
    for c, (c0, c1) in enumerate(IN2):
        w = split_chunk(k, ("in2", l, c))
        for t in range(NT):
            mm = [(k.hT[:, j, t * P:(t + 1) * P], w[:, j, :]) for j in range(ND)]
            jobs.append(Job(mm, P, c1 - c0, copy_to(k, tok[:, t, c0:c1]), engine_of(n), ("in2", l, c)))
            n += 1
    split_gemm_stage(k, f"in2_{l}", jobs, last_key=("in2", l, 3), norm=[(k.x, k.attn_norm[:, l, :], None)], room=room)


def compress_stage(k, l, tok, kcmp, vbd):
    nc = k.nc
    half, last = CB // 4, k.n_groups + 1
    for kv in "kv":
        k.last_group[k.chunk_no[("cmp", l, kv)]] = last
    k.n_groups += 1
    with ExitStack() as ctx:
        def sb(s, shape):
            return ctx.enter_context(nc.sbuf_tensor(f"cmp{l}_{s}", shape, F32))

        def sem(s):
            return nc.alloc_semaphore(f"cmp{l}_{s}")

        def ps(s, n):
            return ctx.enter_context(nc.psum_tensor(f"cmp{l}_{s}", [P, n], F32))

        pair = [sb(f"pair_{kv}", [P, S]) for kv in "kv"]
        x = [sb(f"x_{kv}", [P, CB // 2, G2 * CPAD]) for kv in "kv"]
        pos = sb("pos", [P, 2, CB // 2])
        hid, hidT = sb("hid", [P, CHID]), sb("hidT", [P, 2, G2 * CPAD])
        hid4 = sb("hid4", [P, 2, G2, R2, CPAD])
        w2k, w2v = sb("w2k", [P, 2, 2, DK2]), sb("w2v", [P, 2, DK2])
        turned, paired, placed, zeroed, small_loaded = sem("turned"), sem("paired"), sem("placed"), sem("zeroed"), sem("small_loaded")
        gains_loaded = sem("gains_loaded")
        activated, hid_turned, spread, made, step = sem("activated"), sem("hid_turned"), sem("spread"), sem("made"), sem("step")
        bank = [ps(f"t{i}", COL) for i in range(2)]
        h_bank, ht_bank, k_bank = ps("h", COL), ps("ht", COL), ps("k", COL)
        v_bank = [ps(f"v{g}", COL) for g in range(G2)]
        w1 = [chunk_view(k, ("cmp", l, kv))[0] for kv in "kv"]
        block = ctx.enter_context(nc.Block())

        @block.sync
        def _(sp):
            for i, kv in enumerate("kv"):
                sp.dma_start(pos[:, i, :], k.a[f"cmp_pos_{kv}_2"][l].rearrange("(u a) d -> (a d) u", a=2),
                             allow_slow_non_contiguous=True).then_inc(small_loaded, 16)
            for copy in range(2):
                sp.dma_start(w2k[:, :, copy, :], k.a["cmp_w2_k_2"][l].rearrange("(k p) n -> p k n", p=P)).then_inc(small_loaded, 16)
            sp.dma_start(w2v[:], k.a["cmp_w2_v_2"][l].rearrange("(k p) n -> p k n", p=P)).then_inc(small_loaded, 16)
            if l == 0:
                sp.dma_start(k.final_row[:], row(k.a["final_norm_2"])).then_inc(gains_loaded, 16)
            load_chunks(k, sp, ("cmp", l, "v"))
            if l == 0:
                sp.wait_ge(gains_loaded, 16)

        @block.gpsimd
        def _(pool):
            for i in range(2):
                nc.gpsimd.memset(x[i][:, half:, G2 * CPAD - 1:], 0.0).then_inc(zeroed, 1)
            nc.gpsimd.memset(vbd[:], 0.0).then_inc(zeroed, 1)

        @block.tensor
        def _(pe):
            for i, c0 in enumerate((KC, VC)):
                for t in range(NT):
                    tr = nc.tensor.transpose(bank[i][:, t * P:(t + 1) * P], tok[:, t, c0:c0 + P], k.ident[:])
                tr.then_inc(turned, 1)
            pe.wait_ge(zeroed, 3)
            pe.wait_ge(placed, 4)
            for kv in "kv":
                wait_chunk(k, pe, ("cmp", l, kv))
            for u in range(CB // 2):
                for i in range(2):
                    mm = nc.tensor.matmul(h_bank[64 * i:64 * i + 64, 0:CHID], x[i][:, u, :], w1[i][:, u, :], start=(u == 0), stop=(u == CB // 2 - 1))
            mm.then_inc(k.groups_done, 1)
            pe.wait_ge(activated, 1)
            for m in range(2):
                tr = nc.tensor.transpose(ht_bank[:, m * P:(m + 1) * P], hid[:, m * P:(m + 1) * P], k.ident[:])
            tr.then_inc(hid_turned, 1)
            pe.wait_ge(small_loaded, 16 * 5)
            pe.wait_ge(spread, 1)
            for m in range(2):
                mm = nc.tensor.matmul(k_bank[:, 0:G2 * CPAD], w2k[:, m].rearrange("p a n -> p (a n)"), hidT[:, m, :], start=(m == 0), stop=(m == 1))
            mm.then_inc(made, 1)
            for g in range(G2):
                pe.wait_ge(spread, 2 + 2 * g + 1)
                for m in range(2):
                    mm = nc.tensor.matmul(v_bank[g][:, 0:DK2], hid4[:, m, g].rearrange("p r n -> p (r n)"), w2v[:, m, :], start=(m == 0), stop=(m == 1))
                mm.then_inc(made, 1)

        @block.scalar
        def _(act):
            act.wait_ge(k.groups_done, last)
            nc.scalar.activation(hid[:], h_bank[:, 0:CHID], ACT.Silu).then_inc(activated, 1)
            act.wait_ge(made, 1)
            for g in range(G2):
                nc.scalar.activation(kcmp[64 * g:64 * g + 64, :], k_bank[64 * g:64 * g + 64, g * CPAD:(g + 1) * CPAD], ACT.Copy)

        @block.vector
        def _(dve):
            chain = Chain(dve, step)
            for i in range(2):
                dve.wait_ge(turned, i + 1)
                for g in range(G2):
                    for parity in range(2):
                        nc.vector.tensor_copy(pair[i][64 * parity:64 * parity + 64, g * 256:(g + 1) * 256],
                                              bank[i][64 * g:64 * g + 64, :].rearrange("p (n a) -> p n a", a=2)[:, :, parity]).then_inc(paired, 1)
            dve.wait_ge(small_loaded, 16 * 5)
            for i in range(2):
                dve.wait_ge(paired, 4 * (i + 1))
                for late in range(2):
                    n = G2 * CPAD - late
                    nc.vector.tensor_tensor(x[i][:, late * half:(late + 1) * half, 0:n],
                                            pair[i][:, late * half:].rearrange("p (n u) -> p u n", u=half),
                                            pos[:, i, late * half:(late + 1) * half].unsqueeze(2).to_broadcast([P, half, n]), ALU.add).then_inc(placed, 1)
            dve.wait_ge(hid_turned, 1)
            turned_hid = ht_bank[:, 0:2 * P].rearrange("p (m i n) -> p m i n", m=2, i=2)
            nc.vector.tensor_copy(hidT[:], turned_hid[:, :, 0, :]).then_inc(spread, 1)
            for g in range(G2):
                for m in range(2):
                    nc.vector.tensor_copy(hid4[:, m, g], turned_hid[:, m, 1, g * CPAD:(g + 1) * CPAD].unsqueeze(1).to_broadcast([P, R2, CPAD])).then_inc(spread, 1)
            dve.wait_ge(zeroed, 3)
            for g in range(G2):
                dve.wait_ge(made, 2 + g)
                for r in range(R2):
                    nc.vector.tensor_copy(vbd[32 * r:32 * r + 32, g, 64 * r:64 * r + 64], v_bank[g][32 * r:32 * r + 32, 0:DK2])


def compressed_attention_stage(k, l, qT, kcmp, vbd, gates, o):
    nc = k.nc
    scale = DK2 ** -0.5
    with ExitStack() as ctx:
        def sem(s):
            return nc.alloc_semaphore(f"ca{l}_{s}")

        def sb(s, shape):
            return ctx.enter_context(nc.sbuf_tensor(f"ca{l}_{s}", shape, F32))

        scored, biased, shifted, raised, weighed, turned, taken, valued, step = (
            sem(s) for s in ("scored", "biased", "shifted", "raised", "weighed", "turned", "taken", "valued", "step"))
        s = [sb(f"s{g}", [P, NT, R2, CPAD]) for g in range(G2)]
        top, inv = sb("top", [P, G2, NT, R2]), sb("inv", [P, G2, NT, R2])
        pT = sb("pT", [P, G2, S])
        sc = [ctx.enter_context(nc.psum_tensor(f"ca{l}_scores{i}", [P, COL], F32)) for i in range(G2)]
        tr = [ctx.enter_context(nc.psum_tensor(f"ca{l}_turned{i}", [P, COL], F32)) for i in range(G2)]
        ov = ctx.enter_context(nc.psum_tensor(f"ca{l}_o", [P, NT, COL], F32))
        block = ctx.enter_context(nc.Block())

        def by_tile(bank):
            return bank[:].rearrange("p (t r n) -> p t r n", t=NT, n=CPAD)

        @block.tensor
        def _(pe):
            for t in range(NT):
                for r in range(R2):
                    for g in range(G2):
                        mm = nc.tensor.matmul(sc[g][:, (t * R2 + r) * CPAD:(t * R2 + r + 1) * CPAD], qT[64 * g:64 * g + 64, r, t * P:(t + 1) * P],
                                              kcmp[64 * g:64 * g + 64, :], start=True, stop=True)
            mm.then_inc(scored, 1)
            for g in range(G2):
                pe.wait_ge(weighed, g + 1)
                for t in range(NT):
                    x = nc.tensor.transpose(tr[g][:, t * P:(t + 1) * P], s[g][:, t].rearrange("p r n -> p (r n)"), k.ident[:])
                x.then_inc(turned, 1)
            for g in range(G2):
                pe.wait_ge(taken, g + 1)
                for t in range(NT):
                    mm = nc.tensor.matmul(ov[:, t, g * 256:(g + 1) * 256], pT[:, g, t * P:(t + 1) * P], vbd[:, g, :], start=True, stop=True)
                mm.then_inc(valued, 1)

        @block.scalar
        def _(act):
            for g in range(G2):
                act.wait_ge(shifted, g + 1)
                nc.scalar.activation(s[g][:], s[g][:], ACT.Exp).then_inc(raised, 1)
            for g in range(G2):
                act.wait_ge(turned, g + 1)
                nc.scalar.activation(pT[:, g, :], tr[g][:], ACT.Copy).then_inc(taken, 1)

        @block.vector
        def _(dve):
            chain = Chain(dve, step)
            dve.wait_ge(scored, 1)
            for g in range(G2):
                shape = [P, NT, R2, CPAD]
                for t in range(NT):
                    last = nc.vector.scalar_tensor_tensor(s[g][:, t], by_tile(sc[g])[:, t], scale, k.cmp_bias[:, t].unsqueeze(1).to_broadcast(shape[:1] + shape[2:]),
                                                          ALU.mult, ALU.add)
                    last.then_inc(biased, 1)
                dve.wait_ge(biased, NT * (g + 1))
                chain(nc.vector.tensor_reduce(top[:, g], s[g][:], X, ALU.max))
                nc.vector.tensor_tensor(s[g][:], s[g][:], top[:, g].unsqueeze(3).to_broadcast(shape), ALU.subtract).then_inc(shifted, 1)
            for g in range(G2):
                dve.wait_ge(raised, g + 1)
                nc.vector.tensor_tensor(s[g][:], s[g][:], k.cmp_mask[:].unsqueeze(2).to_broadcast(shape), ALU.mult).then_inc(weighed, 1)
            for g in range(G2):
                dve.wait_ge(weighed, g + 1)
                chain(nc.vector.tensor_reduce(inv[:, g], s[g][:], X, ALU.add))
            chain(nc.vector.tensor_scalar(inv[:], inv[:], 1e-30, None, ALU.max))
            chain(nc.vector.reciprocal(inv[:], inv[:]))
            for g in range(G2):
                chain(nc.vector.tensor_tensor(inv[:, g], inv[:, g], gates[:, :, g * R2:(g + 1) * R2, 0], ALU.mult))
            dve.wait_ge(valued, G2)
            for g in range(G2):
                c = slice(g * 256, (g + 1) * 256)
                nc.vector.tensor_tensor(o[:, :, c].rearrange("p t (r d) -> p t r d", d=DK2), ov[:, :, c].rearrange("p t (r d) -> p t r d", d=DK2),
                                        inv[:, g].unsqueeze(3).to_broadcast([P, NT, R2, DK2]), ALU.mult)


def nsa_stages(k, l, tok, o):
    nc = k.nc
    with ExitStack() as ctx:
        def sb(s, shape):
            return ctx.enter_context(nc.sbuf_tensor(f"nsa{l}_{s}", shape, F32))

        gates = sb("gates", [P, NT, H2, 3])
        qT = sb("qT", [P, R2, S])
        ksT = sb("ksT", [P, 2, S])
        kcmp, vbd = sb("kcmp", [P, CPAD]), sb("vbd", [P, G2, 256])
        with ExitStack() as inner:
            opened = nc.alloc_semaphore(f"nsa{l}_opened")
            block = inner.enter_context(nc.Block())

            @block.scalar
            def _(act):
                nc.scalar.activation(gates[:].rearrange("p t h n -> p t (h n)"), tok[:, :, GA:GA + 24], ACT.Sigmoid).then_inc(opened, 1)
        with nc.sbuf_tensor(f"nsa{l}_q", [P, NT, R2, G2, DK2], F32) as q:
            def heads(c0, n):
                return tok[:, :, c0:c0 + n * DK2].rearrange("p t (n w) -> p t n w", w=DK2)
            spans = [("dve", heads(0, H2), [q[:, t] for t in range(NT)]), ("pool", heads(KC, G2), None),
                     ("pool", heads(KS, G2), None), ("dve", heads(KW, G2), None)]
            rope_stage(k, f"rope{l}", spans, k.cos_a, k.sin_a)
            blocks = [([q[:, t, r].rearrange("p g d -> p (g d)") for t in range(NT)], qT[:, r, :], None, None) for r in range(R2)]
            blocks += [(columns_of(tok, c0, P), ksT[:, j, :], None, None) for j, c0 in enumerate((KS, KW))]
            transpose_stage(k, f"turn_nsa{l}", blocks)
        compress_stage(k, l, tok, kcmp, vbd)
        compressed_attention_stage(k, l, qT, kcmp, vbd, gates, o)

        def step(branch, r, i):
            v0 = (VS, VW)[branch]
            part = [slice(64 * g, 64 * g + 64) for g in range(G2)]

            def out(chain, psum, inv, m):
                h = m * R2 + r
                dst = o[:, i, h * DK2:(h + 1) * DK2]
                return nc.vector.scalar_tensor_tensor(dst, psum, inv, dst, ALU.mult, ALU.add)
            return Step(i=i, q=[qT[part[m], r, i * P:(i + 1) * P] for m in range(2)],
                        k=[ksT[part[m], branch, :] for m in range(2)],
                        v=lambda m, j: tok[:, j, v0 + m * DK2:v0 + (m + 1) * DK2], out=out,
                        gate=gates[:, i, r:H2:R2, 1 + branch])
        attention_stage(k, f"nsa{l}", [step(br, r, i) for br in range(2) for r in range(R2) for i in tiles(r)],
                        DK2 ** -0.5, False, gated=True)


def mla_stages(k, l, tok):
    nc = k.nc
    OUT = H2 * DQ
    with ExitStack() as ctx:
        def sb(s, shape):
            return ctx.enter_context(nc.sbuf_tensor(f"mla{l}_{s}", shape, F32))

        qT = sb("qT", [DQ, H2, S])
        v = sb("v", [P, NT, H2 * DV2])
        kT = sb("kT", [DQ, H2, S])
        rms_stage(k, f"mla_norm{l}", [(tok[:, :, CQ:CQ + RQ].unsqueeze(2), None), (tok[:, :, CKV:CKV + RKV].unsqueeze(2), None)])
        rope_stage(k, f"rope_k{l}", [("dve", tok[:, :, KR:KR + DR].unsqueeze(2), None)], k.cos_b, k.sin_b)
        with nc.sbuf_tensor(f"mla{l}_lat", [P, 3, S], F32) as lat:
            kpe = [(qT[64:64 + DR, 0, :], 64)]
            blocks = [(columns_of(tok, CQ + j * P, P), lat[:, j, :], k.q_norm[:, l, j:j + 1], None) for j in range(2)]
            blocks.append((columns_of(tok, CKV, P), lat[:, 2, :], k.kv_norm[:, l, :], None))
            blocks += [(columns_of(tok, KR - DN, DQ), (kT[DN:DQ, h, :], DN), None, None) for h in range(H2)]
            transpose_stage(k, f"turn_lat{l}", blocks)
            wq, wkv = chunk_view(k, ("up", l))
            key = ("up", l)
            jobs = []
            for t in range(NT):
                c = slice(t * P, (t + 1) * P)
                for c0, c1 in ((0, COL), (COL, H2 * DQ)):
                    jobs.append(Job([(lat[:, j, c], wq[:, j, c0:c1]) for j in range(2)], P, c1 - c0, copy_to(k, tok[:, t, c0:c1]),
                                    engine_of(len(jobs)), key))
                wv = wkv[:, 0, :].rearrange("p (h n) -> p h n", n=DN + DV2)[:, :, DN:]
                jobs.append(Job([(lat[:, 2, c], wv)], P, H2 * DV2, copy_to(k, v[:, t, :]), engine_of(len(jobs)), key))
            for h in range(H2):
                jobs.append(Job([(wkv[:, 0, h * (DN + DV2):h * (DN + DV2) + DN], lat[:, 2, :])], DN, S, copy_to(k, kT[0:DN, h, :]),
                                engine_of(len(jobs)), key))
            gemm_stage(k, f"up{l}", jobs, last_key=key)
        rope_stage(k, f"rope_q{l}", [("dve", tok[:, :, 0:H2 * DQ].rearrange("p t (n w) -> p t n w", w=DQ)[:, :, :, DN:], None)], k.cos_b, k.sin_b)
        transpose_stage(k, f"turn_q{l}", [(columns_of(tok, h * DQ, DQ), qT[:, h, :], None, None) for h in range(H2)])

        def step(pair, i):
            def out(chain, psum, inv, m):
                h = 2 * pair + m
                return nc.vector.tensor_scalar(tok[:, i, OUT + h * DV2:OUT + (h + 1) * DV2], psum, inv, None, ALU.mult)
            return Step(i=i, q=[qT[:, 2 * pair + m, i * P:(i + 1) * P] for m in range(2)],
                                   k=[kT[:, 2 * pair + m, :] for m in range(2)],
                                   v=lambda m, j: v[:, j, (2 * pair + m) * DV2:(2 * pair + m + 1) * DV2], out=out)
        attention_stage(k, f"mla{l}", [step(pair, i) for pair in range(H2 // 2) for i in tiles(pair)], DQ ** -0.5, False)


def mlp_stage(k, l):
    nc = k.nc
    quarter = FF2 // 4 // P
    with nc.sbuf_tensor(f"mlp{l}_u_hi", [P, quarter, S], F32R) as u_hi, nc.sbuf_tensor(f"mlp{l}_u_lo", [P, quarter, S], F32R) as u_lo, \
            nc.sbuf_tensor(f"mlp{l}_relu", [P, 2, S], F32) as relu:
        u = Halves(u_hi, u_lo)
        jobs = []

        def hidden(f, w, cols, key):
            r = relu[:, f % 2, :]

            def evac(e, chain, psum):
                chain(nc.scalar.activation(r, psum, ACT.Relu))
                return nc.scalar.activation(u.hi[:, f, :], r, ACT.Square)

            def finish(chain):
                chain(nc.vector.tensor_tensor(r, r, r, ALU.mult))
                return nc.vector.tensor_tensor(u.lo[:, f, :], r, u.hi[:, f, :].bitcast(F32), ALU.subtract)
            mm = [(w[:, j, cols], k.hT[:, j, :]) for j in range(ND)]
            jobs.append(Job(mm, P, S, evac, "act", key, finish=finish))

        for q in range(4):
            made = len(jobs)
            for c in range(2):
                key = ("ff1", l, 2 * q + c)
                w = split_chunk(k, key)
                for i in range(4):
                    hidden(4 * c + i, w, slice(i * P, (i + 1) * P), key)
            for n in range(2):
                key = ("ff2", l, n, q)
                w = split_chunk(k, key)
                for t in range(NT):
                    mm = [(u[:, f, t * P:(t + 1) * P], w[:, f, :]) for f in range(quarter)]
                    jobs.append(Job(mm, P, COL, residual(k, t, n), "dve", key, needs=[made + f for f in range(quarter)]))
        split_gemm_stage(k, f"mlp{l}", jobs, last_key=key, norm=[(k.x, k.mlp_norm[:, l, :], None)],
                         room=relu)


def part2(k, a, out):
    nc = k.nc
    for l in range(LAYERS):
        with cleared_semaphores(nc):
            layer(k, a, l)
    norm_rows_stage(k, "final_norm", k.x, k.x, k.final_row[:], None, out[0])


def layer(k, a, l):
    nc = k.nc
    with nc.sbuf_tensor(f"tok2_{l}", [P, NT, IN2_W], F32) as tok, nc.sbuf_tensor(f"nsa_o{l}", [P, NT, 512], F32) as o:
        with nc.sbuf_tensor(f"in2_w{l}", [P, 2, 2, SLOT], F32R) as k.w_split:
            project2_stage(k, l, tok, o[:, 0:2, :])
        nsa_stages(k, l, tok, o)
        mla_stages(k, l, tok)
        ob = tok[:, :, H2 * DQ:H2 * DQ + 512]
        with nc.sbuf_tensor(f"out2_w{l}", [P, 2, 2, SLOT], F32R) as k.w_split:
            out_stage(k, f"out2_{l}", [("out2", l, n) for n in range(2)], COL,
                      norm=[(o, k.nsa_norm[:, l, :], None), (ob, k.mla_norm[:, l, :], None)], room=tok[:, 0:3, 0:S])
    with nc.sbuf_tensor(f"mlp_w{l}", [P, 2, 2, SLOT], F32R) as k.w_split:
        mlp_stage(k, l)


class Program:

    def __init__(self, nc, a, ctx):
        self.nc, self.a, self.ctx = nc, a, ctx
        self.small = []
        self.n_groups = 0
        self.next_load = 0
        self.last_group = {}
        self.plan = plan_chunks(a)
        self.chunk_no = {key: n for n, (key, _) in enumerate(self.plan)}
        self.load_end = self.chunk_no[("out1", D // NARROW - 1)]
        self.loaded_at, count = [], [0] * SLOTS
        for n, (_, parts) in enumerate(self.plan):
            count[n % SLOTS] += 16 * len(parts)
            self.loaded_at.append(count[n % SLOTS])

    def sb(self, name, shape, dt=F32):
        return self.ctx.enter_context(self.nc.sbuf_tensor(name, shape, dt))

    def loaded(self, name, shape, *sources):
        t = self.sb(name, shape)
        if len(sources) == 1:
            self.small.append((t[:], sources[0]))
        else:
            self.small += [(t[:, i], src) for i, src in enumerate(sources)]
        return t

    def expert_chunk(self, c, u):
        if u == 1 and c < TWICE:
            where, at = self.expert_w2, c
        else:
            where, at = (self.ring, c) if c < SLOTS else (self.expert_w, c - SLOTS)
        return where[:, at * SLOT:(at + 1) * SLOT].rearrange("p (k n) -> p k n", n=COL if c < 4 else D)

    def constant(self, name):
        src = self.a[f"const_{name}"]
        return self.loaded(name, list(src.shape), src)


def column(v):
    return v.rearrange("(k p) -> p k", p=P)


def row(v):
    return v.partition_broadcast(P)


def build(nc, a, out):
    h2_dram = nc.dram_tensor("h2_rows", [S, D], F32).ap()
    y_dram = nc.dram_tensor("expert_rows", [S * TOPK + P, D], F32).ap()
    with ExitStack() as ctx:
        k = Program(nc, a, ctx)
        k.x = k.sb("x", [P, NT, D])
        k.ring = k.sb("ring", [P, SLOTS * SLOT])
        k.eps = k.sb("eps", [P, 1])
        k.ones = k.sb("ones", [P, P])
        k.ident, k.causal_bias = k.constant("ident"), k.constant("causal_bias")
        k.ident_half, k.causal_half = k.sb("ident_half", [P, P], BF16), k.sb("causal_half", [P, P], BF16)
        k.cmp_mask = k.constant("cmp_mask")
        k.cmp_bias = k.constant("cmp_bias")
        k.cos_a, k.sin_a = k.constant("cos_a"), k.constant("sin_a")
        k.cos_b, k.sin_b = k.constant("cos_b"), k.constant("sin_b")

        def layers(name):
            return [column(a[name][l]) for l in range(LAYERS)]

        k.attn_norm = k.loaded("attn_norm", [P, LAYERS, ND], *layers("attn_norm_2"))
        k.mlp_norm = k.loaded("mlp_norm", [P, LAYERS, ND], *layers("mlp_norm_2"))
        k.nsa_norm = k.loaded("nsa_norm", [P, LAYERS, 4], *layers("nsa_out_norm_2"))
        k.mla_norm = k.loaded("mla_norm", [P, LAYERS, 4], *layers("mla_out_norm_2"))
        k.q_norm = k.loaded("q_norm", [P, LAYERS, 2], *layers("mla_q_norm_2"))
        k.kv_norm = k.loaded("kv_norm", [P, LAYERS, 1], *layers("mla_kv_norm_2"))
        k.ring_loaded = [nc.alloc_semaphore(f"ring_loaded{i}") for i in range(SLOTS)]
        k.groups_done = nc.alloc_semaphore("groups_done")
        k.small_pool_loaded = nc.alloc_semaphore("small_pool_loaded")
        k.gathered, k.y_stored = nc.alloc_semaphore("moe_gathered"), nc.alloc_semaphore("moe_y_stored")
        with cleared_semaphores(nc), ExitStack() as k.ctx:
            k.upper_incl = k.constant("upper_incl")
            k.upper_strict = k.constant("upper_strict")
            k.iota = k.constant("iota")
            k.place_no = k.constant("place_no")
            k.spare_no = k.constant("spare_no")
            k.row_no, k.half_no = k.constant("row_no"), k.constant("half_no")
            k.norm1 = k.loaded("norm1", [P, ND], column(a["norm1_g"][0]))
            k.a_q_gain = k.loaded("a_q_gain", [P, A_DK], row(a["a_q_gain"][0]))
            k.a_k_gain = k.loaded("a_k_gain", [P, A_DK], row(a["a_k_gain"][0]))
            k.a_out_gain = k.loaded("a_out_gain", [P, A_DV], row(a["a_out_gain"][0]))
            k.b_q_gain = k.loaded("b_q_gain", [P, B_DK], row(a["b_q_gain"][0]))
            k.b_k_gain = k.loaded("b_k_gain", [P, B_DK], row(a["b_k_gain"][0]))
            k.c_out_gain = k.loaded("c_out_gain", [P, C_DV], row(a["c_out_gain"][0]))
            k.lam_q = k.loaded("lam_q", [P, 2, A_DK], row(a["a_lam_q1"][0]), row(a["a_lam_q2"][0]))
            k.lam_k = k.loaded("lam_k", [P, 2, A_DK], row(a["a_lam_k1"][0]), row(a["a_lam_k2"][0]))
            k.c_wg2 = k.loaded("c_wg2", [C_RANK, C_HEADS * C_DK], a["c_w_g2"][0])
            k.c_bg = k.loaded("c_bg", [P, 1], column(a["c_b_g"][0]))
            k.conv_w = k.loaded("conv_w", [P, CONV_W, 2], *[column(a["d_conv_w"][0][i]) for i in range(CONV_W)])
            k.conv_b = k.loaded("conv_b", [P, 2], column(a["d_conv_b"][0]))
            k.lru_b = k.loaded("lru_b", [P, 2, 2], column(a["d_b_a"][0]), column(a["d_b_x"][0]))
            k.lru_lam = k.loaded("lru_lam", [P, 2], column(a["d_lambda"][0]))
            k.lru_w = k.sb("lru_w", [P, 2, 2, P])
            k.lru_blocks = [(k.lru_w[64 * (n % 2):64 * (n % 2) + 64, i, n // 2, 64 * (n % 2):64 * (n % 2) + 64], a[name][0][n])
                            for i, name in enumerate(("d_w_a", "d_w_x")) for n in range(4)]
            k.router_w = k.loaded("router_w", [P, ND, NE], a["router_w"][0].rearrange("(k p) n -> p k n", p=P))
            k.router_b = k.loaded("router_b", [1, NE], a["router_b"])
            k.mod = k.sb("mod", [P, 4, D])
            k.cond = k.sb("cond", [P, ND])
            k.scale1, k.shift1 = k.sb("scale1", [P, ND]), k.sb("shift1", [P, ND])
            k.lam = k.sb("lam", [P, 1])
            k.gla_state = k.sb("gla_state", [P, 256])
            k.gla_tile_decay = k.sb("gla_tile_decay", [P, NT])
            k.gates = k.sb("gates", [P, NT, TOPK])
            k.row_token, k.row_place = k.sb("row_token", [P, MAXB + 1], I32), k.sb("row_place", [P, MAXB + 1], I32)
            k.first = k.sb("first_block", [1, NE + 1], I32)
            k.expert_loaded = [nc.alloc_semaphore(f"expert_loaded{c}") for c in range(CHUNKS)]
            k.split_no = {}
            with cleared_semaphores(nc):
                part1(k, a)
            with nc.sbuf_tensor("hT1", [P, ND, S], F32) as k.hT:
                second_norm_stages(k, h2_dram)
                with nc.sbuf_tensor("expert_w", [P, (CHUNKS - SLOTS) * SLOT], F32) as k.expert_w:
                    route_stages(k, a)
                    expert_stage(k, a, h2_dram, y_dram)
            combine_stage(k, y_dram)
        with split_hT(k, "hT2"), nc.sbuf_tensor("final_row", [P, D], F32) as k.final_row:
            part2(k, a, out)


INPUTS = ("x c ada_w ada_b norm1_g norm2_g w_in w_out a_q_gain a_k_gain a_lam_q1 a_lam_k1 a_lam_q2 a_lam_k2 a_out_gain b_q_gain "
          "b_k_gain c_w_g2 c_b_g c_out_gain d_conv_w d_conv_b d_w_a d_b_a d_w_x d_b_x d_lambda router_w router_b exp_w_up exp_b_up "
          "exp_w_down exp_b_down attn_norm_2 w_in_2 cmp_pos_k_2 cmp_w1_k_2 cmp_w2_k_2 cmp_pos_v_2 cmp_w1_v_2 cmp_w2_v_2 mla_q_norm_2 "
          "w_q_up_2 mla_kv_norm_2 w_kv_up_2 nsa_out_norm_2 mla_out_norm_2 w_out_2 mlp_norm_2 w_ff1_2 w_ff2_2 final_norm_2").split()


def kernel(**inputs):
    import concourse.bacc as bacc
    from concourse.bass_utils import run_bass_kernel_spmd

    nc = bacc.Bacc("TRN2", target_bir_lowering=False, num_devices=1)
    arrays = {n: np.ascontiguousarray(inputs[n]) for n in INPUTS}
    arrays |= {f"const_{n}": v for n, v in host_constants().items()}
    a = {n: nc.dram_tensor(f"in_{n}", v.shape, mybir.dt.from_np(v.dtype), kind="ExternalInput").ap() for n, v in arrays.items()}
    out = nc.dram_tensor("out", [1, S, D], F32, kind="ExternalOutput").ap()
    build(nc, a, out)
    result = run_bass_kernel_spmd(nc, [{f"in_{n}": v for n, v in arrays.items()}], core_ids=[0])
    return result.results[0]["out"]
```
